# Optimizing a Trainium2 kernel written in Bass

```python
import jax, jax.numpy as jnp
from jax import lax
import numpy as np

D_MODEL = 2048
BATCH = 1
SEQ = 512
DEPTH = 1
DEC_BATCH = 8
DEC_SEQ = 16
PAST_LEN = 128

CHUNK = 64
N_PREV_CHUNKS = 8
BAND_PAST = N_PREV_CHUNKS * CHUNK
BAND = BAND_PAST + CHUNK
C_CONV = D_MODEL // 2
C_ATTN = D_MODEL - C_CONV
HEAD_DIM = 64
N_HEADS = C_ATTN // HEAD_DIM
CONV_WIDTH = 31
REL_CLIP = 256
N_KEYS = 128
N_EXPERTS = N_KEYS * N_KEYS
PEER_HEADS = 8
PEER_TOPK = 16
D_KEY = 256
D_HALF = D_KEY // 2
PEER_BLOCK = 128
N_IN = 2 * C_CONV + 3 * C_ATTN
EPS = 1e-6

kernel_name = 'hybrid_conv_bandattn_peer_stream_step'

def rmsnorm(x, g):
    x32 = x.astype(jnp.float32)
    y = x32 * lax.rsqrt(jnp.mean(x32 * x32, axis=-1, keepdims=True) + EPS) * g.astype(jnp.float32)
    return y.astype(x.dtype)

def layernorm(x, g, b):
    x32 = x.astype(jnp.float32)
    mu = jnp.mean(x32, axis=-1, keepdims=True)
    xc = x32 - mu
    y = xc * lax.rsqrt(jnp.mean(xc * xc, axis=-1, keepdims=True) + EPS)
    return (y * g.astype(jnp.float32) + b.astype(jnp.float32)).astype(x.dtype)

def causal_dwconv(u_ctx, w, b):
    y = lax.conv_general_dilated(u_ctx, w[:, None, :], window_strides=(1,), padding='VALID',
                                 dimension_numbers=('NWC', 'WIO', 'NWC'),
                                 feature_group_count=w.shape[-1])
    return y + b

def rel_bias(table, rel):
    idx = jnp.clip(rel, -REL_CLIP, REL_CLIP) + REL_CLIP
    return table[:, idx].astype(jnp.float32)

def attend(q, k, v, bias, mask):
    s = jnp.einsum('bqhd,bkhd->bhqk', q.astype(jnp.float32), k.astype(jnp.float32)) * (HEAD_DIM ** -0.5) + bias
    if mask is not None:
        s = jnp.where(mask, s, -1e30)
    p = jax.nn.softmax(s, axis=-1)
    return jnp.einsum('bhqk,bkhd->bqhd', p.astype(v.dtype), v)

def band_attention_prompt(q, k, v, table):
    B, T, H, Dh = q.shape
    nc = T // CHUNK
    qc = q.reshape(B, nc, CHUNK, H, Dh).transpose(1, 0, 2, 3, 4)
    pad = jnp.zeros((B, BAND_PAST, H, Dh), k.dtype)
    kp = jnp.concatenate([pad, k], axis=1)
    vp = jnp.concatenate([pad, v], axis=1)
    a = jnp.arange(CHUNK)[:, None]
    bidx = jnp.arange(BAND)[None, :]
    bias = rel_bias(table, bidx - BAND_PAST - a)

    def one_chunk(args):
        c, qb = args
        kb = lax.dynamic_slice_in_dim(kp, c * CHUNK, BAND, axis=1)
        vb = lax.dynamic_slice_in_dim(vp, c * CHUNK, BAND, axis=1)
        mask = bidx >= (N_PREV_CHUNKS - c) * CHUNK
        return attend(qb, kb, vb, bias, mask)

    o = lax.map(one_chunk, (jnp.arange(nc), qc))
    return o.transpose(1, 0, 2, 3, 4).reshape(B, T, H, Dh)

def band_attention_sample(q, k, v, k_cache, v_cache, table):
    L = k_cache.shape[1]
    S = q.shape[1]
    kk = jnp.concatenate([k_cache, k], axis=1)
    vv = jnp.concatenate([v_cache, v], axis=1)
    qpos = PAST_LEN + jnp.arange(S)
    kpos = jnp.concatenate([PAST_LEN - L + jnp.arange(L), PAST_LEN + jnp.arange(S)])
    bias = rel_bias(table, kpos[None, :] - qpos[:, None])
    return attend(q, kk, vv, bias, None)

def peer(h, w_pq, sub_keys, u_tab, v_tab):
    n, d = h.shape
    n_pad = (-n) % PEER_BLOCK
    hp = jnp.pad(h, ((0, n_pad), (0, 0)))

    def one_block(hb):
        t = hb.shape[0]
        q = (hb @ w_pq).reshape(t, PEER_HEADS, 2, D_HALF).astype(jnp.float32)
        s = jnp.einsum('thpd,pnd->thpn', q, sub_keys.astype(jnp.float32))
        sv, si = lax.top_k(s, PEER_TOPK)
        cand = (sv[:, :, 0, :, None] + sv[:, :, 1, None, :]).reshape(t, PEER_HEADS, PEER_TOPK * PEER_TOPK)
        cidx = (si[:, :, 0, :, None] * N_KEYS + si[:, :, 1, None, :]).reshape(t, PEER_HEADS, PEER_TOPK * PEER_TOPK)
        tv, tpos = lax.top_k(cand, PEER_TOPK)
        eidx = jnp.take_along_axis(cidx, tpos, axis=-1).reshape(t, PEER_HEADS * PEER_TOPK)
        g = jax.nn.softmax(tv, axis=-1).reshape(t, PEER_HEADS * PEER_TOPK)
        u = jnp.take(u_tab, eidx, axis=0)
        vv = jnp.take(v_tab, eidx, axis=0)
        act = jax.nn.gelu(jnp.einsum('td,ted->te', hb, u).astype(jnp.float32))
        return jnp.einsum('te,ted->td', (g * act).astype(hb.dtype), vv)

    out = lax.map(one_block, hp.reshape(-1, PEER_BLOCK, d))
    return out.reshape(-1, d)[:n]

def modulation(c, w_ada, b_ada):
    m = jax.nn.silu(c) @ w_ada + b_ada
    return jnp.split(m[:, None, :], 6, axis=-1)

def layer(x, c, conv_left, attn_fn, norm1_g, norm2_g, w_ada, b_ada, w_in, w_dw, b_dw,
          conv_ln_g, conv_ln_b, w_out, w_pq, sub_keys, u_tab, v_tab):
    B, T, D = x.shape
    sh1, sc1, g1, sh2, sc2, g2 = modulation(c, w_ada, b_ada)
    h = rmsnorm(x, norm1_g) * (1 + sc1) + sh1
    z = h @ w_in
    za, zg, q, k, v = jnp.split(z, [C_CONV, 2 * C_CONV, 2 * C_CONV + C_ATTN, 2 * C_CONV + 2 * C_ATTN], axis=-1)
    u = za * jax.nn.sigmoid(zg)
    y_conv = causal_dwconv(jnp.concatenate([conv_left, u], axis=1), w_dw, b_dw)
    y_conv = jax.nn.silu(layernorm(y_conv, conv_ln_g, conv_ln_b))
    q = q.reshape(B, T, N_HEADS, HEAD_DIM)
    k = k.reshape(B, T, N_HEADS, HEAD_DIM)
    v = v.reshape(B, T, N_HEADS, HEAD_DIM)
    o = attn_fn(q, k, v).reshape(B, T, C_ATTN)
    x = x + g1 * (jnp.concatenate([y_conv, o], axis=-1) @ w_out)
    h2 = rmsnorm(x, norm2_g) * (1 + sc2) + sh2
    x = x + g2 * peer(h2.reshape(B * T, D), w_pq, sub_keys, u_tab, v_tab).reshape(B, T, D)
    return x, u, k, v

def setup_inputs(seed: int = 0) -> dict:
    key = jax.random.key(seed)
    ks = jax.random.split(key, 24)
    f32 = jnp.float32

    def nrm(k, shape, s):
        return s * jax.random.normal(k, shape, f32)

    cache_len = min(BAND_PAST, PAST_LEN)
    return {
        'x_prompt': nrm(ks[0], (BATCH, SEQ, D_MODEL), 1.0),
        'x_sample': nrm(ks[1], (DEC_BATCH, DEC_SEQ, D_MODEL), 1.0),
        'c_prompt': nrm(ks[2], (BATCH, D_MODEL), 1.0),
        'c_sample': nrm(ks[3], (DEC_BATCH, D_MODEL), 1.0),
        'cache_conv': nrm(ks[4], (DEPTH, DEC_BATCH, CONV_WIDTH - 1, C_CONV), 0.5),
        'cache_attn_k': nrm(ks[5], (DEPTH, DEC_BATCH, cache_len, N_HEADS, HEAD_DIM), 1.0),
        'cache_attn_v': nrm(ks[6], (DEPTH, DEC_BATCH, cache_len, N_HEADS, HEAD_DIM), 1.0),
        'norm1_g': 1.0 + nrm(ks[7], (DEPTH, D_MODEL), 0.05),
        'norm2_g': 1.0 + nrm(ks[8], (DEPTH, D_MODEL), 0.05),
        'w_ada': nrm(ks[9], (DEPTH, D_MODEL, 6 * D_MODEL), 0.5 * D_MODEL ** -0.5),
        'b_ada': nrm(ks[10], (DEPTH, 6 * D_MODEL), 0.02),
        'w_in': nrm(ks[11], (DEPTH, D_MODEL, N_IN), D_MODEL ** -0.5),
        'w_dw': nrm(ks[12], (DEPTH, CONV_WIDTH, C_CONV), CONV_WIDTH ** -0.5),
        'b_dw': nrm(ks[13], (DEPTH, C_CONV), 0.02),
        'conv_ln_g': 1.0 + nrm(ks[14], (DEPTH, C_CONV), 0.05),
        'conv_ln_b': nrm(ks[15], (DEPTH, C_CONV), 0.02),
        'rel_bias_table': nrm(ks[16], (DEPTH, N_HEADS, 2 * REL_CLIP + 1), 0.3),
        'w_out': nrm(ks[17], (DEPTH, D_MODEL, D_MODEL), D_MODEL ** -0.5),
        'w_pq': nrm(ks[18], (DEPTH, D_MODEL, PEER_HEADS * D_KEY), D_MODEL ** -0.5),
        'sub_keys': nrm(ks[19], (DEPTH, 2, N_KEYS, D_HALF), D_HALF ** -0.5),
        'u_experts': nrm(ks[20], (DEPTH, N_EXPERTS, D_MODEL), D_MODEL ** -0.5),
        'v_experts': nrm(ks[21], (DEPTH, N_EXPERTS, D_MODEL), 0.5),
        'final_g': 1.0 + nrm(ks[22], (D_MODEL,), 0.05),
    }

def reference(x_prompt, x_sample, c_prompt, c_sample, cache_conv, cache_attn_k, cache_attn_v,
              norm1_g, norm2_g, w_ada, b_ada, w_in, w_dw, b_dw, conv_ln_g, conv_ln_b,
              rel_bias_table, w_out, w_pq, sub_keys, u_experts, v_experts, final_g):
    xp, xs = x_prompt, x_sample
    conv_p, k_p, v_p, conv_s, k_s, v_s = [], [], [], [], [], []
    for l in range(DEPTH):
        params = (norm1_g[l], norm2_g[l], w_ada[l], b_ada[l], w_in[l], w_dw[l], b_dw[l],
                  conv_ln_g[l], conv_ln_b[l], w_out[l], w_pq[l], sub_keys[l], u_experts[l], v_experts[l])
        table = rel_bias_table[l]
        left0 = jnp.zeros((xp.shape[0], CONV_WIDTH - 1, C_CONV), xp.dtype)
        xp, up, kp, vp = layer(xp, c_prompt, left0,
                               lambda q, k, v: band_attention_prompt(q, k, v, table), *params)
        conv_p.append(up[:, -(CONV_WIDTH - 1):])
        k_p.append(kp[:, -BAND_PAST:])
        v_p.append(vp[:, -BAND_PAST:])
        kc, vc, cc = cache_attn_k[l], cache_attn_v[l], cache_conv[l]
        xs, us, ksn, vsn = layer(xs, c_sample, cc,
                                 lambda q, k, v: band_attention_sample(q, k, v, kc, vc, table), *params)
        conv_s.append(jnp.concatenate([cc, us], axis=1)[:, -(CONV_WIDTH - 1):])
        k_s.append(ksn)
        v_s.append(vsn)
    y_prompt = rmsnorm(xp, final_g)
    y_sample = rmsnorm(xs, final_g)
    return (y_prompt, y_sample, jnp.stack(conv_p), jnp.stack(k_p), jnp.stack(v_p),
            jnp.stack(conv_s), jnp.stack(k_s), jnp.stack(v_s))


_drawn_inputs = setup_inputs


def setup_inputs(seed=0):
    import zlib

    import numpy as np

    out = dict(_drawn_inputs(seed))
    spreads = {}
    factors = {'norm2_g': 2.868,
     'b_dw': 6.945,
     'conv_ln_g': 5.151,
     'conv_ln_b': 8.0,
     'rel_bias_table': 4.572}
    for name, (base, spread) in spreads.items():
        noise = np.random.default_rng([zlib.crc32(name.encode()), seed]).standard_normal(out[name].shape)
        drawn = base * np.exp(spread * noise) if base else spread * noise
        out[name] = __import__('jax').numpy.asarray(drawn.astype(out[name].dtype))
    for name, factor in factors.items():
        out[name] = (out[name] * factor).astype(out[name].dtype)
    return out
```

```python
import concourse.bass as bass
from concourse import mybir
from contextlib import ExitStack


def hybrid_encoder_step(nc, ins, outs):
    F32 = mybir.dt.float32
    U32 = mybir.dt.uint32
    ALU = mybir.AluOpType
    ACT = mybir.ActivationFunctionType
    AX = mybir.AxisListType

    P = 128
    D = 2048
    KT = D // P
    CC = 1024
    CT = CC // P
    NB, NS = 8, 16
    TP = 4
    T = TP + 1
    NP = TP * P
    NT = T * P
    NCND = 1 + NB
    WID = 31
    CTX = WID - 1
    NH, DH = 16, 64
    EXT = 640
    XLEN = NP + P - 1
    NPH, TOPK, NKEY = 8, 16, 128
    NG = T * NPH
    EPS = 1e-6
    NEG = -1e30
    BW = 256
    NRING = 4

    ctx = ExitStack()
    with ctx:
        def sem(name):
            return ctx.enter_context(nc.semaphore(name))

        R0 = ctx.enter_context(nc.sbuf_tensor("R0", [P, NRING * KT * BW], F32))
        R12 = ctx.enter_context(nc.sbuf_tensor("R12", [P, 2 * T * D], F32))
        R3 = ctx.enter_context(nc.sbuf_tensor("R3", [P, 12400], F32))
        MS = ctx.enter_context(nc.sbuf_tensor("MS", [P, 3776], F32))
        PB = [ctx.enter_context(nc.psum_tensor(f"bank{i}", [P, 512], F32)) for i in range(8)]
        R2 = T * D

        def r12(a, n, p=P):
            return R12[0:p, a:a + n]

        ms_at = [0]

        def misc(n):
            ms_at[0] += n
            return MS[:, ms_at[0] - n:ms_at[0]]

        ring = R0[:, :].rearrange("p (s k n) -> p s k n", s=NRING, k=KT)
        ident = misc(P)
        mean_w = misc(P)
        blockmask = misc(P)
        wdT = misc(8 * 32).rearrange("p (c k) -> p c k", k=32)
        skT = misc(2 * NKEY).rearrange("p (h n) -> p h n", h=2)
        modT = misc(32 * 16).rearrange("p (k c) -> p k c", c=16)
        A1T = misc(16 * 16).rearrange("p (k c) -> p k c", c=16)
        prmT = misc(64)
        VS = misc(1280)
        biasC = misc(2 * P).rearrange("p (b n) -> p b n", b=2)
        biasN = misc(NH * NS).rearrange("p (h n) -> p h n", h=NH)
        cT = misc(16 * 9).rearrange("p (k c) -> p k c", c=9)
        sm = misc(64)
        ssq, rs, tmpa = sm[:, 0:5], sm[:, 8:13], sm[:, 16:21]
        nmax = sm[:, 24:34].rearrange("p (b n) -> p b n", b=2)
        esum = sm[:, 40:50].rearrange("p (b n) -> p b n", b=2)
        mrow = r12(0, 6 * D, NCND)
        cnd = r12(12288, D, NCND)
        prm = r12(14336, P, 40)
        wdw = r12(14464, CC, WID)
        skn = r12(15488, 2 * P).rearrange("p (h n) -> p h n", h=2)
        ext = r12(15744, EXT, NH)
        xt = R3[:, 0:T * D].rearrange("p (t n) -> p t n", t=T)
        junk1 = R3[:, T * D:T * D + D]
        ccx = R3[0:120, T * D:T * D + 2 * CC].rearrange("p (h n) -> p h n", h=2)
        hT = r12(0, KT * NT).rearrange("p (k n) -> p k n", k=KT)
        cat = r12(R2, KT * NT).rearrange("p (k n) -> p k n", k=KT)
        UPW, USW = CTX + NP, CTX + NS
        uP = R3[:, 0:CT * UPW].rearrange("p (c n) -> p c n", c=CT)
        uS = R3[:, CT * UPW:CT * (UPW + NB * USW)].rearrange("p (c b n) -> p c b n", c=CT, b=NB)
        UEND = CT * (UPW + NB * USW)
        kT = R3[:, UEND:UEND + CT * NT].rearrange("p (c n) -> p c n", c=CT)
        sig = VS.rearrange("p (b n) -> p b n", b=2)
        vst = VS[:, 0:1024].rearrange("p (b n) -> p b n", b=4)
        ost = r12(0, 4096).rearrange("p (b n) -> p b n", b=4)
        sP = r12(0, 4096).rearrange("p (b i n) -> p b i n", b=2, i=TP)
        uC = r12(4096, CC).rearrange("p (c n) -> p c n", c=CT)
        pT = r12(4096, 1536)
        sS = r12(5632, 512).rearrange("p (b n) -> p b n", b=2)
        biasP = r12(6144, 1024).rearrange("p (b n) -> p b n", b=2)
        vP = r12(7168, 2 * T * P).rearrange("p (b t n) -> p b t n", b=2, t=T)
        kC = R3[:, 0:2048].rearrange("p (b s n) -> p b s n", b=2, s=NB)
        vC = R3[:, 2048:4096].rearrange("p (b s n) -> p b s n", b=2, s=NB)
        kCT = R3[:, 4096:6144].rearrange("p (b s n) -> p b s n", b=2, s=NB)
        qX = R3[:, 6144:7168].rearrange("p (s n) -> p s n", s=NB)
        qXd = bass.AP(tensor=qX.tensor, offset=qX.offset, ap=[list(qX.ap)[0], [P + NS, NB], [1, NS]])
        x1 = r12(0, T * D).rearrange("p (t n) -> p t n", t=T)
        g1b = R3[:, 8192:12288].rearrange("p (b n) -> p b n", b=2)
        otmp = VS[:, 0:512].rearrange("p (b n) -> p b n", b=2)
        A2 = R3[:, 0:2 * D].rearrange("p (b n) -> p b n", b=2)
        B2 = R3[:, 2 * D:4 * D].rearrange("p (b n) -> p b n", b=2)
        n2g = R3[:, 8192:8192 + D]
        junk2 = R3[:, 10240:10240 + D]
        h2T = cat
        q2s = VS.rearrange("p (b n) -> p b n", b=2)
        S = R3[:, 0:T * D].rearrange("p (t r n) -> p t r n", t=T, r=16)
        Sf = R3[:, 0:T * D]
        idx_all = R3[:, 10240:10880].bitcast(U32)
        gates = R3[:, 10880:11520]
        ux = R0[:, 0:4 * D].rearrange("p (s n) -> p s n", s=4)
        vx = R0[:, 4 * D:8 * D].rearrange("p (s n) -> p s n", s=4)
        diag = VS[:, 0:512].rearrange("p (b n) -> p b n", b=4)
        acc = r12(R2, D)
        x1r = r12(R2 + D, D)
        fgb = r12(R2 + 2 * D, D)
        g2b = r12(R2 + 3 * D, D)
        tk_at = [R2 + 4 * D]

        def tk(n):
            tk_at[0] += n
            return R12[:, tk_at[0] - n:tk_at[0]]

        tv2, ti2, tf2 = tk(32), tk(32).bitcast(U32), tk(32)
        tks, cand, eqa, eqb = tk(256), tk(256), tk(256), tk(256)
        tv, tpos, tau, tbu = tk(16), tk(16).bitcast(U32), tk(16).bitcast(U32), tk(16).bitcast(U32)
        taf, tbf, ti0, ti1, tef, tsub, tex = (tk(16) for _ in range(7))
        tsum, trc = tk(8), tk(8)
        iota_u, iota_f = tk(16).bitcast(U32), tk(16)
        iu, iv = tk(16).bitcast(U32), tk(16).bitcast(U32)
        dots, gel, wgt = tk(16), tk(16), tk(16)
        fin = tk(16)
        assert ms_at[0] <= 3776 and tk_at[0] <= 2 * T * D

        mod_d = nc.dram_tensor("mod_scratch", (NCND, 6 * D), F32)
        ext_d = nc.dram_tensor("ext_scratch", (NH, P, EXT), F32)
        x1_d = nc.dram_tensor("x1_scratch", (T, P, D), F32)

        def rows(t, p, n, off=0):
            return bass.AP(tensor=t, offset=off, ap=[*p, [1, n]])

        xp = ins["x_prompt"].rearrange("o (t p) n -> (o t) p n", p=P)
        xs = ins["x_sample"].rearrange("b s n -> (b s) n")
        kvo = {}
        for kind in "kv":
            kvo[kind, 0] = outs[f"new_{kind}_prompt"].rearrange("l o (t p) h d -> (l o t) p (h d)", p=P)
            kvo[kind, 1] = outs[f"new_{kind}_sample"].rearrange("l b s h d -> (l b s) (h d)")
        kcache = ins["cache_attn_k"].rearrange("l b k h d -> k (l b) (h d)")
        vcache = ins["cache_attn_v"].rearrange("l b k h d -> k (l b) (h d)")
        yp = outs["y_prompt"].rearrange("o (t p) n -> (o t) p n", p=P)
        ys = outs["y_sample"].rearrange("b s n -> (b s) n")
        u_tab = ins["u_experts"].rearrange("l e n -> (l e) n")
        v_tab = ins["v_experts"].rearrange("l e n -> (l e) n")
        wv = {n: ins[n].rearrange("l (k p) n -> p (l k) n", p=P) for n in ("w_ada", "w_in", "w_out", "w_pq")}

        w_in_s = [sem(f"weights_{j}") for j in range(NRING)]
        s_small, s_x, s_cc, s_ext = sem("small_in"), sem("x_in"), sem("conv_cache_in"), sem("ext_saved")
        s_bada = sem("b_ada_in")
        s_const, s_pool = sem("consts"), sem("pool_chain")
        s_silu, s_setT, s_setE = sem("cond_silu"), sem("setup_transposed"), sem("setup_copied")
        mod_done, mod_free, mod_saved = sem("mod_done"), sem("mod_free"), sem("mod_saved")
        s_modT, s_A1 = sem("mod_transposed"), sem("A1_ready")
        s_sq, s_v1, s_r1, s_xn = sem("sumsq"), sem("var_ready"), sem("sqrt_ready"), sem("xn_ready")
        xT_done, xT_act, xT_dve = sem("xT_done"), sem("xT_copied_act"), sem("xT_copied_dve")
        cc_T, cc_E = sem("cc_transposed"), sem("cc_copied")
        z_done, z_free, s_sig, s_u = sem("z_done"), sem("z_free"), sem("sigmoid_ready"), sem("u_ready")
        s_vst = [sem(f"v_stored_{i}") for i in range(4)]
        s_uc, s_oT, s_oE = sem("u_packed"), sem("out_transposed"), sem("out_copied")
        s_ost = [sem(f"rows_stored_{i}") for i in range(4)]
        s_cso = sem("conv_cache_moved")
        s_hp = [sem(f"pair_in_{i}") for i in range(2)]
        s_b = [sem(f"bias_in_{i}") for i in range(2)]
        s_bn, s_q0, s_qx = sem("biasN_in"), sem("qX_zeroed"), sem("qX_ready")
        kct_T, kct_E = sem("kct_transposed"), sem("kct_copied")
        sc_ready, sc_read, mx_ready, ex_ready = sem("scores"), sem("scores_read"), sem("max"), sem("exp")
        p_ready, pt_ready, pt_read, pv_done, pv_read = (sem(n) for n in ("p", "pT", "pT_read", "pv", "pv_read"))
        s_conv, s_mean, s_xc, s_ysq, s_ysq_used = (sem(n) for n in ("conv", "mean", "centred", "ysq", "ysq_used"))
        s_var, s_lnv, s_lnr, s_lnx, s_cat = (sem(n) for n in ("var", "ln_var", "ln_sqrt", "ln_x", "cat_ready"))
        s_x5, s_g1, s_m2 = sem("x_again"), sem("g1_in"), sem("mod2_in")
        o_done, o_free = sem("wout_done"), sem("wout_free")
        s_x1, s_x1s, s_h2, s_h2T, s_h2E = (sem(n) for n in ("x1_ready", "x1_saved", "h2_ready", "h2_T", "h2_copied"))
        q_done, q_read, s_s, s_se = sem("q2_done"), sem("q2_read"), sem("key_scores"), sem("key_scores_read")
        u_in = [sem(f"u_rows_{i}") for i in range(4)]
        v_in = [sem(f"v_rows_{i}") for i in range(4)]
        s_iota = sem("iota")
        idx_rdy, sub_rdy, exp_rdy = sem("idx_ready"), sem("gate_logits"), sem("gate_exp")
        dots_done, gel_rdy, w_rdy = sem("dots"), sem("gelu"), sem("weights_ready")
        dg_rdy, v_used, grp_read = sem("diag"), sem("v_used"), sem("group_read")
        s_fg, s_x1b, s_y, s_yst = sem("final_g_in"), sem("x1_back"), sem("y_ready"), sem("y_stored")
        f_sq, f_v, f_r, f_x2 = sem("f_sumsq"), sem("f_var"), sem("f_sqrt"), sem("f_x2")
        s_dve = sem("dve_chain")
        dve_passed, pool_passed = sem("dve_passed"), sem("pool_passed")

        class Chain:

            def __init__(self, eng, s):
                self.eng, self.s, self.n, self.base = eng, s, 0, 0

            def mark(self, ins):
                ins.then_inc(self.s, 1)
                self.n += 1

            def sync(self):
                self.eng.wait_ge(self.s, self.base + self.n)

            def link(self, ins):
                self.mark(ins)
                self.sync()

        def loop(eng, ch, n0, n1, per, body):
            at = ch.n
            with eng.Fori(n0, n1) as i:
                ch.base = (i - n0) * per if n0 else i * per
                body(i)
                assert ch.n - at == per, (ch.n - at, per)
            ch.base, ch.n = 0, at + per * (n1 - n0)

        block = ctx.enter_context(nc.Block())

        @block.sync
        def _(sp):
            def load(name, j, col):
                sp.dma_start(ring[:, j], wv[name][:, :, bass.ds(col, BW)]).then_inc(w_in_s[j], 16)

            for j in range(NRING):
                load("w_ada", j, j * BW)
            with sp.Fori(1, 12) as it:
                for j in range(NRING):
                    sp.wait_ge(mod_done, it * 4 + (j - 3))
                    load("w_ada", j, it * (4 * BW) + j * BW)
            for j in range(NRING):
                sp.wait_ge(mod_done, 44 + j + 1)
                load("w_in", j, j * BW)
            with sp.Fori(1, 4) as kd:
                for j in range(NRING):
                    sp.wait_ge(z_done, kd * 8 + (2 * j - 6))
                    load("w_in", j, kd * (4 * BW) + j * BW)
            for j in range(NRING):
                sp.wait_ge(z_done, 24 + 2 * (j + 1))
                load("w_in", j, 4096 + j * BW)
            for j in range(NRING):
                sp.wait_ge(z_done, 32 + 5 * (j + 1))
                load("w_out", j, j * BW)
            for j in range(NRING):
                sp.wait_ge(o_done, 5 * (j + 1))
                load("w_out", j, 1024 + j * BW)
            for j in range(NRING):
                sp.wait_ge(o_done, 20 + 5 * (j + 1))
                load("w_pq", j, j * BW)
            for j in range(NRING):
                sp.wait_ge(q_done, 2 * (j + 1))
                load("w_pq", j, 1024 + j * BW)
            sp.wait_ge(q_done, 16)
            sp.wait_ge(s_x1s, 16 * T)
            sp.wait_ge(mod_saved, 16)
            sp.dma_start(fgb, rows(ins["final_g"].tensor, [[0, P]], D)).then_inc(s_fg, 16)
            sp.dma_start(g2b, rows(mod_d, [[0, P]], D, 5 * D)).then_inc(s_x1b, 16)
            for t in range(T):
                if t >= 1:
                    sp.wait_ge(s_yst, 16 * t)
                if t == TP:
                    for b in range(NB):
                        sp.dma_start(g2b[NS * b:NS * b + NS],
                                     rows(mod_d, [[0, NS]], D, (1 + b) * 6 * D + 5 * D)).then_inc(s_x1b, 16)
                sp.dma_start(x1r, x1_d[t]).then_inc(s_x1b, 16)
                sp.wait_ge(s_y, t + 1)
                sp.dma_start(yp[t] if t < TP else ys, x1r).then_inc(s_yst, 16)
            sp.wait_ge(s_yst, 16 * T)

        @block.gpsimd
        def _(pool):
            ch = Chain(pool, s_pool)
            dma = pool.dma_start
            dma(cnd[0:1, :], ins["c_prompt"]).then_inc(s_small, 16)
            dma(cnd[1:NCND, :], ins["c_sample"]).then_inc(s_small, 16)
            dma(prm[0:16, :], ins["norm1_g"].rearrange("l (k p) -> (l k) p", p=P)).then_inc(s_small, 16)
            for i, n in enumerate(("b_dw", "conv_ln_g", "conv_ln_b")):
                dma(prm[16 + 8 * i:24 + 8 * i, :], ins[n].rearrange("l (k p) -> (l k) p", p=P)).then_inc(s_small, 16)
            dma(wdw, ins["w_dw"].rearrange("l k c -> (l k) c")).then_inc(s_small, 16)
            dma(skn, ins["sub_keys"].rearrange("l h n d -> n (l h) d")).then_inc(s_small, 16)
            dma(ext[:, 255:EXT - 1], ins["rel_bias_table"].rearrange("l h n -> (l h) n")[:, 0:384]).then_inc(s_small, 16)
            dma(mrow, rows(ins["b_ada"].tensor, [[0, NCND]], 6 * D)).then_inc(s_bada, 16)
            ch.link(pool.memset(ident, 0.0))
            pool.affine_select(out=ident, in_=ident, compare_op=ALU.not_equal, fill=1.0, base=0,
                               pattern=[[-1, P]], channel_multiplier=1).then_inc(s_const, 1)
            pool.memset(mean_w, 1.0 / CC).then_inc(s_const, 1)
            bm = blockmask.rearrange("p (b s) -> p b s", s=NS)
            ch.link(pool.memset(blockmask, 0.0))
            ch.link(pool.affine_select(out=bm, in_=bm, compare_op=ALU.is_ge, fill=NEG, base=0,
                                       pattern=[[-NS, NB], [0, NS]], channel_multiplier=1))
            pool.affine_select(out=bm, in_=bm, compare_op=ALU.is_ge, fill=NEG, base=NS - 1,
                               pattern=[[NS, NB], [0, NS]], channel_multiplier=-1).then_inc(s_const, 1)
            for t in range(TP):
                dma(xt[:, t], xp[t]).then_inc(s_x, 16)
            dma(xt[:, TP], xs).then_inc(s_x, 16)
            dma(outs["new_conv_sample"].rearrange("l b k c -> (l b) k c")[:, 0:CTX - NS, :],
                ins["cache_conv"].rearrange("l b k c -> (l b) k c")[:, NS:CTX, :]).then_inc(s_cso, 16)
            pool.wait_ge(s_setE, 2)
            dma(ext_d[:, :, :], ext.unsqueeze(1).to_broadcast([NH, P, EXT])).then_inc(s_ext, 16)
            pool.wait_ge(s_sq, 5)
            ccv = ins["cache_conv"].rearrange("l (h b) k c -> (l h) (b k) c", h=2)
            for h in range(2):
                dma(ccx[:, h], ccv[h]).then_inc(s_cc, 16)
            pool.wait_ge(mod_free, 4 + 48)
            dma(mod_d[:, 2 * D:], mrow[:, 2 * D:]).then_inc(mod_saved, 16)
            pool.wait_ge(s_ext, 16)
            for b in range(NB):
                dma(biasN[NS * b:NS * b + NS], bass.AP(tensor=ext_d, offset=511,
                    ap=[[EXT - 1, NS], [P * EXT, NH], [1, NS]])).then_inc(s_bn, 16)
            for v in range(4 * T):
                j, t = divmod(v, T)
                pool.wait_ge(z_free, 2 + 32 + v + 1)
                dst = kvo["v", 0][t] if t < TP else kvo["v", 1]
                dma(dst[:, j * BW:(j + 1) * BW], vst[:, v % 4]).then_inc(s_vst[v % 4], 16)
            for i in range(7):
                pool.wait_ge(s_oE, i + 1)
                if i == 0:
                    dma(outs["new_conv_prompt"].rearrange("l o k c -> (l o k) c"), ost[0:CTX, 0]).then_inc(s_ost[0], 16)
                elif i == 1:
                    for b in range(NB):
                        dma(outs["new_conv_sample"].rearrange("l b k c -> (l b) k c")[b, CTX - NS:, :],
                            ost[NS * b:NS * b + NS, 1]).then_inc(s_ost[1], 16)
                else:
                    dma(kvo["k", 0][i - 2] if i < 6 else kvo["k", 1], ost[:, i % 4]).then_inc(s_ost[i % 4], 16)
            for i in range(4):
                pool.wait_ge(s_vst[i], 16 * T)
            pool.wait_ge(s_conv, 1)
            ch.link(pool.memset(qX, 0.0))
            pool.sem_inc(s_q0, 1)
            for h in range(NH):
                hp, b = divmod(h, 2)
                if b == 0:
                    pb = hp % 2
                    if hp >= 2:
                        pool.wait_ge(pv_done, 2 * (hp - 1))
                    cs = slice(hp * P, (hp + 1) * P)
                    dma(vP[:, pb, 0:TP], kvo["v", 0].rearrange("t p n -> p t n")[:, :, cs]).then_inc(s_hp[pb], 16)
                    dma(vP[:, pb, TP], kvo["v", 1][:, cs]).then_inc(s_hp[pb], 16)
                    dma(kC[:, pb], kcache[:, :, cs]).then_inc(s_hp[pb], 16)
                    dma(vC[:, pb], vcache[:, :, cs]).then_inc(s_hp[pb], 16)
                if h >= 2:
                    pool.wait_ge(sc_read, h - 1)
                dma(biasP[:, b], rows(ext_d, [[EXT - 1, P]], 512, h * P * EXT + 127)).then_inc(s_b[b], 16)
                for s in range(NB):
                    dma(biasC[NS * s:NS * s + NS, b], rows(ext_d, [[EXT - 1, NS]], P, h * P * EXT + 383)).then_inc(s_b[b], 16)
            pool.wait_ge(pv_done, NH)
            pool.wait_ge(p_ready, NH)
            for t in range(TP):
                dma(x1[:, t], xp[t]).then_inc(s_x5, 16)
            dma(x1[:, TP], xs).then_inc(s_x5, 16)

            def spread(dst, chunk, s):
                dma(dst(0), rows(mod_d, [[0, P]], D, chunk * D)).then_inc(s, 16)
                for b in range(NB):
                    dma(dst(1)[NS * b:NS * b + NS], rows(mod_d, [[0, NS]], D, (1 + b) * 6 * D + chunk * D)).then_inc(s, 16)

            pool.wait_ge(mod_saved, 16)
            spread(lambda b: g1b[:, b], 2, s_g1)
            pool.wait_ge(s_lnx, 1)
            spread(lambda b: A2[:, b], 4, s_m2)
            spread(lambda b: B2[:, b], 3, s_m2)
            pool.wait_ge(o_free, 4 + 40)
            dma(n2g, rows(ins["norm2_g"].tensor, [[0, P]], D)).then_inc(s_m2, 16)
            for t in range(T):
                dma(x1_d[t], x1[:, t]).then_inc(s_x1s, 16)
            pool.wait_ge(q_done, 16)
            pool.iota(iota_u, pattern=[[1, TOPK]], base=0, channel_multiplier=0).then_inc(s_iota, 1)

            HALF = TOPK // 2

            def gather(dst, table, ix, g, s, signal):
                if s % HALF == 0:
                    ch.link(pool.tensor_copy(ix[:, s:s + HALF], idx_all[:, bass.ds(g * TOPK + s, HALF)]))
                pool.sem_inc(pool_passed, 1)
                pool.indirect_dma_start(dst[:, s % 4], None, table,
                                        bass.IndirectOffsetOnAxis(ap=ix[:, s:s + 1], axis=0)
                                        ).then_inc(signal[s % 4], 16)

            pool.wait_ge(idx_rdy, 1)
            for s in range(TOPK):
                if s >= 4:
                    pool.wait_ge(dots_done, s - 3)
                gather(ux, u_tab, iu, 0, s, u_in)

            def both(g):
                pool.wait_ge(idx_rdy, g + 2)
                for s in range(TOPK):
                    pool.wait_ge(dots_done, g * TOPK + (TOPK + s - 3))
                    gather(ux, u_tab, iu, g + 1, s, u_in)
                    pool.wait_ge(v_used, g * TOPK + (s + 1))
                    gather(vx, v_tab, iv, g, s, v_in)

            loop(pool, ch, 0, NG - 1, 4, both)
            for s in range(TOPK):
                pool.wait_ge(v_used, (NG - 1) * TOPK + s + 1)
                gather(vx, v_tab, iv, NG - 1, s, v_in)
            pool.wait_ge(s_cso, 16)
            pool.wait_ge(s_ost[0], 16 * 2)
            pool.wait_ge(s_ost[1], 16 * (NB + 1))
            pool.wait_ge(s_ost[2], 16 * 2)
            pool.wait_ge(s_ost[3], 16)

        @block.tensor
        def _(pe):
            def tr(out, in_, k):
                return pe.transpose(out, in_, ident[0:k, 0:k])

            pe.wait_ge(s_const, 1)
            pe.wait_ge(s_small, 16 * 9)
            tr(PB[4][:, 0:40], prm, 40).then_inc(s_setT, 1)
            for c in range(CT):
                t = tr(PB[5][:, 32 * c:32 * c + WID], wdw[:, c * P:(c + 1) * P], WID)
            t.then_inc(s_setT, 1)
            for h in range(2):
                t = tr(PB[6][:, h * P:(h + 1) * P], skn[:, h], P)
            t.then_inc(s_setT, 1)
            pe.wait_ge(s_silu, 1)
            for k in range(KT):
                t = tr(PB[7][:, 9 * k:9 * k + 9], cnd[:, k * P:(k + 1) * P], NCND)
            t.then_inc(s_setT, 1)
            pe.wait_ge(s_setE, 6)
            with pe.Fori(0, 12) as it:
                for j in range(NRING):
                    pe.wait_ge(w_in_s[j], it * 16 + 16)
                    pe.wait_ge(mod_free, it * 4 + (j + 1))
                    for k in range(KT):
                        m = pe.matmul(PB[j][0:NCND, 0:BW], cT[:, k, :], ring[:, j, k, :],
                                      start=(k == 0), stop=(k == KT - 1))
                    m.then_inc(mod_done, 1)
            pe.wait_ge(mod_free, 4 + 48)
            for k in range(2 * KT):
                t = tr(PB[4][:, 16 * k:16 * k + 9], mrow[:, k * P:(k + 1) * P], NCND)
            t.then_inc(s_modT, 1)
            pe.wait_ge(s_xn, T)
            for g in range(KT + 4):
                if g >= 4:
                    pe.wait_ge(xT_act, g - 3)
                for i in range(4):
                    src = xt[:, i, g * P:(g + 1) * P] if g < KT else xt[:, TP, (4 * (g - KT) + i) * P:][:, 0:P]
                    t = tr(PB[g % 4][:, i * P:(i + 1) * P], src, P)
                t.then_inc(xT_done, 1)
            pe.wait_ge(s_cc, 32)
            pe.wait_ge(s_A1, 1)
            for c2 in range(4):
                for i in range(4):
                    c, h = 2 * c2 + i // 2, i % 2
                    t = tr(PB[4 + c2][:, i * 120:(i + 1) * 120], ccx[:, h, c * P:(c + 1) * P], 120)
                t.then_inc(cc_T, 1)

            pe.wait_ge(xT_act, KT)
            pe.wait_ge(xT_dve, 4)

            def project(src, j, c, par, signal):
                for k in range(KT):
                    w = ring[:, j, k, c * P:(c + 1) * P]
                    pe.matmul(PB[2 * par][:, 0:NP], w, src[:, k, 0:NP], start=(k == 0), stop=(k == KT - 1))
                    m = pe.matmul(PB[2 * par + 1][:, 0:P], w, src[:, k, NP:NT], start=(k == 0), stop=(k == KT - 1))
                m.then_inc(signal, 1)

            with pe.Fori(0, 4) as kd:
                for j in range(NRING):
                    pe.wait_ge(w_in_s[j], kd * 16 + 16 * 13)
                    for c in range(2):
                        pe.wait_ge(z_free, kd * 8 + (2 * j + c + 1))
                        project(hT, j, c, c, z_done)
            for v in range(4 * T):
                j, t = divmod(v, T)
                if t == 0:
                    pe.wait_ge(w_in_s[j], 16 * 17)
                pe.wait_ge(z_free, 32 + v + 1)
                for k in range(KT):
                    m = pe.matmul(PB[2 * (v % 2)][:, 0:BW], hT[:, k, t * P:(t + 1) * P], ring[:, j, k, :],
                                  start=(k == 0), stop=(k == KT - 1))
                m.then_inc(z_done, 1)
            pe.wait_ge(s_u, 8)
            pe.wait_ge(cc_E, 4)
            for i in range(7):
                if i >= 2:
                    pe.wait_ge(s_oE, i - 1)
                if i == 1:
                    pe.wait_ge(s_uc, 1)
                for c in range(CT):
                    src = (uP[:, c, NP:NP + CTX] if i == 0 else uC[:, c] if i == 1
                           else kT[:, c, (i - 2) * P:(i - 1) * P])
                    n = CTX if i == 0 else P
                    t = pe.transpose(PB[4 + 2 * (i % 2) + c // 4][0:n, (c % 4) * P:(c % 4 + 1) * P], src, ident)
                t.then_inc(s_oT, 1)

            def pair_keys(hp):
                b = hp % 2
                pe.wait_ge(s_hp[b], 64 * (hp // 2 + 1))
                if hp == 0:
                    pe.wait_ge(s_oE, 7)
                else:
                    pe.wait_ge(pt_read, 2 * hp - 1)
                for s in range(NB):
                    t = tr(PB[3 + s // 4][:, (s % 4) * P:(s % 4 + 1) * P], kC[:, b, s], P)
                t.then_inc(kct_T, 1)

            def scores(h):
                hp, b = divmod(h, 2)
                r = slice(DH * b, DH * b + DH)
                q, k = cat[r, CT + hp], kT[r, hp]
                if h >= 1:
                    pe.wait_ge(sc_read, h)
                else:
                    pe.wait_ge(z_free, 2 + 52)
                pe.matmul(PB[0][:, 0:512], q[:, 384:512], k[:, 0:512], start=True, stop=True)
                pe.matmul(PB[1][:, 0:384], q[:, 256:384], k[:, 0:384], start=True, stop=True)
                pe.matmul(PB[1][:, 384:512], q[:, 0:128], k[:, 0:128], start=True, stop=True)
                pe.matmul(PB[2][:, 0:256], q[:, 128:256], k[:, 0:256], start=True, stop=True)
                pe.matmul(PB[2][:, 384:512], q[:, NP:NT], k[:, NP:NT], start=True, stop=True)
                pe.wait_ge(s_qx, hp + 1)
                pe.wait_ge(kct_E, hp + 1)
                for s in range(NB):
                    m = pe.matmul(PB[2][:, 256:384], qX[r, s], kCT[r, hp % 2, s], start=(s == 0), stop=(s == NB - 1))
                m.then_inc(sc_ready, 1)

            def weigh(h):
                hp, b = divmod(h, 2)
                pb = hp % 2
                r, vc = slice(DH * b, DH * b + DH), slice(DH * b, DH * b + DH)
                pe.wait_ge(p_ready, h + 1)
                if h >= 1:
                    pe.wait_ge(pt_read, h)
                pe.wait_ge(kct_E, (h + 1) // 2 + 1 if h + 1 < NH else 8)
                for i in range(4):
                    tr(PB[3][:, i * P:(i + 1) * P], sP[:, b, i, 384 - P * i:512 - P * i], P)
                for i in range(1, 4):
                    tr(PB[4][:, (i - 1) * P:i * P], sP[:, b, i, 512 - P * i:640 - P * i], P)
                tr(PB[4][:, 384:512], sP[:, b, 3, 384:512], P)
                for i in range(2, 4):
                    tr(PB[5][:, (i - 2) * P:(i - 1) * P], sP[:, b, i, 640 - P * i:768 - P * i], P)
                tr(PB[5][:, 256:384], sS[:, b, 0:P], P)
                tr(PB[5][:, 384:512], sS[:, b, P:2 * P], P).then_inc(pt_ready, 1)
                pe.wait_ge(pt_read, h + 1)
                if h >= 1:
                    pe.wait_ge(pv_read, h)
                o, os = PB[6][r], PB[7][r]
                pe.matmul(o[:, 0:512], vP[:, pb, 0, vc], pT[:, 0:512], start=True, stop=False)
                pe.matmul(o[:, 128:512], vP[:, pb, 1, vc], pT[:, 512:896], start=False, stop=False)
                pe.matmul(o[:, 256:512], vP[:, pb, 2, vc], pT[:, 1024:1280], start=False, stop=False)
                pe.matmul(o[:, 384:512], vP[:, pb, 3, vc], pT[:, 896:1024], start=False, stop=True)
                pe.matmul(os[:, 0:P], vP[:, pb, 4, vc], pT[:, 1408:1536], start=True, stop=False)
                for s in range(NB):
                    m = pe.matmul(os[:, NS * s:NS * s + NS], vC[:, pb, s, vc],
                                  pT[:, 1280 + NS * s:1280 + NS * s + NS], start=False, stop=(s == NB - 1))
                m.then_inc(pv_done, 1)

            for h in range(NH + 1):
                if h < NH:
                    if h % 2 == 0:
                        pair_keys(h // 2)
                    scores(h)
                if h >= 1:
                    weigh(h - 1)

            def channel_sum(banks, src, wait, used):
                for c in range(CT):
                    if wait is not None:
                        pe.wait_ge(wait, c + 1)
                    pe.matmul(PB[banks][:, 0:NP], mean_w, src(c)[:, 0:NP], start=(c == 0), stop=(c == CT - 1))
                    m = pe.matmul(PB[banks + 1][:, 0:P], mean_w, src(c)[:, NP:NT], start=(c == 0), stop=(c == CT - 1))
                    if used is not None:
                        m.then_inc(used, 1)
                return m

            pe.wait_ge(s_const, 2)
            pe.wait_ge(s_conv, 1)
            pe.wait_ge(sc_read, NH)
            channel_sum(0, lambda c: cat[:, c], None, None).then_inc(s_mean, 1)
            pe.wait_ge(pt_read, NH)
            channel_sum(2, lambda c: q2s[:, c % 2], s_ysq, s_ysq_used)

            pe.wait_ge(s_cat, CT)
            pe.wait_ge(pv_read, NH)
            pe.wait_ge(s_lnv, 1)
            with pe.Fori(0, 2) as it:
                for v in range(4 * T):
                    j, t = divmod(v, T)
                    if t == 0:
                        pe.wait_ge(w_in_s[j], it * 16 + 16 * 18)
                    pe.wait_ge(o_free, it * 20 + (v + 1))
                    for k in range(KT):
                        m = pe.matmul(PB[v % 4][:, 0:BW], cat[:, k, t * P:(t + 1) * P], ring[:, j, k, :],
                                      start=(k == 0), stop=(k == KT - 1))
                    m.then_inc(o_done, 1)
            for t in range(T):
                pe.wait_ge(s_h2, t + 1)
                if t >= 2:
                    pe.wait_ge(s_h2E, 4 * (t - 1))
                for q in range(4):
                    for i in range(4):
                        k = 4 * q + i
                        m = tr(PB[4 * (t % 2) + q][:, i * P:(i + 1) * P], x1[:, t, k * P:(k + 1) * P], P)
                    m.then_inc(s_h2T, 1)

            def key_scores(n):
                b = n % 2
                pe.wait_ge(q_read, n + 1)
                if n >= 2:
                    pe.wait_ge(s_se, n - 1)
                for t in range(TP):
                    pe.matmul(PB[4 + 2 * b][:, t * P:(t + 1) * P], q2s[:, b, t * P:(t + 1) * P], skT[:, n % 2],
                              start=True, stop=True)
                pe.matmul(PB[5 + 2 * b][:, 0:P], q2s[:, b, NP:NT], skT[:, n % 2], start=True, stop=True).then_inc(s_s, 1)

            pe.wait_ge(s_h2E, 4 * T)
            for n in range(16):
                it, j, c = n // 8, (n % 8) // 2, n % 2
                if c == 0:
                    pe.wait_ge(w_in_s[j], 16 * (20 + it))
                if n >= 2:
                    pe.wait_ge(q_read, n - 1)
                project(h2T, j, c, n % 2, q_done)
                if n >= 1:
                    key_scores(n - 1)
            key_scores(15)

            pe.wait_ge(q_read, 16)
            pe.sem_inc(v_used, 4)
            with pe.Fori(0, NG) as g:
                pe.wait_ge(grp_read, g + 1)
                for s in range(TOPK):
                    pe.wait_ge(v_in[s % 4], g * 64 + 16 * (s // 4 + 1))
                    pe.wait_ge(dg_rdy, g * TOPK + (s + 1))
                    for c in range(4):
                        m = pe.matmul(PB[c][:, :], diag[:, s % 4], vx[:, s % 4, c * 512:(c + 1) * 512],
                                      start=(s == 0), stop=(s == TOPK - 1))
                    m.then_inc(v_used, 1)

        @block.scalar
        def _(act):
            A = nc.scalar.activation
            act.wait_ge(s_small, 16 * 9)
            A(cnd, cnd, ACT.Silu).then_inc(s_silu, 1)
            act.wait_ge(s_x, 16 * T)
            for t in range(T):
                if t >= 1:
                    act.wait_ge(s_sq, t)
                A(junk1, xt[:, t], ACT.Square, accum_out=ssq[:, t:t + 1]).then_inc(s_sq, 1)
            act.wait_ge(s_v1, 1)
            A(rs, tmpa, ACT.Sqrt).then_inc(s_r1, 1)
            act.wait_ge(s_A1, 1)
            act.wait_ge(mod_saved, 16)
            for k in range(KT):
                act.wait_ge(xT_done, k + 1)
                A(hT[:, k, 0:NP], PB[k % 4][:, :], ACT.Identity, scale=A1T[:, k, 0:1],
                  bias=modT[:, k, 0:1]).then_inc(xT_act, 1)
            act.sem_inc(z_free, 2)
            for n in range(32):
                kind, c = divmod(n, 8)
                pa, pb = PB[2 * (n % 2)][:, 0:NP], PB[2 * (n % 2) + 1][:, 0:P]
                act.wait_ge(z_done, n + 1)
                if kind == 0:
                    A(uP[:, c, CTX:], pa, ACT.Copy)
                    A(uS[:, c, :, CTX:], pb.rearrange("p (b s) -> p b s", s=NS), ACT.Copy).then_inc(z_free, 1)
                elif kind == 1:
                    if c >= 2:
                        act.wait_ge(s_u, c - 1)
                    A(sig[:, c % 2, 0:NP], pa, ACT.Sigmoid)
                    A(sig[:, c % 2, NP:NT], pb, ACT.Sigmoid).then_inc(z_free, 1)
                else:
                    dst = cat[:, CT + c] if kind == 2 else kT[:, c]
                    if n == 16:
                        act.wait_ge(cc_E, 4)
                    A(dst[:, 0:NP], pa, ACT.Copy)
                    A(dst[:, NP:NT], pb, ACT.Copy).then_inc(z_free, 1)
            act.wait_ge(s_u, 8)
            for v in range(4 * T):
                act.wait_ge(z_done, 32 + v + 1)
                if v >= 4:
                    act.wait_ge(s_vst[v % 4], 16 * (v // 4))
                A(vst[:, v % 4], PB[2 * (v % 2)][:, 0:BW], ACT.Copy).then_inc(z_free, 1)
            for c in range(CT):
                m = A(uC[:, c].rearrange("p (b s) -> p b s", s=NS), uS[:, c, :, CTX:], ACT.Copy)
            m.then_inc(s_uc, 1)
            for i in range(7):
                n = CTX if i == 0 else P
                act.wait_ge(s_oT, i + 1)
                if i >= 4:
                    act.wait_ge(s_ost[i % 4], 16 * NB if i % 4 == 1 else 16)
                A(ost[0:n, i % 4, 0:512], PB[4 + 2 * (i % 2)][0:n, :], ACT.Copy)
                A(ost[0:n, i % 4, 512:1024], PB[5 + 2 * (i % 2)][0:n, :], ACT.Copy).then_inc(s_oE, 1)

            def copy_pT(h):
                act.wait_ge(pt_ready, h + 1)
                if h >= 1:
                    act.wait_ge(pv_done, h)
                for i in range(3):
                    m = A(pT[:, i * 512:(i + 1) * 512], PB[3 + i][:, :], ACT.Copy)
                m.then_inc(pt_read, 1)

            for h in range(NH + 1):
                if h < NH and h % 2 == 0:
                    hp = h // 2
                    act.wait_ge(kct_T, hp + 1)
                    if hp >= 2:
                        act.wait_ge(sc_ready, 2 * (hp - 1))
                    if hp == 0:
                        act.wait_ge(s_conv, 1)
                    A(kCT[:, hp % 2, 0:4, :], PB[3][:, :].rearrange("p (s n) -> p s n", s=4), ACT.Copy)
                    A(kCT[:, hp % 2, 4:8, :], PB[4][:, :].rearrange("p (s n) -> p s n", s=4), ACT.Copy).then_inc(kct_E, 1)
                if h >= 1:
                    copy_pT(h - 1)
                if h < NH:
                    b = h % 2
                    act.wait_ge(mx_ready, h + 1)
                    for i in range(4):
                        s = sP[:, b, i, 384 - P * i:512]
                        A(s, s, ACT.Exp, bias=nmax[:, b, i:i + 1], accum_out=esum[:, b, i:i + 1])
                    A(sS[:, b], sS[:, b], ACT.Exp, bias=nmax[:, b, 4:5], accum_out=esum[:, b, 4:5]).then_inc(ex_ready, 1)

            for c in range(CT):
                act.wait_ge(s_xc, c + 1)
                if c >= 2:
                    act.wait_ge(s_ysq_used, c - 1)
                A(q2s[:, c % 2], cat[:, c], ACT.Square).then_inc(s_ysq, 1)
            act.wait_ge(s_lnv, 1)
            A(q2s[:, 1], q2s[:, 0], ACT.Sqrt).then_inc(s_lnr, 1)
            for c in range(CT):
                act.wait_ge(s_lnx, c + 1)
                A(cat[:, c], cat[:, c], ACT.Silu, scale=prmT[:, 24 + c:25 + c], bias=prmT[:, 32 + c:33 + c]).then_inc(s_cat, 1)
            act.wait_ge(o_free, 4 + 40)
            for t in range(T):
                if t >= 1:
                    act.wait_ge(s_sq, T + t)
                A(junk2, x1[:, t], ACT.Square, accum_out=ssq[:, t:t + 1]).then_inc(s_sq, 1)
            act.wait_ge(s_v1, 2)
            A(rs, tmpa, ACT.Sqrt).then_inc(s_r1, 1)
            for t in range(T):
                for q in range(4):
                    act.wait_ge(s_h2T, 4 * t + q + 1)
                    A(h2T[:, 4 * q:4 * q + 4, t * P:(t + 1) * P],
                      PB[4 * (t % 2) + q][:, :].rearrange("p (k n) -> p k n", k=4), ACT.Copy).then_inc(s_h2E, 1)
            for n in range(16):
                act.wait_ge(q_done, n + 1)
                if n >= 2:
                    act.wait_ge(s_s, n - 1)
                A(q2s[:, n % 2, 0:NP], PB[2 * (n % 2)][:, 0:NP], ACT.Copy)
                A(q2s[:, n % 2, NP:NT], PB[2 * (n % 2) + 1][:, 0:P], ACT.Copy).then_inc(q_read, 1)

            def gate_exp(g):
                act.wait_ge(sub_rdy, g + 1)
                A(tex, tsub, ACT.Exp, accum_out=tsum[:, 0:1]).then_inc(exp_rdy, 1)

            def group(g, ahead):
                act.wait_ge(dots_done, g * TOPK + TOPK)
                A(gel, dots, ACT.Gelu_apprx_tanh).then_inc(gel_rdy, 1)
                if ahead:
                    gate_exp(g + 2)
                act.wait_ge(w_rdy, g + 1)
                for s in range(TOPK):
                    act.wait_ge(v_used, g * TOPK + (s + 1))
                    A(diag[:, s % 4], ident, ACT.Copy, scale=wgt[:, s:s + 1]).then_inc(dg_rdy, 1)

            def norm_tile(t):
                act.wait_ge(f_x2, t + 1)
                A(x1r, acc, ACT.Square, accum_out=fin[:, 0:1]).then_inc(f_sq, 1)
                act.wait_ge(f_v, t + 1)
                A(fin[:, 2:3], fin[:, 1:2], ACT.Sqrt).then_inc(f_r, 1)

            act.wait_ge(s_s, 16)
            gate_exp(0)
            gate_exp(1)
            for t in range(T):
                if t >= 1:
                    norm_tile(t - 1)
                group(t * NPH, True)
                last = 2 if t == T - 1 else 0
                with act.Fori(t * NPH + 1, (t + 1) * NPH - last) as g:
                    group(g, True)
                for i in range(last):
                    group(NG - last + i, False)
            norm_tile(T - 1)

        @block.vector
        def _(dve):
            ch = Chain(dve, s_dve)
            V = nc.vector
            STT, TT, TS, CP = V.scalar_tensor_tensor, V.tensor_tensor, V.tensor_scalar, V.tensor_copy

            def refine(r, v, t):
                ch.link(TT(t, r, r, ALU.mult))
                ch.link(TT(t, t, v, ALU.mult))
                ch.link(TS(t, t, -0.5, 1.5, ALU.mult, ALU.add))
                return TT(r, r, t, ALU.mult)

            dve.sem_inc(mod_free, 4)
            dve.sem_inc(o_free, 4)
            dve.wait_ge(s_small, 16 * 9)
            CP(ext[:, 0:255], ext[:, 255:256].to_broadcast([NH, 255])).then_inc(s_setE, 1)
            V.memset(ext[:, EXT - 1:EXT], 0.0).then_inc(s_setE, 1)
            dve.wait_ge(s_setT, 3)
            CP(prmT[:, 0:40], PB[4][:, 0:40]).then_inc(s_setE, 1)
            CP(wdT[:, :, 0:WID], PB[5][:, 0:256].rearrange("p (c k) -> p c k", k=32)[:, :, 0:WID]).then_inc(s_setE, 1)
            CP(skT, PB[6][:, 0:256].rearrange("p (h n) -> p h n", h=2)).then_inc(s_setE, 1)
            dve.wait_ge(s_setT, 4)
            CP(cT, PB[7][:, 0:9 * KT].rearrange("p (k c) -> p k c", c=9)).then_inc(s_setE, 1)
            dve.wait_ge(s_setE, 6)
            dve.wait_ge(s_sq, T)
            ch.link(TS(tmpa, ssq, 1.0 / D, EPS, ALU.mult, ALU.add))
            dve.sem_inc(s_v1, 1)
            dve.wait_ge(s_r1, 1)
            ch.link(V.reciprocal(rs, rs))
            ch.link(refine(rs, tmpa, ssq))
            for t in range(T):
                TS(xt[:, t], xt[:, t], rs[:, t:t + 1], None, ALU.mult).then_inc(s_xn, 1)
            dve.wait_ge(s_bada, 16)
            with dve.Fori(0, 12) as it:
                for j in range(NRING):
                    dve.wait_ge(mod_done, it * 4 + (j + 1))
                    m = mrow[:, bass.ds(it * (4 * BW) + j * BW, BW)]
                    TT(m, PB[j][0:NCND, 0:BW], m, ALU.add).then_inc(mod_free, 1)
            dve.wait_ge(s_modT, 1)
            ch.link(CP(modT[:, :, 0:9], PB[4][:, :].rearrange("p (k c) -> p k c", c=16)[:, :, 0:9]))
            STT(out=A1T[:, :, 0:9], in0=modT[:, KT:, 0:9], scalar=1.0,
                in1=prmT[:, 0:KT].unsqueeze(2).to_broadcast([P, KT, 9]), op0=ALU.add, op1=ALU.mult).then_inc(s_A1, 1)
            dve.wait_ge(s_A1, 1)
            dve.wait_ge(mod_saved, 16)
            for g in range(4):
                dve.wait_ge(xT_done, KT + g + 1)
                for i in range(4):
                    k = 4 * g + i
                    o = hT[:, k, NP:NT].rearrange("p (b s) -> p b s", s=NS)
                    src = PB[(KT + g) % 4][:, i * P:(i + 1) * P].rearrange("p (b s) -> p b s", s=NS)
                    ch.mark(TT(o, src, A1T[:, k, 1:9].unsqueeze(2).to_broadcast([P, NB, NS]), ALU.mult))
                ch.sync()
                for i in range(4):
                    k = 4 * g + i
                    o = hT[:, k, NP:NT].rearrange("p (b s) -> p b s", s=NS)
                    m = TT(o, o, modT[:, k, 1:9].unsqueeze(2).to_broadcast([P, NB, NS]), ALU.add)
                m.then_inc(xT_dve, 1)
            V.memset(uP[:, :, 0:CTX], 0.0)
            for c2 in range(4):
                dve.wait_ge(cc_T, c2 + 1)
                CP(uS[:, 2 * c2:2 * c2 + 2, :, 0:CTX].rearrange("p c b k -> p (c b) k"),
                   PB[4 + c2][:, 0:480].rearrange("p (a k) -> p a k", k=CTX)).then_inc(cc_E, 1)
            for c in range(CT):
                dve.wait_ge(z_free, 2 + 8 + c + 1)
                TT(uP[:, c, CTX:], uP[:, c, CTX:], sig[:, c % 2, 0:NP], ALU.mult)
                TT(uS[:, c, :, CTX:], uS[:, c, :, CTX:], sig[:, c % 2, NP:NT].rearrange("p (b s) -> p b s", s=NS),
                   ALU.mult).then_inc(s_u, 1)
            dve.wait_ge(s_u, CT)
            dve.wait_ge(cc_E, 4)
            uSf = uS.rearrange("p c b n -> p (c b) n")
            catf = r12(R2, CT * NT)
            wdf = wdT.rearrange("p c k -> p (c k)")

            def conv(c):
                oP = catf[:, bass.ds(c * NT, NP)]
                oS = catf[:, bass.ds(c * NT + NP, P)].rearrange("p (b s) -> p b s", s=NS)
                uPf = R3[:, 0:CT * UPW]
                uSr = R3[:, CT * UPW:UEND]
                for k in range(WID):
                    w = wdf[:, bass.ds(c * 32 + k, 1)]
                    iP = uPf[:, bass.ds(c * UPW + k, NP)]
                    iS = uSr[:, bass.ds(c * (NB * USW), NB * USW)].rearrange("p (b n) -> p b n", b=NB)[:, :, k:k + NS]
                    if k == 0:
                        ch.mark(TS(oP, iP, w, prmT[:, bass.ds(c + 16, 1)], ALU.mult, ALU.add))
                        ch.mark(TS(oS, iS, w, prmT[:, bass.ds(c + 16, 1)], ALU.mult, ALU.add))
                    else:
                        ch.n -= 1
                        ch.sync()
                        ch.n += 1
                        ch.mark(STT(out=oP, in0=iP, scalar=w, in1=oP, op0=ALU.mult, op1=ALU.add))
                        ch.n -= 1
                        ch.sync()
                        ch.n += 1
                        ch.mark(STT(out=oS, in0=iS, scalar=w, in1=oS, op0=ALU.mult, op1=ALU.add))

            loop(dve, ch, 0, CT, 2 * WID, conv)
            ch.sync()
            dve.sem_inc(s_conv, 1)

            def head_max(h):
                b = h % 2
                dve.wait_ge(s_b[b], 16 * 9 * (h // 2 + 1))
                dve.wait_ge(sc_ready, h + 1)
                if h >= 2:
                    dve.wait_ge(pt_ready, h - 1)
                src = [PB[1][:, 384:512], PB[2][:, 0:256], PB[1][:, 0:384], PB[0][:, :]]
                for i in range(4):
                    ch.mark(STT(out=sP[:, b, i, 384 - P * i:512], in0=src[i], scalar=DH ** -0.5,
                                in1=biasP[:, b, 384 - P * i:512], op0=ALU.mult, op1=ALU.add))
                STT(out=sS[:, b, 0:P], in0=PB[2][:, 256:384], scalar=DH ** -0.5, in1=biasC[:, b],
                    op0=ALU.mult, op1=ALU.add)
                STT(out=sS[:, b, P:2 * P], in0=PB[2][:, 384:512], scalar=DH ** -0.5, in1=blockmask,
                    op0=ALU.mult, op1=ALU.add).then_inc(sc_read, 1)
                ch.sync()
                dve.wait_ge(sc_read, h + 1)
                ch.mark(V.memset(sP[0:DH, b, :, 448:512], NEG))
                n = sS[:, b, P:2 * P].rearrange("p (c s) -> p c s", s=NS)
                ch.mark(TT(n, n, biasN[:, h].unsqueeze(1).to_broadcast([P, NB, NS]), ALU.add))
                ch.sync()
                for i in range(4):
                    V.tensor_reduce(nmax[:, b, i:i + 1], sP[:, b, i, 384 - P * i:512], AX.X, ALU.max, negate=True)
                V.tensor_reduce(nmax[:, b, 4:5], sS[:, b], AX.X, ALU.max, negate=True).then_inc(mx_ready, 1)

            def head_out(h):
                hp, b = divmod(h, 2)
                r = slice(DH * b, DH * b + DH)
                dve.wait_ge(pv_done, h + 1)
                CP(cat[r, CT + hp, 0:NP], PB[6][r, :])
                CP(cat[r, CT + hp, NP:NT], PB[7][r, 0:P]).then_inc(pv_read, 1)

            def head_norm(h):
                b = h % 2
                dve.wait_ge(ex_ready, h + 1)
                ch.link(V.reciprocal(esum[:, b], esum[:, b]))
                for i in range(4):
                    s = sP[:, b, i, 384 - P * i:512]
                    TS(s, s, esum[:, b, i:i + 1], None, ALU.mult)
                TS(sS[:, b], sS[:, b], esum[:, b, 4:5], None, ALU.mult).then_inc(p_ready, 1)

            dve.wait_ge(s_bn, 16 * NB)
            dve.wait_ge(s_const, 3)
            dve.wait_ge(s_q0, 1)
            for i in range(4):
                dve.wait_ge(s_ost[i], 16 * (9 if i == 1 else 1 if i == 3 else 2))
            for h in range(NH + 2):
                if h < NH:
                    if h % 2 == 0:
                        if h >= 2:
                            dve.wait_ge(sc_ready, h)
                        CP(qXd, cat[:, CT + h // 2, NP:NT].rearrange("p (b s) -> p b s", s=NS)).then_inc(s_qx, 1)
                    head_max(h)
                if h >= 2:
                    head_out(h - 2)
                if h < NH:
                    head_norm(h)

            dve.wait_ge(s_mean, 1)
            for c in range(CT):
                TT(cat[:, c, 0:NP], cat[:, c, 0:NP], PB[0][:, :], ALU.subtract)
                TT(cat[:, c, NP:NT], cat[:, c, NP:NT], PB[1][:, 0:P], ALU.subtract).then_inc(s_xc, 1)
            dve.wait_ge(s_ysq_used, CT)
            v, r, t = q2s[:, 0], q2s[:, 1], R3[:, 0:NT]
            dve.wait_ge(pv_done, NH)
            ch.mark(TS(v[:, 0:NP], PB[2][:, :], EPS, None, ALU.add))
            ch.link(TS(v[:, NP:NT], PB[3][:, 0:P], EPS, None, ALU.add))
            dve.sem_inc(s_lnv, 1)
            dve.wait_ge(s_lnr, 1)
            ch.link(V.reciprocal(r, r))
            ch.link(refine(r, v, t))
            for c in range(CT):
                TT(cat[:, c], cat[:, c], r, ALU.mult).then_inc(s_lnx, 1)

            dve.wait_ge(s_x5, 16 * T)
            dve.wait_ge(s_g1, 16 * (1 + NB))
            dve.wait_ge(s_lnx, CT)
            x1f = r12(0, T * D)
            g1f = R3[:, 8192:12288]

            def residual(it):
                for v in range(4 * T):
                    j, t = divmod(v, T)
                    dve.wait_ge(o_done, it * 20 + (v + 1))
                    g = g1f[:, bass.ds(it * 1024 + ((0 if t < TP else D) + j * BW), BW)]
                    xx = x1f[:, bass.ds(it * 1024 + (t * D + j * BW), BW)]
                    ch.link(TT(otmp[:, v % 2], PB[v % 4][:, 0:BW], g, ALU.mult))
                    TT(xx, xx, otmp[:, v % 2], ALU.add).then_inc(o_free, 1)

            loop(dve, ch, 0, 2, 4 * T, residual)
            dve.wait_ge(s_m2, 16 * (2 * (1 + NB) + 1))
            for b in range(2):
                ch.mark(STT(out=A2[:, b], in0=A2[:, b], scalar=1.0, in1=n2g, op0=ALU.add, op1=ALU.mult))
            dve.wait_ge(s_sq, 2 * T)
            ch.link(TS(tmpa, ssq, 1.0 / D, EPS, ALU.mult, ALU.add))
            dve.sem_inc(s_v1, 1)
            dve.wait_ge(s_r1, 2)
            ch.link(V.reciprocal(rs, rs))
            ch.link(refine(rs, tmpa, ssq))
            dve.wait_ge(s_x1s, 16 * T)
            for t in range(T):
                b = 0 if t < TP else 1
                ch.link(STT(out=x1[:, t], in0=x1[:, t], scalar=rs[:, t:t + 1], in1=A2[:, b], op0=ALU.mult, op1=ALU.mult))
                TT(x1[:, t], x1[:, t], B2[:, b], ALU.add).then_inc(s_h2, 1)
            dve.wait_ge(s_h2, T)
            for n in range(16):
                b = n % 2
                dve.wait_ge(s_s, n + 1)
                CP(S[:, 0:TP, n], PB[4 + 2 * b][:, :].rearrange("p (t n) -> p t n", t=TP))
                CP(S[:, TP, n], PB[5 + 2 * b][:, 0:P]).then_inc(s_se, 1)
            dve.wait_ge(s_se, 16)

            A16 = [P, TOPK, TOPK]

            def settle():
                ch.sync()
                dve.sem_inc(dve_passed, 1)

            def top16(vals, idxs, srcs):
                settle()
                for v, s in zip(vals, srcs):
                    ch.mark(V.max(v[:, 0:8], s))
                settle()
                for v, i, s in zip(vals, idxs, srcs):
                    ch.mark(V.max_index(i[:, 0:8], v[:, 0:8], s))
                settle()
                for v, s in zip(vals, srcs):
                    ch.mark(V.match_replace(s, v[:, 0:8], s, -3e38))
                settle()
                for v, s in zip(vals, srcs):
                    ch.mark(V.max(v[:, 8:16], s))
                settle()
                for v, i, s in zip(vals, idxs, srcs):
                    ch.mark(V.max_index(i[:, 8:16], v[:, 8:16], s))
                ch.sync()

            def choose(g):
                ch.mark(CP(tks, Sf[:, bass.ds(g * 256, 256)]))
                rows2 = [tks[:, p * P:(p + 1) * P] for p in range(2)]
                top16([tv2[:, 0:16], tv2[:, 16:32]], [ti2[:, 0:16], ti2[:, 16:32]], rows2)
                c3 = cand.rearrange("p (a b) -> p a b", b=TOPK)
                ch.mark(CP(tf2, ti2))
                ch.link(TT(c3, tv2[:, 0:16].unsqueeze(2).to_broadcast(A16),
                           tv2[:, 16:32].unsqueeze(1).to_broadcast(A16), ALU.add))
                top16([tv], [tpos], [cand])
                TS(tsub, tv, tv[:, 0:1], None, ALU.subtract).then_inc(sub_rdy, 1)
                ch.mark(TS(tau, tpos, 4, None, ALU.logical_shift_right))
                ch.link(TS(tbu, tpos, 15, None, ALU.bitwise_and))
                ch.mark(CP(taf, tau))
                ch.link(CP(tbf, tbu))
                ea, eb = (e.rearrange("p (j a) -> p j a", a=TOPK) for e in (eqa, eqb))
                io = iota_f.unsqueeze(1).to_broadcast(A16)
                ch.mark(TT(ea, io, taf.unsqueeze(2).to_broadcast(A16), ALU.is_equal))
                ch.link(TT(eb, io, tbf.unsqueeze(2).to_broadcast(A16), ALU.is_equal))
                ch.mark(TT(ea, ea, tf2[:, 0:16].unsqueeze(1).to_broadcast(A16), ALU.mult))
                ch.link(TT(eb, eb, tf2[:, 16:32].unsqueeze(1).to_broadcast(A16), ALU.mult))
                ch.mark(V.tensor_reduce(ti0, ea, AX.X, ALU.add))
                ch.link(V.tensor_reduce(ti1, eb, AX.X, ALU.add))
                ch.link(STT(out=tef, in0=ti0, scalar=float(NKEY), in1=ti1, op0=ALU.mult, op1=ALU.add))
                CP(idx_all[:, bass.ds(g * TOPK, TOPK)], tef).then_inc(idx_rdy, 1)
                dve.wait_ge(exp_rdy, g + 1)
                ch.link(V.reciprocal(trc[:, 0:1], tsum[:, 0:1]))
                ch.mark(TS(gates[:, bass.ds(g * TOPK, TOPK)], tex, trc[:, 0:1], None, ALU.mult))

            CHOOSE = 1 + 10 + 2 + 5 + 2 + 2 + 2 + 2 + 2 + 1 + 2

            def dot(g, t):
                for s in range(TOPK):
                    dve.wait_ge(u_in[s % 4], g * 64 + 16 * (s // 4 + 1))
                    u = ux[:, s % 4]
                    V.tensor_tensor_reduce(u, u, x1[:, t], 1.0, 0.0, ALU.mult, ALU.add,
                                           dots[:, s:s + 1]).then_inc(dots_done, 1)

            def add_group(first, g):
                dve.wait_ge(v_used, g * TOPK + 4)
                ch.sync()
                dve.wait_ge(grp_read, g)
                if first:
                    for c in range(4):
                        m = CP(acc[:, c * 512:(c + 1) * 512], PB[c][:, :])
                        if c < 3:
                            ch.mark(m)
                else:
                    for c in range(4):
                        a = acc[:, c * 512:(c + 1) * 512]
                        m = TT(a, PB[c][:, :], a, ALU.add)
                        if c < 3:
                            ch.mark(m)
                m.then_inc(grp_read, 1)

            def weights(g):
                dve.wait_ge(gel_rdy, g + 1)
                dve.wait_ge(dg_rdy, g * TOPK) if not isinstance(g, int) or g > 0 else None
                TT(wgt, gel, gates[:, bass.ds(g * TOPK, TOPK)], ALU.mult).then_inc(w_rdy, 1)

            def finish(t):
                dve.wait_ge(s_x1b, 32 + 16 * t + (16 * NB if t == TP else 0))
                ch.sync()
                dve.wait_ge(grp_read, NPH * (t + 1) + 1)
                ch.link(TT(acc, acc, g2b, ALU.mult))
                TT(acc, acc, x1r, ALU.add).then_inc(f_x2, 1)
                dve.wait_ge(f_sq, t + 1)
                ch.link(TS(fin[:, 1:2], fin[:, 0:1], 1.0 / D, EPS, ALU.mult, ALU.add))
                dve.sem_inc(f_v, 1)
                dve.wait_ge(f_r, t + 1)
                ch.link(V.reciprocal(fin[:, 3:4], fin[:, 2:3]))
                ch.link(refine(fin[:, 3:4], fin[:, 1:2], fin[:, 4:5]))
                ch.link(STT(out=x1r, in0=acc, scalar=fin[:, 3:4], in1=fgb, op0=ALU.mult, op1=ALU.mult))
                dve.sem_inc(s_y, 1)

            dve.wait_ge(s_h2E, 4 * T)
            dve.wait_ge(q_done, 16)
            dve.wait_ge(s_iota, 1)
            ch.link(CP(iota_f, iota_u))
            dve.sem_inc(grp_read, 1)
            choose(0)
            choose(1)
            dve.wait_ge(s_fg, 16)
            for t in range(T):
                g0 = t * NPH
                dot(g0, t)
                if t >= 1:
                    add_group(False, g0)
                    finish(t - 1)
                weights(g0)
                choose(g0 + 2)
                dot(g0 + 1, t)
                add_group(True, g0 + 1)
                weights(g0 + 1)
                choose(g0 + 3)

                def inner(g):
                    dot(g, t)
                    add_group(False, g)
                    weights(g)
                    choose(g + 2)

                last = 2 if t == T - 1 else 0
                loop(dve, ch, g0 + 2, g0 + NPH - last, CHOOSE + 3, inner)
                for i in range(last):
                    g = NG - last + i
                    dot(g, t)
                    add_group(False, g)
                    weights(g)
            add_group(False, NG)
            finish(T - 1)


_INS = ["x_prompt", "x_sample", "c_prompt", "c_sample", "cache_conv", "cache_attn_k", "cache_attn_v", "norm1_g",
        "norm2_g", "w_ada", "b_ada", "w_in", "w_dw", "b_dw", "conv_ln_g", "conv_ln_b", "rel_bias_table", "w_out",
        "w_pq", "sub_keys", "u_experts", "v_experts", "final_g"]
_OUTS = [("y_prompt", (1, 512, 2048)), ("y_sample", (8, 16, 2048)), ("new_conv_prompt", (1, 1, 30, 1024)),
         ("new_k_prompt", (1, 1, 512, 16, 64)), ("new_v_prompt", (1, 1, 512, 16, 64)),
         ("new_conv_sample", (1, 8, 30, 1024)), ("new_k_sample", (1, 8, 16, 16, 64)),
         ("new_v_sample", (1, 8, 16, 16, 64))]


def kernel(**inputs):
    import numpy as _np
    import concourse.bacc as _bacc
    from concourse import mybir as _mybir
    from concourse.bass_utils import run_bass_kernel_spmd as _run

    nc = _bacc.Bacc("TRN2", target_bir_lowering=False, num_devices=1)
    arrays, ins, outs = {}, {}, {}
    for name in _INS:
        a = _np.ascontiguousarray(inputs[name])
        arrays[f"in_{name}"] = a
        ins[name] = nc.dram_tensor(f"in_{name}", a.shape, _mybir.dt.from_np(a.dtype), kind="ExternalInput").ap()
    for name, shape in _OUTS:
        outs[name] = nc.dram_tensor(f"out_{name}", shape, _mybir.dt.float32, kind="ExternalOutput").ap()
    hybrid_encoder_step(nc, ins, outs)
    r = _run(nc, [arrays], core_ids=[0])
    return tuple(r.results[0][f"out_{name}"] for name, _ in _OUTS)
```

```python
import concourse.bass as bass
from concourse import mybir
from contextlib import ExitStack


def hybrid_encoder_step(nc, ins, outs):
    F32 = mybir.dt.float32
    U32 = mybir.dt.uint32
    ALU = mybir.AluOpType
    ACT = mybir.ActivationFunctionType
    AX = mybir.AxisListType

    P = 128
    D = 2048
    KT = D // P
    CC = 1024
    CT = CC // P
    NB, NS = 8, 16
    TP = 4
    T = TP + 1
    NP = TP * P
    NT = T * P
    NCND = 1 + NB
    WID = 31
    CTX = WID - 1
    NH, DH = 16, 64
    EXT = 640
    XLEN = NP + P - 1
    NPH, TOPK, NKEY = 8, 16, 128
    NG = T * NPH
    EPS = 1e-6
    NEG = -1e30
    BW = 256
    GT = 2
    ND = (T - GT) * P
    NEXP = NKEY * NKEY
    NCH = NEXP // P
    NRING = 4

    ctx = ExitStack()
    with ctx:
        def sem(name):
            return ctx.enter_context(nc.semaphore(name))

        R0 = ctx.enter_context(nc.sbuf_tensor("R0", [P, NRING * KT * BW], F32))
        R12 = ctx.enter_context(nc.sbuf_tensor("R12", [P, 2 * T * D], F32))
        R3 = ctx.enter_context(nc.sbuf_tensor("R3", [P, 12400], F32))
        MS = ctx.enter_context(nc.sbuf_tensor("MS", [P, 3776], F32))
        PB = [ctx.enter_context(nc.psum_tensor(f"bank{i}", [P, 512], F32)) for i in range(8)]
        R2 = T * D

        def r12(a, n, p=P):
            return R12[0:p, a:a + n]

        ms_at = [0]

        def misc(n):
            ms_at[0] += n
            return MS[:, ms_at[0] - n:ms_at[0]]

        ring = R0[:, :].rearrange("p (s k n) -> p s k n", s=NRING, k=KT)
        ident = misc(P)
        mean_w = misc(P)
        blockmask = misc(P)
        wdT = misc(8 * 32).rearrange("p (c k) -> p c k", k=32)
        modT = misc(32 * 16).rearrange("p (k c) -> p k c", c=16)
        A1T = misc(16 * 16).rearrange("p (k c) -> p k c", c=16)
        prmT = misc(64)
        biasC = misc(2 * P).rearrange("p (b n) -> p b n", b=2)
        biasN = misc(NH * NS).rearrange("p (h n) -> p h n", h=NH)
        cT = misc(16 * 9).rearrange("p (k c) -> p k c", c=9)
        sm = misc(64)
        skT = misc(2 * NKEY).rearrange("p (h n) -> p h n", h=2)
        VS = misc(1280)
        ssq, rs, tmpa = sm[:, 0:5], sm[:, 8:13], sm[:, 16:21]
        nmax = sm[:, 24:34].rearrange("p (b n) -> p b n", b=2)
        esum = sm[:, 40:50].rearrange("p (b n) -> p b n", b=2)
        mrow = r12(0, 6 * D, NCND)
        cnd = r12(12288, D, NCND)
        prm = r12(14336, P, 40)
        wdw = r12(14464, CC, WID)
        skn = r12(15488, 2 * P).rearrange("p (h n) -> p h n", h=2)
        ext = r12(15744, EXT, NH)
        xt = R3[:, 0:T * D].rearrange("p (t n) -> p t n", t=T)
        junk1 = R3[:, T * D:T * D + D]
        ccx = R3[0:120, T * D:T * D + 2 * CC].rearrange("p (h n) -> p h n", h=2)
        hT = r12(0, KT * NT).rearrange("p (k n) -> p k n", k=KT)
        cat = r12(R2, KT * NT).rearrange("p (k n) -> p k n", k=KT)
        UPW, USW = CTX + NP, CTX + NS
        uP = R3[:, 0:CT * UPW].rearrange("p (c n) -> p c n", c=CT)
        uS = R3[:, CT * UPW:CT * (UPW + NB * USW)].rearrange("p (c b n) -> p c b n", c=CT, b=NB)
        UEND = CT * (UPW + NB * USW)
        kT = R3[:, UEND:UEND + CT * NT].rearrange("p (c n) -> p c n", c=CT)
        sig = VS.rearrange("p (b n) -> p b n", b=2)
        vst = VS[:, 0:1024].rearrange("p (b n) -> p b n", b=4)
        ost = r12(0, 4096).rearrange("p (b n) -> p b n", b=4)
        sP = r12(0, 4096).rearrange("p (b i n) -> p b i n", b=2, i=TP)
        uC = r12(4096, CC).rearrange("p (c n) -> p c n", c=CT)
        pT = r12(4096, 1536)
        sS = r12(5632, 512).rearrange("p (b n) -> p b n", b=2)
        biasP = r12(6144, 1024).rearrange("p (b n) -> p b n", b=2)
        vP = r12(7168, 2 * T * P).rearrange("p (b t n) -> p b t n", b=2, t=T)
        kC = R3[:, 0:2048].rearrange("p (b s n) -> p b s n", b=2, s=NB)
        vC = R3[:, 2048:4096].rearrange("p (b s n) -> p b s n", b=2, s=NB)
        kCT = R3[:, 4096:6144].rearrange("p (b s n) -> p b s n", b=2, s=NB)
        qX = R3[:, 6144:7168].rearrange("p (s n) -> p s n", s=NB)
        qXd = bass.AP(tensor=qX.tensor, offset=qX.offset, ap=[list(qX.ap)[0], [P + NS, NB], [1, NS]])
        x1 = r12(0, T * D).rearrange("p (t n) -> p t n", t=T)
        g1b = R3[:, 8192:12288].rearrange("p (b n) -> p b n", b=2)
        otmp = VS[:, 0:512].rearrange("p (b n) -> p b n", b=2)
        A2 = R3[:, 0:2 * D].rearrange("p (b n) -> p b n", b=2)
        B2 = R3[:, 2 * D:4 * D].rearrange("p (b n) -> p b n", b=2)
        n2g = R3[:, 8192:8192 + D]
        junk2 = R3[:, 10240:10240 + D]
        h2A = r12(R2, KT * GT * P).rearrange("p (k n) -> p k n", k=KT)
        h2B = r12(R2 + KT * GT * P, KT * ND).rearrange("p (k n) -> p k n", k=KT)
        q2s = VS.rearrange("p (b n) -> p b n", b=2)
        S = R3[:, 0:T * D].rearrange("p (t r n) -> p t r n", t=T, r=16)
        Sf = R3[:, 0:T * D]
        idx_all = R3[:, 10240:10880].bitcast(U32)
        gates = R3[:, 10880:11520]
        dstage = R3[:, 11520:11520 + 2 * ND].rearrange("p (b n) -> p b n", b=2)
        ux = R0[:, 0:4 * D].rearrange("p (s n) -> p s n", s=4)
        vx = R0[:, 4 * D:8 * D].rearrange("p (s n) -> p s n", s=4)
        uchunk = [r12(at, D).rearrange("p (q n) -> p q n", q=4) for at in (R2, 4 * D)]
        acc = r12(R2 + D, D)
        x1r, g2b = r12(2 * D, D), r12(3 * D, D)
        fgb = x1[:, 0]
        uT = MS[:, 3776 - D:3776].rearrange("p (k n) -> p k n", k=KT)
        tk_at = [P]

        def tk(n):
            tk_at[0] += n
            return MS[:, tk_at[0] - n:tk_at[0]]

        tv2, ti2, tf2 = tk(32), tk(32).bitcast(U32), tk(32)
        tks, cand = tk(256), tk(256)
        eqa, eqb = cand, tks
        tv, tpos, tau, tbu = tk(16), tk(16).bitcast(U32), tk(16).bitcast(U32), tk(16).bitcast(U32)
        taf, tbf, ti0, ti1, tef, tsub, tex = (tk(16) for _ in range(7))
        tsum, trc = tk(8), tk(8)
        iota_u, iota_f = tk(16).bitcast(U32), tk(16)
        token_u, token_f = tk(8).bitcast(U32), tk(8)
        iu, iv = tk(16).bitcast(U32), tk(16).bitcast(U32)
        ief, ie = tk(16), tk(16).bitcast(U32)
        dots, dots_in, dhold, gel, wgt = (tk(16) for _ in range(5))
        fin = tk(16)
        assert ms_at[0] <= 3776 and tk_at[0] <= 3776 - D
        assert KT * GT * P == 2 * D and (2 + 3) * D <= T * D

        mod_d = nc.dram_tensor("mod_scratch", (NCND, 6 * D), F32)
        ext_d = nc.dram_tensor("ext_scratch", (NH, P, EXT), F32)
        x1_d = nc.dram_tensor("x1_scratch", (T, P, D), F32)
        dots_d = nc.dram_tensor("dots_scratch", (NEXP, ND), F32)

        def rows(t, p, n, off=0):
            return bass.AP(tensor=t, offset=off, ap=[*p, [1, n]])

        xp = ins["x_prompt"].rearrange("o (t p) n -> (o t) p n", p=P)
        xs = ins["x_sample"].rearrange("b s n -> (b s) n")
        kvo = {}
        for kind in "kv":
            kvo[kind, 0] = outs[f"new_{kind}_prompt"].rearrange("l o (t p) h d -> (l o t) p (h d)", p=P)
            kvo[kind, 1] = outs[f"new_{kind}_sample"].rearrange("l b s h d -> (l b s) (h d)")
        kcache = ins["cache_attn_k"].rearrange("l b k h d -> k (l b) (h d)")
        vcache = ins["cache_attn_v"].rearrange("l b k h d -> k (l b) (h d)")
        yp = outs["y_prompt"].rearrange("o (t p) n -> (o t) p n", p=P)
        ys = outs["y_sample"].rearrange("b s n -> (b s) n")
        u_tab = ins["u_experts"].rearrange("l e n -> (l e) n")
        v_tab = ins["v_experts"].rearrange("l e n -> (l e) n")
        wv = {n: ins[n].rearrange("l (k p) n -> p (l k) n", p=P) for n in ("w_ada", "w_in", "w_out", "w_pq")}

        w_in_s = [sem(f"weights_{j}") for j in range(NRING)]
        s_small, s_x, s_cc, s_ext = sem("small_in"), sem("x_in"), sem("conv_cache_in"), sem("ext_saved")
        s_bada = sem("b_ada_in")
        s_const, s_pool = sem("consts"), sem("pool_chain")
        s_silu, s_setT, s_setE = sem("cond_silu"), sem("setup_transposed"), sem("setup_copied")
        mod_done, mod_free, mod_saved = sem("mod_done"), sem("mod_free"), sem("mod_saved")
        s_modT, s_A1 = sem("mod_transposed"), sem("A1_ready")
        s_sq, s_v1, s_r1, s_xn = sem("sumsq"), sem("var_ready"), sem("sqrt_ready"), sem("xn_ready")
        xT_done, xT_act, xT_dve = sem("xT_done"), sem("xT_copied_act"), sem("xT_copied_dve")
        cc_T, cc_E = sem("cc_transposed"), sem("cc_copied")
        z_done, z_free, s_sig, s_u = sem("z_done"), sem("z_free"), sem("sigmoid_ready"), sem("u_ready")
        s_vst = [sem(f"v_stored_{i}") for i in range(4)]
        s_uc, s_oT, s_oE = sem("u_packed"), sem("out_transposed"), sem("out_copied")
        s_ost = [sem(f"rows_stored_{i}") for i in range(4)]
        s_cso = sem("conv_cache_moved")
        s_hp = [sem(f"pair_in_{i}") for i in range(2)]
        s_b = [sem(f"bias_in_{i}") for i in range(2)]
        s_bn, s_q0, s_qx = sem("biasN_in"), sem("qX_zeroed"), sem("qX_ready")
        kct_T, kct_E = sem("kct_transposed"), sem("kct_copied")
        sc_ready, sc_read, mx_ready, ex_ready = sem("scores"), sem("scores_read"), sem("max"), sem("exp")
        p_ready, pt_ready, pt_read, pv_done, pv_read = (sem(n) for n in ("p", "pT", "pT_read", "pv", "pv_read"))
        s_conv, s_mean, s_xc, s_ysq, s_ysq_used = (sem(n) for n in ("conv", "mean", "centred", "ysq", "ysq_used"))
        s_var, s_lnv, s_lnr, s_lnx, s_cat = (sem(n) for n in ("var", "ln_var", "ln_sqrt", "ln_x", "cat_ready"))
        s_x5, s_g1, s_m2 = sem("x_again"), sem("g1_in"), sem("mod2_in")
        o_done, o_free = sem("wout_done"), sem("wout_free")
        s_x1, s_x1s, s_h2, s_h2T, s_h2E = (sem(n) for n in ("x1_ready", "x1_saved", "h2_ready", "h2_T", "h2_copied"))
        q_done, q_read, s_s, s_se = sem("q2_done"), sem("q2_read"), sem("key_scores"), sem("key_scores_read")
        u_in = [sem(f"u_rows_{i}") for i in range(4)]
        v_in = [sem(f"v_rows_{i}") for i in range(4)]
        s_iota = sem("iota")
        idx_rdy, sub_rdy, exp_rdy = sem("idx_ready"), sem("gate_logits"), sem("gate_exp")
        dots_done, dh_rdy, gel_rdy = sem("dots"), sem("dots_held"), sem("gelu")
        v_used, dots_el = sem("v_used"), sem("dots_fetched")
        ch_in = [[sem(f"u_chunk_{b}_{q}") for q in range(4)] for b in range(2)]
        tr_done, uT_rdy, mm_done, sc_out = sem("u_transposed"), sem("uT_ready"), sem("dots_dense"), sem("dots_staged")
        sc_st = [sem(f"dots_stored_{i}") for i in range(2)]
        s_fg, s_x1b, s_y, s_yst = sem("final_g_in"), sem("x1_back"), sem("y_ready"), sem("y_stored")
        f_v, f_r = sem("f_var"), sem("f_sqrt")
        s_dve = sem("dve_chain")
        dve_passed, pool_passed = sem("dve_passed"), sem("pool_passed")

        class Chain:

            def __init__(self, eng, s):
                self.eng, self.s, self.n, self.base = eng, s, 0, 0

            def mark(self, ins):
                ins.then_inc(self.s, 1)
                self.n += 1

            def sync(self):
                self.eng.wait_ge(self.s, self.base + self.n)

            def link(self, ins):
                self.mark(ins)
                self.sync()

        def loop(eng, ch, n0, n1, per, body):
            at = ch.n
            with eng.Fori(n0, n1) as i:
                ch.base = (i - n0) * per if n0 else i * per
                body(i)
                assert ch.n - at == per, (ch.n - at, per)
            ch.base, ch.n = 0, at + per * (n1 - n0)

        GG = GT * NPH
        SEG = [(0, 1), (1, 2), (2, 8), (8, 9), (9, 10), (10, 11), (11, 15), (15, 16), (16, 17), (17, 18), (18, 19),
               (19, 24), (24, 25), (25, 26), (26, 27), (27, 32), (32, 33), (33, 34), (34, 35), (35, 38), (38, 39), (39, 40), (40, 41), (41, 42)]
        CPP = NCH // GG
        assert CPP * GG == NCH and SEG[-1][1] == NG + 2

        def p0_tile(p0):
            return p0 // NPH

        def v_slot(g, p0, s):
            if p0 < GG:
                return vx[:, s % 4], v_in[s % 4], g * 64 + 16 * (s // 4 + 1)
            n, last = g * 32 + 16 * (s // 8 + 1), GG - 2
            if s % 8 < 4:
                return vx[:, s % 4], v_in[s % 4], n + (64 - 32) * last
            return ux[:, s % 4], u_in[s % 4], n + 64 * GG - 32 * last

        def periods(eng, ch, per, body):
            for a, z in SEG:
                if z - a == 1:
                    body(a, a)
                elif ch is None:
                    with eng.Fori(a, z) as p:
                        body(p, a)
                else:
                    loop(eng, ch, a, z, per, lambda p: body(p, a))

        block = ctx.enter_context(nc.Block())

        @block.sync
        def _(sp):
            def load(name, j, col):
                sp.dma_start(ring[:, j], wv[name][:, :, bass.ds(col, BW)]).then_inc(w_in_s[j], 16)

            for j in range(NRING):
                load("w_ada", j, j * BW)
            with sp.Fori(1, 12) as it:
                for j in range(NRING):
                    sp.wait_ge(mod_done, it * 4 + (j - 3))
                    load("w_ada", j, it * (4 * BW) + j * BW)
            for j in range(NRING):
                sp.wait_ge(mod_done, 44 + j + 1)
                load("w_in", j, j * BW)
            with sp.Fori(1, 4) as kd:
                for j in range(NRING):
                    sp.wait_ge(z_done, kd * 8 + (2 * j - 6))
                    load("w_in", j, kd * (4 * BW) + j * BW)
            for j in range(NRING):
                sp.wait_ge(z_done, 24 + 2 * (j + 1))
                load("w_in", j, 4096 + j * BW)
            for j in range(NRING):
                sp.wait_ge(z_done, 32 + 5 * (j + 1))
                load("w_out", j, j * BW)
            for j in range(NRING):
                sp.wait_ge(o_done, 5 * (j + 1))
                load("w_out", j, 1024 + j * BW)
            for j in range(NRING):
                sp.wait_ge(o_done, 20 + 5 * (j + 1))
                load("w_pq", j, j * BW)
            for j in range(NRING):
                sp.wait_ge(q_done, 2 * (j + 1))
                load("w_pq", j, 1024 + j * BW)
            sp.wait_ge(s_h2E, 4 * T)
            sp.wait_ge(s_x1s, 16 * T)
            sp.wait_ge(mod_saved, 16)
            sp.dma_start(g2b, rows(mod_d, [[0, P]], D, 5 * D)).then_inc(s_x1b, 16)
            sp.dma_start(x1r, x1_d[0]).then_inc(s_x1b, 16)

            def chunk_in(n, b, q):
                sp.dma_start(uchunk[b][:, q], u_tab[bass.ds(n * P, P), q * 512:(q + 1) * 512]).then_inc(ch_in[b][q], 16)

            def dots_out(n, b):
                sp.wait_ge(sc_out, n + 3)
                sp.dma_start(dots_d[bass.ds(n * P, P), :], dstage[:, b]).then_inc(sc_st[b], 16)

            sp.wait_ge(q_done, 16)
            for n in range(2):
                for q in range(4):
                    chunk_in(n, n, q)
            for q in range(4):
                sp.wait_ge(tr_done, q + 1)
                chunk_in(2, 0, q)
            with sp.Fori(0, NCH // 2 - 2) as i:
                for b in range(2):
                    for q in range(4):
                        sp.wait_ge(tr_done, i * 8 + (4 * b + q + 5))
                        chunk_in(i * 2 + (b + 3), 1 - b, q)
                    dots_out(i * 2 + b, b)
            for q in range(4):
                sp.wait_ge(tr_done, 4 * (NCH - 3) + q + 1)
                chunk_in(NCH - 1, 1, q)
            for b in range(4):
                dots_out(NCH - 4 + b, b % 2)
            for t in range(T):
                if t >= 1:
                    sp.wait_ge(s_yst, 16 * t)
                if t == TP:
                    for b in range(NB):
                        sp.dma_start(g2b[NS * b:NS * b + NS],
                                     rows(mod_d, [[0, NS]], D, (1 + b) * 6 * D + 5 * D)).then_inc(s_x1b, 16)
                if t >= 1:
                    sp.dma_start(x1r, x1_d[t]).then_inc(s_x1b, 16)
                sp.wait_ge(s_y, t + 1)
                sp.dma_start(yp[t] if t < TP else ys, x1r).then_inc(s_yst, 16)
            sp.wait_ge(s_yst, 16 * T)

        @block.gpsimd
        def _(pool):
            ch = Chain(pool, s_pool)
            dma = pool.dma_start
            dma(cnd[0:1, :], ins["c_prompt"]).then_inc(s_small, 16)
            dma(cnd[1:NCND, :], ins["c_sample"]).then_inc(s_small, 16)
            dma(prm[0:16, :], ins["norm1_g"].rearrange("l (k p) -> (l k) p", p=P)).then_inc(s_small, 16)
            for i, n in enumerate(("b_dw", "conv_ln_g", "conv_ln_b")):
                dma(prm[16 + 8 * i:24 + 8 * i, :], ins[n].rearrange("l (k p) -> (l k) p", p=P)).then_inc(s_small, 16)
            dma(wdw, ins["w_dw"].rearrange("l k c -> (l k) c")).then_inc(s_small, 16)
            dma(skn, ins["sub_keys"].rearrange("l h n d -> n (l h) d")).then_inc(s_small, 16)
            dma(ext[:, 255:EXT - 1], ins["rel_bias_table"].rearrange("l h n -> (l h) n")[:, 0:384]).then_inc(s_small, 16)
            dma(mrow, rows(ins["b_ada"].tensor, [[0, NCND]], 6 * D)).then_inc(s_bada, 16)
            ch.link(pool.memset(ident, 0.0))
            pool.affine_select(out=ident, in_=ident, compare_op=ALU.not_equal, fill=1.0, base=0,
                               pattern=[[-1, P]], channel_multiplier=1).then_inc(s_const, 1)
            pool.memset(mean_w, 1.0 / CC).then_inc(s_const, 1)
            bm = blockmask.rearrange("p (b s) -> p b s", s=NS)
            ch.link(pool.memset(blockmask, 0.0))
            ch.link(pool.affine_select(out=bm, in_=bm, compare_op=ALU.is_ge, fill=NEG, base=0,
                                       pattern=[[-NS, NB], [0, NS]], channel_multiplier=1))
            pool.affine_select(out=bm, in_=bm, compare_op=ALU.is_ge, fill=NEG, base=NS - 1,
                               pattern=[[NS, NB], [0, NS]], channel_multiplier=-1).then_inc(s_const, 1)
            for t in range(TP):
                dma(xt[:, t], xp[t]).then_inc(s_x, 16)
            dma(xt[:, TP], xs).then_inc(s_x, 16)
            dma(outs["new_conv_sample"].rearrange("l b k c -> (l b) k c")[:, 0:CTX - NS, :],
                ins["cache_conv"].rearrange("l b k c -> (l b) k c")[:, NS:CTX, :]).then_inc(s_cso, 16)
            pool.wait_ge(s_setE, 2)
            dma(ext_d[:, :, :], ext.unsqueeze(1).to_broadcast([NH, P, EXT])).then_inc(s_ext, 16)
            pool.wait_ge(s_sq, 5)
            ccv = ins["cache_conv"].rearrange("l (h b) k c -> (l h) (b k) c", h=2)
            for h in range(2):
                dma(ccx[:, h], ccv[h]).then_inc(s_cc, 16)
            pool.wait_ge(mod_free, 4 + 48)
            dma(mod_d[:, 2 * D:], mrow[:, 2 * D:]).then_inc(mod_saved, 16)
            pool.wait_ge(s_ext, 16)
            for b in range(NB):
                dma(biasN[NS * b:NS * b + NS], bass.AP(tensor=ext_d, offset=511,
                    ap=[[EXT - 1, NS], [P * EXT, NH], [1, NS]])).then_inc(s_bn, 16)
            for v in range(4 * T):
                j, t = divmod(v, T)
                pool.wait_ge(z_free, 2 + 32 + v + 1)
                dst = kvo["v", 0][t] if t < TP else kvo["v", 1]
                dma(dst[:, j * BW:(j + 1) * BW], vst[:, v % 4]).then_inc(s_vst[v % 4], 16)
            for i in range(7):
                pool.wait_ge(s_oE, i + 1)
                if i == 0:
                    dma(outs["new_conv_prompt"].rearrange("l o k c -> (l o k) c"), ost[0:CTX, 0]).then_inc(s_ost[0], 16)
                elif i == 1:
                    for b in range(NB):
                        dma(outs["new_conv_sample"].rearrange("l b k c -> (l b) k c")[b, CTX - NS:, :],
                            ost[NS * b:NS * b + NS, 1]).then_inc(s_ost[1], 16)
                else:
                    dma(kvo["k", 0][i - 2] if i < 6 else kvo["k", 1], ost[:, i % 4]).then_inc(s_ost[i % 4], 16)
            for i in range(4):
                pool.wait_ge(s_vst[i], 16 * T)
            pool.wait_ge(s_conv, 1)
            ch.link(pool.memset(qX, 0.0))
            pool.sem_inc(s_q0, 1)
            for h in range(NH):
                hp, b = divmod(h, 2)
                if b == 0:
                    pb = hp % 2
                    if hp >= 2:
                        pool.wait_ge(pv_done, 2 * (hp - 1))
                    cs = slice(hp * P, (hp + 1) * P)
                    dma(vP[:, pb, 0:TP], kvo["v", 0].rearrange("t p n -> p t n")[:, :, cs]).then_inc(s_hp[pb], 16)
                    dma(vP[:, pb, TP], kvo["v", 1][:, cs]).then_inc(s_hp[pb], 16)
                    dma(kC[:, pb], kcache[:, :, cs]).then_inc(s_hp[pb], 16)
                    dma(vC[:, pb], vcache[:, :, cs]).then_inc(s_hp[pb], 16)
                if h >= 2:
                    pool.wait_ge(sc_read, h - 1)
                dma(biasP[:, b], rows(ext_d, [[EXT - 1, P]], 512, h * P * EXT + 127)).then_inc(s_b[b], 16)
                for s in range(NB):
                    dma(biasC[NS * s:NS * s + NS, b], rows(ext_d, [[EXT - 1, NS]], P, h * P * EXT + 383)).then_inc(s_b[b], 16)
            pool.wait_ge(pv_done, NH)
            pool.wait_ge(p_ready, NH)
            for t in range(TP):
                dma(x1[:, t], xp[t]).then_inc(s_x5, 16)
            dma(x1[:, TP], xs).then_inc(s_x5, 16)

            def spread(dst, chunk, s):
                dma(dst(0), rows(mod_d, [[0, P]], D, chunk * D)).then_inc(s, 16)
                for b in range(NB):
                    dma(dst(1)[NS * b:NS * b + NS], rows(mod_d, [[0, NS]], D, (1 + b) * 6 * D + chunk * D)).then_inc(s, 16)

            pool.wait_ge(mod_saved, 16)
            spread(lambda b: g1b[:, b], 2, s_g1)
            pool.wait_ge(s_lnx, 1)
            spread(lambda b: A2[:, b], 4, s_m2)
            spread(lambda b: B2[:, b], 3, s_m2)
            pool.wait_ge(o_free, 4 + 40)
            dma(n2g, rows(ins["norm2_g"].tensor, [[0, P]], D)).then_inc(s_m2, 16)
            for t in range(T):
                dma(x1_d[t], x1[:, t]).then_inc(s_x1s, 16)
            pool.wait_ge(s_h2E, 4 * T)
            pool.iota(iota_u, pattern=[[1, TOPK]], base=0, channel_multiplier=0).then_inc(s_iota, 1)
            pool.iota(token_u, pattern=[[P, 8]], base=0, channel_multiplier=1).then_inc(s_iota, 1)

            HALF = TOPK // 2

            def gather(dst, table, ix, g, s, signal):
                if s % HALF == 0:
                    ch.link(pool.tensor_copy(ix[:, s:s + HALF], idx_all[:, bass.ds(g * TOPK + s, HALF)]))
                pool.sem_inc(pool_passed, 1)
                pool.indirect_dma_start(dst, None, table,
                                        bass.IndirectOffsetOnAxis(ap=ix[:, s:s + 1], axis=0)).then_inc(signal, 16)

            dots_rows = bass.AP(tensor=dots_d, offset=0, ap=[[1, NEXP * ND], [1, 1]])

            def fetch_prepare(p, p0):
                if p0 == GG:
                    for b in range(2):
                        pool.wait_ge(sc_st[b], 16 * NCH // 2)
                else:
                    pool.wait_ge(dots_el, (p - GG) * (16 * TOPK))
                ch.link(pool.tensor_copy(ief, idx_all[:, bass.ds(p * TOPK, TOPK)]))
                pool.sem_inc(pool_passed, 1)
                tile = p0 // NPH - GT
                ch.link(pool.tensor_scalar(ie, ief, float(ND), token_f[:, tile:tile + 1], ALU.mult, ALU.add))
                pool.wait_ge(dh_rdy, p)
                pool.sem_inc(pool_passed, 1)

            def fetch(e):
                pool.indirect_dma_start(dots_in[:, e:e + 1], None, dots_rows,
                                        bass.IndirectOffsetOnAxis(ap=ie[:, e:e + 1], axis=0)).then_inc(dots_el, 16)

            def gathers(p, p0):
                if p0 < GG:
                    pool.wait_ge(idx_rdy, p + 1)
                for s in range(TOPK):
                    if p0 < GG:
                        if p0 >= 1 or s >= 4:
                            pool.wait_ge(dots_done, p * TOPK + (s - 3))
                        elif s % 2 == 0:
                            pool.wait_ge(q_done, 10 + s)
                        gather(ux[:, s % 4], u_tab, iu, p, s, u_in[s % 4])
                    if p0 == 2 and s == 0:
                        pool.wait_ge(q_done, 16)
                    if 2 <= p0 < GG or p0 == GG and s < 4:
                        pool.wait_ge(v_used, (p - 2) * TOPK + (s + 1))
                    elif p0 >= GG:
                        if p0 == GG and s == 4:
                            pool.wait_ge(dots_done, GG * TOPK)
                        pool.wait_ge(v_used, (p - 2) * TOPK + (s - 3))
                    if p0 >= 2:
                        dst, signal, _ = v_slot(p - 2, p0, s)
                        gather(dst, v_tab, iv, p - 2, s, signal)
                    if GG <= p0 < NG and s >= FETCH:
                        if s == FETCH:
                            fetch_prepare(p, p0)
                        for e in fetches[s - FETCH]:
                            fetch(e)

            FETCH = 8
            fetches = [(2 * i, 2 * i + 1) for i in range(8)]
            periods(pool, ch, 4, gathers)
            pool.wait_ge(s_cso, 16)
            pool.wait_ge(s_ost[0], 16 * 2)
            pool.wait_ge(s_ost[1], 16 * (NB + 1))
            pool.wait_ge(s_ost[2], 16 * 2)
            pool.wait_ge(s_ost[3], 16)

        @block.tensor
        def _(pe):
            def tr(out, in_, k):
                return pe.transpose(out, in_, ident[0:k, 0:k])

            pe.wait_ge(s_const, 1)
            pe.wait_ge(s_small, 16 * 9)
            tr(PB[4][:, 0:40], prm, 40).then_inc(s_setT, 1)
            for c in range(CT):
                t = tr(PB[5][:, 32 * c:32 * c + WID], wdw[:, c * P:(c + 1) * P], WID)
            t.then_inc(s_setT, 1)
            for h in range(2):
                t = tr(PB[6][:, h * P:(h + 1) * P], skn[:, h], P)
            t.then_inc(s_setT, 1)
            pe.wait_ge(s_silu, 1)
            for k in range(KT):
                t = tr(PB[7][:, 9 * k:9 * k + 9], cnd[:, k * P:(k + 1) * P], NCND)
            t.then_inc(s_setT, 1)
            pe.wait_ge(s_setE, 6)
            with pe.Fori(0, 12) as it:
                for j in range(NRING):
                    pe.wait_ge(w_in_s[j], it * 16 + 16)
                    pe.wait_ge(mod_free, it * 4 + (j + 1))
                    for k in range(KT):
                        m = pe.matmul(PB[j][0:NCND, 0:BW], cT[:, k, :], ring[:, j, k, :],
                                      start=(k == 0), stop=(k == KT - 1))
                    m.then_inc(mod_done, 1)
            pe.wait_ge(mod_free, 4 + 48)
            for k in range(2 * KT):
                t = tr(PB[4][:, 16 * k:16 * k + 9], mrow[:, k * P:(k + 1) * P], NCND)
            t.then_inc(s_modT, 1)
            pe.wait_ge(s_xn, T)
            for g in range(KT + 4):
                if g >= 4:
                    pe.wait_ge(xT_act, g - 3)
                for i in range(4):
                    src = xt[:, i, g * P:(g + 1) * P] if g < KT else xt[:, TP, (4 * (g - KT) + i) * P:][:, 0:P]
                    t = tr(PB[g % 4][:, i * P:(i + 1) * P], src, P)
                t.then_inc(xT_done, 1)
            pe.wait_ge(s_cc, 32)
            pe.wait_ge(s_A1, 1)
            for c2 in range(4):
                for i in range(4):
                    c, h = 2 * c2 + i // 2, i % 2
                    t = tr(PB[4 + c2][:, i * 120:(i + 1) * 120], ccx[:, h, c * P:(c + 1) * P], 120)
                t.then_inc(cc_T, 1)

            pe.wait_ge(xT_act, KT)
            pe.wait_ge(xT_dve, 4)

            def project(srcs, j, c, par, signal):
                for k in range(KT):
                    w = ring[:, j, k, c * P:(c + 1) * P]
                    for i, src in enumerate(srcs):
                        m = pe.matmul(PB[2 * par + i][:, 0:src.shape[-1]], w, src[:, k],
                                      start=(k == 0), stop=(k == KT - 1))
                m.then_inc(signal, 1)

            with pe.Fori(0, 4) as kd:
                for j in range(NRING):
                    pe.wait_ge(w_in_s[j], kd * 16 + 16 * 13)
                    for c in range(2):
                        pe.wait_ge(z_free, kd * 8 + (2 * j + c + 1))
                        project((hT[:, :, 0:NP], hT[:, :, NP:NT]), j, c, c, z_done)
            for v in range(4 * T):
                j, t = divmod(v, T)
                if t == 0:
                    pe.wait_ge(w_in_s[j], 16 * 17)
                pe.wait_ge(z_free, 32 + v + 1)
                for k in range(KT):
                    m = pe.matmul(PB[2 * (v % 2)][:, 0:BW], hT[:, k, t * P:(t + 1) * P], ring[:, j, k, :],
                                  start=(k == 0), stop=(k == KT - 1))
                m.then_inc(z_done, 1)
            pe.wait_ge(s_u, 8)
            pe.wait_ge(cc_E, 4)
            for i in range(7):
                if i >= 2:
                    pe.wait_ge(s_oE, i - 1)
                if i == 1:
                    pe.wait_ge(s_uc, 1)
                for c in range(CT):
                    src = (uP[:, c, NP:NP + CTX] if i == 0 else uC[:, c] if i == 1
                           else kT[:, c, (i - 2) * P:(i - 1) * P])
                    n = CTX if i == 0 else P
                    t = pe.transpose(PB[4 + 2 * (i % 2) + c // 4][0:n, (c % 4) * P:(c % 4 + 1) * P], src, ident)
                t.then_inc(s_oT, 1)

            def pair_keys(hp):
                b = hp % 2
                pe.wait_ge(s_hp[b], 64 * (hp // 2 + 1))
                if hp == 0:
                    pe.wait_ge(s_oE, 7)
                else:
                    pe.wait_ge(pt_read, 2 * hp - 1)
                for s in range(NB):
                    t = tr(PB[3 + s // 4][:, (s % 4) * P:(s % 4 + 1) * P], kC[:, b, s], P)
                t.then_inc(kct_T, 1)

            def scores(h):
                hp, b = divmod(h, 2)
                r = slice(DH * b, DH * b + DH)
                q, k = cat[r, CT + hp], kT[r, hp]
                if h >= 1:
                    pe.wait_ge(sc_read, h)
                else:
                    pe.wait_ge(z_free, 2 + 52)
                pe.matmul(PB[0][:, 0:512], q[:, 384:512], k[:, 0:512], start=True, stop=True)
                pe.matmul(PB[1][:, 0:384], q[:, 256:384], k[:, 0:384], start=True, stop=True)
                pe.matmul(PB[1][:, 384:512], q[:, 0:128], k[:, 0:128], start=True, stop=True)
                pe.matmul(PB[2][:, 0:256], q[:, 128:256], k[:, 0:256], start=True, stop=True)
                pe.matmul(PB[2][:, 384:512], q[:, NP:NT], k[:, NP:NT], start=True, stop=True)
                pe.wait_ge(s_qx, hp + 1)
                pe.wait_ge(kct_E, hp + 1)
                for s in range(NB):
                    m = pe.matmul(PB[2][:, 256:384], qX[r, s], kCT[r, hp % 2, s], start=(s == 0), stop=(s == NB - 1))
                m.then_inc(sc_ready, 1)

            def weigh(h):
                hp, b = divmod(h, 2)
                pb = hp % 2
                r, vc = slice(DH * b, DH * b + DH), slice(DH * b, DH * b + DH)
                pe.wait_ge(p_ready, h + 1)
                if h >= 1:
                    pe.wait_ge(pt_read, h)
                pe.wait_ge(kct_E, (h + 1) // 2 + 1 if h + 1 < NH else 8)
                for i in range(4):
                    tr(PB[3][:, i * P:(i + 1) * P], sP[:, b, i, 384 - P * i:512 - P * i], P)
                for i in range(1, 4):
                    tr(PB[4][:, (i - 1) * P:i * P], sP[:, b, i, 512 - P * i:640 - P * i], P)
                tr(PB[4][:, 384:512], sP[:, b, 3, 384:512], P)
                for i in range(2, 4):
                    tr(PB[5][:, (i - 2) * P:(i - 1) * P], sP[:, b, i, 640 - P * i:768 - P * i], P)
                tr(PB[5][:, 256:384], sS[:, b, 0:P], P)
                tr(PB[5][:, 384:512], sS[:, b, P:2 * P], P).then_inc(pt_ready, 1)
                pe.wait_ge(pt_read, h + 1)
                if h >= 1:
                    pe.wait_ge(pv_read, h)
                o, os = PB[6][r], PB[7][r]
                pe.matmul(o[:, 0:512], vP[:, pb, 0, vc], pT[:, 0:512], start=True, stop=False)
                pe.matmul(o[:, 128:512], vP[:, pb, 1, vc], pT[:, 512:896], start=False, stop=False)
                pe.matmul(o[:, 256:512], vP[:, pb, 2, vc], pT[:, 1024:1280], start=False, stop=False)
                pe.matmul(o[:, 384:512], vP[:, pb, 3, vc], pT[:, 896:1024], start=False, stop=True)
                pe.matmul(os[:, 0:P], vP[:, pb, 4, vc], pT[:, 1408:1536], start=True, stop=False)
                for s in range(NB):
                    m = pe.matmul(os[:, NS * s:NS * s + NS], vC[:, pb, s, vc],
                                  pT[:, 1280 + NS * s:1280 + NS * s + NS], start=False, stop=(s == NB - 1))
                m.then_inc(pv_done, 1)

            for h in range(NH + 1):
                if h < NH:
                    if h % 2 == 0:
                        pair_keys(h // 2)
                    scores(h)
                if h >= 1:
                    weigh(h - 1)

            def channel_sum(banks, src, wait, used):
                for c in range(CT):
                    if wait is not None:
                        pe.wait_ge(wait, c + 1)
                    pe.matmul(PB[banks][:, 0:NP], mean_w, src(c)[:, 0:NP], start=(c == 0), stop=(c == CT - 1))
                    m = pe.matmul(PB[banks + 1][:, 0:P], mean_w, src(c)[:, NP:NT], start=(c == 0), stop=(c == CT - 1))
                    if used is not None:
                        m.then_inc(used, 1)
                return m

            pe.wait_ge(s_const, 2)
            pe.wait_ge(s_conv, 1)
            pe.wait_ge(sc_read, NH)
            channel_sum(0, lambda c: cat[:, c], None, None).then_inc(s_mean, 1)
            pe.wait_ge(pt_read, NH)
            channel_sum(2, lambda c: q2s[:, c % 2], s_ysq, s_ysq_used)

            pe.wait_ge(s_cat, CT)
            pe.wait_ge(pv_read, NH)
            pe.wait_ge(s_lnv, 1)
            with pe.Fori(0, 2) as it:
                for v in range(4 * T):
                    j, t = divmod(v, T)
                    if t == 0:
                        pe.wait_ge(w_in_s[j], it * 16 + 16 * 18)
                    pe.wait_ge(o_free, it * 20 + (v + 1))
                    for k in range(KT):
                        m = pe.matmul(PB[v % 4][:, 0:BW], cat[:, k, t * P:(t + 1) * P], ring[:, j, k, :],
                                      start=(k == 0), stop=(k == KT - 1))
                    m.then_inc(o_done, 1)
            for t in range(T):
                pe.wait_ge(s_h2, t + 1)
                if t >= 2:
                    pe.wait_ge(s_h2E, 4 * (t - 1))
                for q in range(4):
                    for i in range(4):
                        k = 4 * q + i
                        m = tr(PB[4 * (t % 2) + q][:, i * P:(i + 1) * P], x1[:, t, k * P:(k + 1) * P], P)
                    m.then_inc(s_h2T, 1)

            def key_scores(n):
                b = n % 2
                pe.wait_ge(q_read, n + 1)
                if n >= 2:
                    pe.wait_ge(s_se, n - 1)
                for t in range(TP):
                    pe.matmul(PB[4 + 2 * b][:, t * P:(t + 1) * P], q2s[:, b, t * P:(t + 1) * P], skT[:, n % 2],
                              start=True, stop=True)
                pe.matmul(PB[5 + 2 * b][:, 0:P], q2s[:, b, NP:NT], skT[:, n % 2], start=True, stop=True).then_inc(s_s, 1)

            pe.wait_ge(s_h2E, 4 * T)
            for n in range(16):
                it, j, c = n // 8, (n % 8) // 2, n % 2
                if c == 0:
                    pe.wait_ge(w_in_s[j], 16 * (20 + it))
                if n >= 2:
                    pe.wait_ge(q_read, n - 1)
                project((h2A, h2B), j, c, n % 2, q_done)
                if n >= 1:
                    key_scores(n - 1)
            key_scores(15)

            def turn(b, q):
                for i in range(4):
                    m = tr(PB[q % 2][:, i * P:(i + 1) * P], uchunk[b][:, q, i * P:(i + 1) * P], P)
                m.then_inc(tr_done, 1)

            pe.wait_ge(q_read, 16)
            pe.sem_inc(sc_out, 2)
            for q in range(4):
                pe.wait_ge(ch_in[0][q], 16)
                if q >= 2:
                    pe.wait_ge(uT_rdy, q - 1)
                turn(0, q)

            def products(n, b, more):
                pe.wait_ge(sc_out, n + 1)
                for q in range(4):
                    pe.wait_ge(uT_rdy, n * 4 + (q + 1))
                    for k in range(4 * q, 4 * q + 4):
                        m = pe.matmul(PB[2 + b][:, 0:ND], uT[:, k], h2B[:, k], start=(k == 0), stop=(k == KT - 1))
                    if q == 3:
                        m.then_inc(mm_done, 1)
                    if more:
                        pe.wait_ge(ch_in[1 - b][q], (n - b) * 8 + 16 + 16 * b)
                        pe.wait_ge(uT_rdy, n * 4 + (q + 3))
                        turn(1 - b, q)

            with pe.Fori(0, NCH // 2 - 1) as i:
                for b in range(2):
                    products(i * 2 + b, b, True)
            products(NCH - 2, 0, True)
            products(NCH - 1, 1, False)

        @block.scalar
        def _(act):
            A = nc.scalar.activation
            act.wait_ge(s_small, 16 * 9)
            A(cnd, cnd, ACT.Silu).then_inc(s_silu, 1)
            act.wait_ge(s_x, 16 * T)
            for t in range(T):
                if t >= 1:
                    act.wait_ge(s_sq, t)
                A(junk1, xt[:, t], ACT.Square, accum_out=ssq[:, t:t + 1]).then_inc(s_sq, 1)
            act.wait_ge(s_v1, 1)
            A(rs, tmpa, ACT.Sqrt).then_inc(s_r1, 1)
            act.wait_ge(s_A1, 1)
            act.wait_ge(mod_saved, 16)
            for k in range(KT):
                act.wait_ge(xT_done, k + 1)
                A(hT[:, k, 0:NP], PB[k % 4][:, :], ACT.Identity, scale=A1T[:, k, 0:1],
                  bias=modT[:, k, 0:1]).then_inc(xT_act, 1)
            act.sem_inc(z_free, 2)
            for n in range(32):
                kind, c = divmod(n, 8)
                pa, pb = PB[2 * (n % 2)][:, 0:NP], PB[2 * (n % 2) + 1][:, 0:P]
                act.wait_ge(z_done, n + 1)
                if kind == 0:
                    A(uP[:, c, CTX:], pa, ACT.Copy)
                    A(uS[:, c, :, CTX:], pb.rearrange("p (b s) -> p b s", s=NS), ACT.Copy).then_inc(z_free, 1)
                elif kind == 1:
                    if c >= 2:
                        act.wait_ge(s_u, c - 1)
                    A(sig[:, c % 2, 0:NP], pa, ACT.Sigmoid)
                    A(sig[:, c % 2, NP:NT], pb, ACT.Sigmoid).then_inc(z_free, 1)
                else:
                    dst = cat[:, CT + c] if kind == 2 else kT[:, c]
                    if n == 16:
                        act.wait_ge(cc_E, 4)
                    A(dst[:, 0:NP], pa, ACT.Copy)
                    A(dst[:, NP:NT], pb, ACT.Copy).then_inc(z_free, 1)
            act.wait_ge(s_u, 8)
            for v in range(4 * T):
                act.wait_ge(z_done, 32 + v + 1)
                if v >= 4:
                    act.wait_ge(s_vst[v % 4], 16 * (v // 4))
                A(vst[:, v % 4], PB[2 * (v % 2)][:, 0:BW], ACT.Copy).then_inc(z_free, 1)
            for c in range(CT):
                m = A(uC[:, c].rearrange("p (b s) -> p b s", s=NS), uS[:, c, :, CTX:], ACT.Copy)
            m.then_inc(s_uc, 1)
            for i in range(7):
                n = CTX if i == 0 else P
                act.wait_ge(s_oT, i + 1)
                if i >= 4:
                    act.wait_ge(s_ost[i % 4], 16 * NB if i % 4 == 1 else 16)
                A(ost[0:n, i % 4, 0:512], PB[4 + 2 * (i % 2)][0:n, :], ACT.Copy)
                A(ost[0:n, i % 4, 512:1024], PB[5 + 2 * (i % 2)][0:n, :], ACT.Copy).then_inc(s_oE, 1)

            def copy_pT(h):
                act.wait_ge(pt_ready, h + 1)
                if h >= 1:
                    act.wait_ge(pv_done, h)
                for i in range(3):
                    m = A(pT[:, i * 512:(i + 1) * 512], PB[3 + i][:, :], ACT.Copy)
                m.then_inc(pt_read, 1)

            for h in range(NH + 1):
                if h < NH and h % 2 == 0:
                    hp = h // 2
                    act.wait_ge(kct_T, hp + 1)
                    if hp >= 2:
                        act.wait_ge(sc_ready, 2 * (hp - 1))
                    if hp == 0:
                        act.wait_ge(s_conv, 1)
                    A(kCT[:, hp % 2, 0:4, :], PB[3][:, :].rearrange("p (s n) -> p s n", s=4), ACT.Copy)
                    A(kCT[:, hp % 2, 4:8, :], PB[4][:, :].rearrange("p (s n) -> p s n", s=4), ACT.Copy).then_inc(kct_E, 1)
                if h >= 1:
                    copy_pT(h - 1)
                if h < NH:
                    b = h % 2
                    act.wait_ge(mx_ready, h + 1)
                    for i in range(4):
                        s = sP[:, b, i, 384 - P * i:512]
                        A(s, s, ACT.Exp, bias=nmax[:, b, i:i + 1], accum_out=esum[:, b, i:i + 1])
                    A(sS[:, b], sS[:, b], ACT.Exp, bias=nmax[:, b, 4:5], accum_out=esum[:, b, 4:5]).then_inc(ex_ready, 1)

            for c in range(CT):
                act.wait_ge(s_xc, c + 1)
                if c >= 2:
                    act.wait_ge(s_ysq_used, c - 1)
                A(q2s[:, c % 2], cat[:, c], ACT.Square).then_inc(s_ysq, 1)
            act.wait_ge(s_lnv, 1)
            A(q2s[:, 1], q2s[:, 0], ACT.Sqrt).then_inc(s_lnr, 1)
            for c in range(CT):
                act.wait_ge(s_lnx, c + 1)
                A(cat[:, c], cat[:, c], ACT.Silu, scale=prmT[:, 24 + c:25 + c], bias=prmT[:, 32 + c:33 + c]).then_inc(s_cat, 1)
            act.wait_ge(o_free, 4 + 40)
            for t in range(T):
                if t >= 1:
                    act.wait_ge(s_sq, T + t)
                A(junk2, x1[:, t], ACT.Square, accum_out=ssq[:, t:t + 1]).then_inc(s_sq, 1)
            act.wait_ge(s_v1, 2)
            A(rs, tmpa, ACT.Sqrt).then_inc(s_r1, 1)
            for t in range(T):
                for q in range(4):
                    act.wait_ge(s_h2T, 4 * t + q + 1)
                    dst = h2A[:, :, t * P:(t + 1) * P] if t < GT else h2B[:, :, (t - GT) * P:(t - GT + 1) * P]
                    A(dst[:, 4 * q:4 * q + 4],
                      PB[4 * (t % 2) + q][:, :].rearrange("p (k n) -> p k n", k=4), ACT.Copy).then_inc(s_h2E, 1)
            def gate_exp(g):
                act.wait_ge(sub_rdy, g + 1)
                A(tex, tsub, ACT.Exp, accum_out=tsum[:, 0:1]).then_inc(exp_rdy, 1)

            for n in range(16):
                act.wait_ge(q_done, n + 1)
                if n >= 2:
                    act.wait_ge(s_s, n - 1)
                A(q2s[:, n % 2, 0:GT * P], PB[2 * (n % 2)][:, 0:GT * P], ACT.Copy)
                A(q2s[:, n % 2, GT * P:NT], PB[2 * (n % 2) + 1][:, 0:ND], ACT.Copy).then_inc(q_read, 1)
                if n == 5:
                    gate_exp(0)

            def uT_copy(n):
                for q in range(4):
                    act.wait_ge(tr_done, n * 4 + (q + 1))
                    A(uT[:, 4 * q:4 * q + 4], PB[q % 2][:, :].rearrange("p (k n) -> p k n", k=4),
                      ACT.Copy).then_inc(uT_rdy, 1)

            def scalar_part(p, p0):
                if p0 < GG:
                    for c in range(CPP // 2):
                        dense_step(p, p0, c)
                if p0 < NG - 1:
                    gate_exp(p + 1)
                if 1 <= p0 <= NG:
                    act.wait_ge(dh_rdy, p)
                    A(gel, dhold, ACT.Gelu_apprx_tanh).then_inc(gel_rdy, 1)
                if p0 == NPH + 1:
                    act.wait_ge(dots_done, NPH * TOPK)
                    act.dma_start(fgb, rows(ins["final_g"].tensor, [[0, P]], D)).then_inc(s_fg, 16)
                if p0 >= NPH + 2 and (p0 - 2) % NPH == 0:
                    tile_sqrt((p0 - 2) // NPH - 1)
                if p0 < GG:
                    for c in range(CPP // 2, CPP):
                        dense_step(p, p0, c)

            def dense_step(p, p0, c):
                last = p0 == GG - 1 and c == CPP - 1
                if not last:
                    uT_copy(p * CPP + (c + 1))
                act.wait_ge(mm_done, p * CPP + (c + 1))
                act.wait_ge(sc_st[c % 2], p * (16 * CPP // 2) + 16 * (c // 2))
                A(dstage[:, c % 2], PB[2 + c % 2][:, 0:ND], ACT.Copy).then_inc(sc_out, 1)

            def tile_sqrt(t):
                act.wait_ge(f_v, t + 1)
                A(fin[:, 2:3], fin[:, 1:2], ACT.Sqrt).then_inc(f_r, 1)

            act.wait_ge(s_s, 16)
            uT_copy(0)
            periods(act, None, 0, scalar_part)
            tile_sqrt(T - 1)

        @block.vector
        def _(dve):
            ch = Chain(dve, s_dve)
            V = nc.vector
            STT, TT, TS, CP = V.scalar_tensor_tensor, V.tensor_tensor, V.tensor_scalar, V.tensor_copy

            def refine(r, v, t):
                ch.link(TT(t, r, r, ALU.mult))
                ch.link(TT(t, t, v, ALU.mult))
                ch.link(TS(t, t, -0.5, 1.5, ALU.mult, ALU.add))
                return TT(r, r, t, ALU.mult)

            dve.sem_inc(mod_free, 4)
            dve.sem_inc(o_free, 4)
            dve.wait_ge(s_small, 16 * 9)
            CP(ext[:, 0:255], ext[:, 255:256].to_broadcast([NH, 255])).then_inc(s_setE, 1)
            V.memset(ext[:, EXT - 1:EXT], 0.0).then_inc(s_setE, 1)
            dve.wait_ge(s_setT, 3)
            CP(prmT[:, 0:40], PB[4][:, 0:40]).then_inc(s_setE, 1)
            CP(wdT[:, :, 0:WID], PB[5][:, 0:256].rearrange("p (c k) -> p c k", k=32)[:, :, 0:WID]).then_inc(s_setE, 1)
            CP(skT, PB[6][:, 0:256].rearrange("p (h n) -> p h n", h=2)).then_inc(s_setE, 1)
            dve.wait_ge(s_setT, 4)
            CP(cT, PB[7][:, 0:9 * KT].rearrange("p (k c) -> p k c", c=9)).then_inc(s_setE, 1)
            dve.wait_ge(s_setE, 6)
            dve.wait_ge(s_sq, T)
            ch.link(TS(tmpa, ssq, 1.0 / D, EPS, ALU.mult, ALU.add))
            dve.sem_inc(s_v1, 1)
            dve.wait_ge(s_r1, 1)
            ch.link(V.reciprocal(rs, rs))
            ch.link(refine(rs, tmpa, ssq))
            for t in range(T):
                TS(xt[:, t], xt[:, t], rs[:, t:t + 1], None, ALU.mult).then_inc(s_xn, 1)
            dve.wait_ge(s_bada, 16)
            with dve.Fori(0, 12) as it:
                for j in range(NRING):
                    dve.wait_ge(mod_done, it * 4 + (j + 1))
                    m = mrow[:, bass.ds(it * (4 * BW) + j * BW, BW)]
                    TT(m, PB[j][0:NCND, 0:BW], m, ALU.add).then_inc(mod_free, 1)
            dve.wait_ge(s_modT, 1)
            ch.link(CP(modT[:, :, 0:9], PB[4][:, :].rearrange("p (k c) -> p k c", c=16)[:, :, 0:9]))
            STT(out=A1T[:, :, 0:9], in0=modT[:, KT:, 0:9], scalar=1.0,
                in1=prmT[:, 0:KT].unsqueeze(2).to_broadcast([P, KT, 9]), op0=ALU.add, op1=ALU.mult).then_inc(s_A1, 1)
            dve.wait_ge(s_A1, 1)
            dve.wait_ge(mod_saved, 16)
            for g in range(4):
                dve.wait_ge(xT_done, KT + g + 1)
                for i in range(4):
                    k = 4 * g + i
                    o = hT[:, k, NP:NT].rearrange("p (b s) -> p b s", s=NS)
                    src = PB[(KT + g) % 4][:, i * P:(i + 1) * P].rearrange("p (b s) -> p b s", s=NS)
                    ch.mark(TT(o, src, A1T[:, k, 1:9].unsqueeze(2).to_broadcast([P, NB, NS]), ALU.mult))
                ch.sync()
                for i in range(4):
                    k = 4 * g + i
                    o = hT[:, k, NP:NT].rearrange("p (b s) -> p b s", s=NS)
                    m = TT(o, o, modT[:, k, 1:9].unsqueeze(2).to_broadcast([P, NB, NS]), ALU.add)
                m.then_inc(xT_dve, 1)
            V.memset(uP[:, :, 0:CTX], 0.0)
            for c2 in range(4):
                dve.wait_ge(cc_T, c2 + 1)
                CP(uS[:, 2 * c2:2 * c2 + 2, :, 0:CTX].rearrange("p c b k -> p (c b) k"),
                   PB[4 + c2][:, 0:480].rearrange("p (a k) -> p a k", k=CTX)).then_inc(cc_E, 1)
            for c in range(CT):
                dve.wait_ge(z_free, 2 + 8 + c + 1)
                TT(uP[:, c, CTX:], uP[:, c, CTX:], sig[:, c % 2, 0:NP], ALU.mult)
                TT(uS[:, c, :, CTX:], uS[:, c, :, CTX:], sig[:, c % 2, NP:NT].rearrange("p (b s) -> p b s", s=NS),
                   ALU.mult).then_inc(s_u, 1)
            dve.wait_ge(s_u, CT)
            dve.wait_ge(cc_E, 4)
            uSf = uS.rearrange("p c b n -> p (c b) n")
            catf = r12(R2, CT * NT)
            wdf = wdT.rearrange("p c k -> p (c k)")

            def conv(c):
                oP = catf[:, bass.ds(c * NT, NP)]
                oS = catf[:, bass.ds(c * NT + NP, P)].rearrange("p (b s) -> p b s", s=NS)
                uPf = R3[:, 0:CT * UPW]
                uSr = R3[:, CT * UPW:UEND]
                for k in range(WID):
                    w = wdf[:, bass.ds(c * 32 + k, 1)]
                    iP = uPf[:, bass.ds(c * UPW + k, NP)]
                    iS = uSr[:, bass.ds(c * (NB * USW), NB * USW)].rearrange("p (b n) -> p b n", b=NB)[:, :, k:k + NS]
                    if k == 0:
                        ch.mark(TS(oP, iP, w, prmT[:, bass.ds(c + 16, 1)], ALU.mult, ALU.add))
                        ch.mark(TS(oS, iS, w, prmT[:, bass.ds(c + 16, 1)], ALU.mult, ALU.add))
                    else:
                        ch.n -= 1
                        ch.sync()
                        ch.n += 1
                        ch.mark(STT(out=oP, in0=iP, scalar=w, in1=oP, op0=ALU.mult, op1=ALU.add))
                        ch.n -= 1
                        ch.sync()
                        ch.n += 1
                        ch.mark(STT(out=oS, in0=iS, scalar=w, in1=oS, op0=ALU.mult, op1=ALU.add))

            loop(dve, ch, 0, CT, 2 * WID, conv)
            ch.sync()
            dve.sem_inc(s_conv, 1)

            def head_max(h):
                b = h % 2
                dve.wait_ge(s_b[b], 16 * 9 * (h // 2 + 1))
                dve.wait_ge(sc_ready, h + 1)
                if h >= 2:
                    dve.wait_ge(pt_ready, h - 1)
                src = [PB[1][:, 384:512], PB[2][:, 0:256], PB[1][:, 0:384], PB[0][:, :]]
                for i in range(4):
                    ch.mark(STT(out=sP[:, b, i, 384 - P * i:512], in0=src[i], scalar=DH ** -0.5,
                                in1=biasP[:, b, 384 - P * i:512], op0=ALU.mult, op1=ALU.add))
                STT(out=sS[:, b, 0:P], in0=PB[2][:, 256:384], scalar=DH ** -0.5, in1=biasC[:, b],
                    op0=ALU.mult, op1=ALU.add)
                STT(out=sS[:, b, P:2 * P], in0=PB[2][:, 384:512], scalar=DH ** -0.5, in1=blockmask,
                    op0=ALU.mult, op1=ALU.add).then_inc(sc_read, 1)
                ch.sync()
                dve.wait_ge(sc_read, h + 1)
                ch.mark(V.memset(sP[0:DH, b, :, 448:512], NEG))
                n = sS[:, b, P:2 * P].rearrange("p (c s) -> p c s", s=NS)
                ch.mark(TT(n, n, biasN[:, h].unsqueeze(1).to_broadcast([P, NB, NS]), ALU.add))
                ch.sync()
                for i in range(4):
                    V.tensor_reduce(nmax[:, b, i:i + 1], sP[:, b, i, 384 - P * i:512], AX.X, ALU.max, negate=True)
                V.tensor_reduce(nmax[:, b, 4:5], sS[:, b], AX.X, ALU.max, negate=True).then_inc(mx_ready, 1)

            def head_out(h):
                hp, b = divmod(h, 2)
                r = slice(DH * b, DH * b + DH)
                dve.wait_ge(pv_done, h + 1)
                CP(cat[r, CT + hp, 0:NP], PB[6][r, :])
                CP(cat[r, CT + hp, NP:NT], PB[7][r, 0:P]).then_inc(pv_read, 1)

            def head_norm(h):
                b = h % 2
                dve.wait_ge(ex_ready, h + 1)
                ch.link(V.reciprocal(esum[:, b], esum[:, b]))
                for i in range(4):
                    s = sP[:, b, i, 384 - P * i:512]
                    TS(s, s, esum[:, b, i:i + 1], None, ALU.mult)
                TS(sS[:, b], sS[:, b], esum[:, b, 4:5], None, ALU.mult).then_inc(p_ready, 1)

            dve.wait_ge(s_bn, 16 * NB)
            dve.wait_ge(s_const, 3)
            dve.wait_ge(s_q0, 1)
            for i in range(4):
                dve.wait_ge(s_ost[i], 16 * (9 if i == 1 else 1 if i == 3 else 2))
            for h in range(NH + 2):
                if h < NH:
                    if h % 2 == 0:
                        if h >= 2:
                            dve.wait_ge(sc_ready, h)
                        CP(qXd, cat[:, CT + h // 2, NP:NT].rearrange("p (b s) -> p b s", s=NS)).then_inc(s_qx, 1)
                    head_max(h)
                if h >= 2:
                    head_out(h - 2)
                if h < NH:
                    head_norm(h)

            dve.wait_ge(s_mean, 1)
            for c in range(CT):
                TT(cat[:, c, 0:NP], cat[:, c, 0:NP], PB[0][:, :], ALU.subtract)
                TT(cat[:, c, NP:NT], cat[:, c, NP:NT], PB[1][:, 0:P], ALU.subtract).then_inc(s_xc, 1)
            dve.wait_ge(s_ysq_used, CT)
            v, r, t = q2s[:, 0], q2s[:, 1], R3[:, 0:NT]
            dve.wait_ge(pv_done, NH)
            ch.mark(TS(v[:, 0:NP], PB[2][:, :], EPS, None, ALU.add))
            ch.link(TS(v[:, NP:NT], PB[3][:, 0:P], EPS, None, ALU.add))
            dve.sem_inc(s_lnv, 1)
            dve.wait_ge(s_lnr, 1)
            ch.link(V.reciprocal(r, r))
            ch.link(refine(r, v, t))
            for c in range(CT):
                TT(cat[:, c], cat[:, c], r, ALU.mult).then_inc(s_lnx, 1)

            dve.wait_ge(s_x5, 16 * T)
            dve.wait_ge(s_g1, 16 * (1 + NB))
            dve.wait_ge(s_lnx, CT)
            x1f = r12(0, T * D)
            g1f = R3[:, 8192:12288]

            def residual(it):
                for v in range(4 * T):
                    j, t = divmod(v, T)
                    dve.wait_ge(o_done, it * 20 + (v + 1))
                    g = g1f[:, bass.ds(it * 1024 + ((0 if t < TP else D) + j * BW), BW)]
                    xx = x1f[:, bass.ds(it * 1024 + (t * D + j * BW), BW)]
                    ch.link(TT(otmp[:, v % 2], PB[v % 4][:, 0:BW], g, ALU.mult))
                    TT(xx, xx, otmp[:, v % 2], ALU.add).then_inc(o_free, 1)

            loop(dve, ch, 0, 2, 4 * T, residual)
            dve.wait_ge(s_m2, 16 * (2 * (1 + NB) + 1))
            for b in range(2):
                ch.mark(STT(out=A2[:, b], in0=A2[:, b], scalar=1.0, in1=n2g, op0=ALU.add, op1=ALU.mult))
            dve.wait_ge(s_sq, 2 * T)
            ch.link(TS(tmpa, ssq, 1.0 / D, EPS, ALU.mult, ALU.add))
            dve.sem_inc(s_v1, 1)
            dve.wait_ge(s_r1, 2)
            ch.link(V.reciprocal(rs, rs))
            ch.link(refine(rs, tmpa, ssq))
            dve.wait_ge(s_x1s, 16 * T)
            for t in range(T):
                b = 0 if t < TP else 1
                ch.link(STT(out=x1[:, t], in0=x1[:, t], scalar=rs[:, t:t + 1], in1=A2[:, b], op0=ALU.mult, op1=ALU.mult))
                TT(x1[:, t], x1[:, t], B2[:, b], ALU.add).then_inc(s_h2, 1)
            dve.wait_ge(s_h2, T)
            A16 = [P, TOPK, TOPK]

            def settle():
                ch.sync()
                dve.sem_inc(dve_passed, 1)

            def top16(vals, idxs, srcs):
                settle()
                for v, s in zip(vals, srcs):
                    ch.mark(V.max(v[:, 0:8], s))
                settle()
                for v, i, s in zip(vals, idxs, srcs):
                    ch.mark(V.max_index(i[:, 0:8], v[:, 0:8], s))
                settle()
                for v, s in zip(vals, srcs):
                    ch.mark(V.match_replace(s, v[:, 0:8], s, -3e38))
                settle()
                for v, s in zip(vals, srcs):
                    ch.mark(V.max(v[:, 8:16], s))
                settle()
                for v, i, s in zip(vals, idxs, srcs):
                    ch.mark(V.max_index(i[:, 8:16], v[:, 8:16], s))
                ch.sync()

            def choose(g):
                ch.mark(CP(tks, Sf[:, bass.ds(g * 256, 256)]))
                rows2 = [tks[:, p * P:(p + 1) * P] for p in range(2)]
                top16([tv2[:, 0:16], tv2[:, 16:32]], [ti2[:, 0:16], ti2[:, 16:32]], rows2)
                c3 = cand.rearrange("p (a b) -> p a b", b=TOPK)
                ch.mark(CP(tf2, ti2))
                ch.link(TT(c3, tv2[:, 0:16].unsqueeze(2).to_broadcast(A16),
                           tv2[:, 16:32].unsqueeze(1).to_broadcast(A16), ALU.add))
                top16([tv], [tpos], [cand])
                TS(tsub, tv, tv[:, 0:1], None, ALU.subtract).then_inc(sub_rdy, 1)
                ch.mark(TS(tau, tpos, 4, None, ALU.logical_shift_right))
                ch.link(TS(tbu, tpos, 15, None, ALU.bitwise_and))
                ch.mark(CP(taf, tau))
                ch.link(CP(tbf, tbu))
                ea, eb = (e.rearrange("p (j a) -> p j a", a=TOPK) for e in (eqa, eqb))
                io = iota_f.unsqueeze(1).to_broadcast(A16)
                ch.mark(TT(ea, io, taf.unsqueeze(2).to_broadcast(A16), ALU.is_equal))
                ch.link(TT(eb, io, tbf.unsqueeze(2).to_broadcast(A16), ALU.is_equal))
                ch.mark(TT(ea, ea, tf2[:, 0:16].unsqueeze(1).to_broadcast(A16), ALU.mult))
                ch.link(TT(eb, eb, tf2[:, 16:32].unsqueeze(1).to_broadcast(A16), ALU.mult))
                ch.mark(V.tensor_reduce(ti0, ea, AX.X, ALU.add))
                ch.link(V.tensor_reduce(ti1, eb, AX.X, ALU.add))
                ch.link(STT(out=tef, in0=ti0, scalar=float(NKEY), in1=ti1, op0=ALU.mult, op1=ALU.add))
                CP(idx_all[:, bass.ds(g * TOPK, TOPK)], tef).then_inc(idx_rdy, 1)

            def gate(g):
                dve.wait_ge(exp_rdy, g + 1)
                ch.link(V.reciprocal(trc[:, 0:1], tsum[:, 0:1]))
                ch.mark(TS(gates[:, bass.ds(g * TOPK, TOPK)], tex, trc[:, 0:1], None, ALU.mult))

            def weighted(g, p0, s):
                row, signal, value = v_slot(g, p0, s)
                dve.wait_ge(signal, value)
                dve.wait_ge(v_used, g * TOPK + (s + 4))
                STT(out=acc, in0=row, scalar=wgt[:, s:s + 1], in1=acc,
                    op0=ALU.mult, op1=ALU.add).then_inc(v_used, 1)

            def residual_out(t):
                dve.wait_ge(s_x1b, 32 + 16 * t + (16 * NB if t == TP else 0))
                dve.wait_ge(v_used, 4 + TOPK * NPH * (t + 1))
                ch.link(TT(acc, acc, g2b, ALU.mult))
                ch.link(TT(x1r, x1r, acc, ALU.add))
                ch.link(V.tensor_tensor_reduce(acc, x1r, x1r, 1.0, 0.0, ALU.mult, ALU.add, fin[:, 0:1]))
                ch.link(TS(fin[:, 1:2], fin[:, 0:1], 1.0 / D, EPS, ALU.mult, ALU.add))
                dve.sem_inc(f_v, 1)
                if t < T - 1:
                    ch.link(V.memset(acc, 0.0))

            def final_norm(t):
                dve.wait_ge(f_r, t + 1)
                ch.link(V.reciprocal(fin[:, 3:4], fin[:, 2:3]))
                ch.link(refine(fin[:, 3:4], fin[:, 1:2], fin[:, 4:5]))
                if t == 0:
                    dve.wait_ge(s_fg, 16)
                ch.link(STT(out=x1r, in0=x1r, scalar=fin[:, 3:4], in1=fgb, op0=ALU.mult, op1=ALU.mult))
                dve.sem_inc(s_y, 1)

            def vector_part(p, p0):
                for s in range(TOPK):
                    if p0 < GG:
                        dve.wait_ge(u_in[s % 4], p * 64 + 16 * (s // 4 + 1))
                        u = ux[:, s % 4]
                        V.tensor_tensor_reduce(u, u, x1[:, p0_tile(p0)], 1.0, 0.0, ALU.mult, ALU.add,
                                               dots[:, s:s + 1]).then_inc(dots_done, 1)
                    if p0 >= 2:
                        weighted(p - 2, p0, s)
                if p0 < NG - 1:
                    gate(p + 1)
                if 1 <= p0 <= NG:
                    dve.wait_ge(gel_rdy, p)
                    dve.wait_ge(v_used, (p - 1) * TOPK + 4) if p0 >= 2 else None
                    ch.sync()
                    ch.mark(TT(wgt, gel, gates[:, bass.ds((p - 1) * TOPK, TOPK)], ALU.mult))
                if p0 < NG:
                    if p0 < GG:
                        dve.wait_ge(dots_done, (p + 1) * TOPK)
                    else:
                        dve.wait_ge(dots_el, (p - (GG - 1)) * (16 * TOPK))
                    CP(dhold, dots if p0 < GG else dots_in).then_inc(dh_rdy, 1)
                if p0 < NG - 2:
                    choose(p + 2)
                ch.sync()
                if p0 >= NPH + 1 and (p0 - 1) % NPH == 0:
                    residual_out((p0 - 1) // NPH - 1)
                if p0 >= NPH + 2 and (p0 - 2) % NPH == 0:
                    final_norm((p0 - 2) // NPH - 1)

            dve.wait_ge(s_h2E, 4 * T)
            dve.wait_ge(s_iota, 2)
            ch.mark(CP(iota_f, iota_u))
            ch.link(CP(token_f, token_u))
            for n in range(16):
                b = n % 2
                dve.wait_ge(s_s, n + 1)
                CP(S[:, 0:TP, n], PB[4 + 2 * b][:, :].rearrange("p (t n) -> p t n", t=TP))
                CP(S[:, TP, n], PB[5 + 2 * b][:, 0:P]).then_inc(s_se, 1)
                if n == 1:
                    dve.wait_ge(s_se, 2)
                    choose(0)
                elif n == 8:
                    gate(0)
                elif n == 9:
                    dve.wait_ge(s_se, 4)
                    choose(1)
            dve.wait_ge(s_se, 16)
            dve.wait_ge(q_done, 16)
            ch.link(V.memset(acc, 0.0))
            dve.sem_inc(v_used, 4)
            periods(dve, ch, 1 + 10 + 2 + 5 + 2 + 2 + 2 + 2 + 2 + 1 + 2 + 1, vector_part)
            final_norm(T - 1)


_INS = ["x_prompt", "x_sample", "c_prompt", "c_sample", "cache_conv", "cache_attn_k", "cache_attn_v", "norm1_g",
        "norm2_g", "w_ada", "b_ada", "w_in", "w_dw", "b_dw", "conv_ln_g", "conv_ln_b", "rel_bias_table", "w_out",
        "w_pq", "sub_keys", "u_experts", "v_experts", "final_g"]
_OUTS = [("y_prompt", (1, 512, 2048)), ("y_sample", (8, 16, 2048)), ("new_conv_prompt", (1, 1, 30, 1024)),
         ("new_k_prompt", (1, 1, 512, 16, 64)), ("new_v_prompt", (1, 1, 512, 16, 64)),
         ("new_conv_sample", (1, 8, 30, 1024)), ("new_k_sample", (1, 8, 16, 16, 64)),
         ("new_v_sample", (1, 8, 16, 16, 64))]


def kernel(**inputs):
    import numpy as _np
    import concourse.bacc as _bacc
    from concourse import mybir as _mybir
    from concourse.bass_utils import run_bass_kernel_spmd as _run

    nc = _bacc.Bacc("TRN2", target_bir_lowering=False, num_devices=1)
    arrays, ins, outs = {}, {}, {}
    for name in _INS:
        a = _np.ascontiguousarray(inputs[name])
        arrays[f"in_{name}"] = a
        ins[name] = nc.dram_tensor(f"in_{name}", a.shape, _mybir.dt.from_np(a.dtype), kind="ExternalInput").ap()
    for name, shape in _OUTS:
        outs[name] = nc.dram_tensor(f"out_{name}", shape, _mybir.dt.float32, kind="ExternalOutput").ap()
    hybrid_encoder_step(nc, ins, outs)
    r = _run(nc, [arrays], core_ids=[0])
    return tuple(r.results[0][f"out_{name}"] for name, _ in _OUTS)
```

```python
import concourse.bass as bass
from concourse import mybir
from contextlib import ExitStack


def hybrid_encoder_step(nc, ins, outs):
    F32 = mybir.dt.float32
    U32 = mybir.dt.uint32
    ALU = mybir.AluOpType
    ACT = mybir.ActivationFunctionType
    AX = mybir.AxisListType

    P = 128
    D = 2048
    KT = D // P
    CC = 1024
    CT = CC // P
    NB, NS = 8, 16
    TP = 4
    T = TP + 1
    NP = TP * P
    NT = T * P
    NCND = 1 + NB
    WID = 31
    CTX = WID - 1
    NH, DH = 16, 64
    EXT = 640
    XLEN = NP + P - 1
    NPH, TOPK, NKEY = 8, 16, 128
    NG = T * NPH
    EPS = 1e-6
    NEG = -1e30
    BW = 256
    GT = 2
    ND = (T - GT) * P
    NEXP = NKEY * NKEY
    NCH = NEXP // P
    NRING = 4

    ctx = ExitStack()
    with ctx:
        def sem(name):
            return ctx.enter_context(nc.semaphore(name))

        R0 = ctx.enter_context(nc.sbuf_tensor("R0", [P, NRING * KT * BW], F32))
        R12 = ctx.enter_context(nc.sbuf_tensor("R12", [P, 2 * T * D], F32))
        R3 = ctx.enter_context(nc.sbuf_tensor("R3", [P, 12400], F32))
        MS = ctx.enter_context(nc.sbuf_tensor("MS", [P, 3776], F32))
        PB = [ctx.enter_context(nc.psum_tensor(f"bank{i}", [P, 512], F32)) for i in range(8)]
        R2 = T * D

        def r12(a, n, p=P):
            return R12[0:p, a:a + n]

        ms_at = [0]

        def misc(n):
            ms_at[0] += n
            return MS[:, ms_at[0] - n:ms_at[0]]

        ring = R0[:, :].rearrange("p (s k n) -> p s k n", s=NRING, k=KT)
        ident = misc(P)
        mean_w = misc(P)
        blockmask = misc(P)
        wdT = misc(8 * 32).rearrange("p (c k) -> p c k", k=32)
        modT = misc(32 * 16).rearrange("p (k c) -> p k c", c=16)
        A1T = misc(16 * 16).rearrange("p (k c) -> p k c", c=16)
        prmT = misc(64)
        biasC = misc(2 * P).rearrange("p (b n) -> p b n", b=2)
        biasN = misc(NH * NS).rearrange("p (h n) -> p h n", h=NH)
        cT = misc(16 * 9).rearrange("p (k c) -> p k c", c=9)
        sm = misc(64)
        skT = misc(2 * NKEY).rearrange("p (h n) -> p h n", h=2)
        VS = misc(1280)
        part = sm[:, 24:44].rearrange("p (t c) -> p t c", c=4)
        ssq, rs, tmpa = sm[:, 0:5], sm[:, 8:13], sm[:, 16:21]
        nmax = sm[:, 24:34].rearrange("p (b n) -> p b n", b=2)
        esum = sm[:, 40:50].rearrange("p (b n) -> p b n", b=2)
        mrow = r12(0, 2 * D, NCND)
        mrow2 = r12(R2, 4 * D, NCND)
        cnd = r12(4096, D, NCND)
        prm = r12(6144, P, 40)
        wdw = r12(6272, CC, WID)
        skn = r12(7296, 2 * P).rearrange("p (h n) -> p h n", h=2)
        ext = r12(18432, EXT, NH)
        xt = R3[:, 0:T * D].rearrange("p (t n) -> p t n", t=T)
        junk1 = R3[:, T * D:T * D + D]
        ccx = R3[0:120, T * D:T * D + 2 * CC].rearrange("p (h n) -> p h n", h=2)
        hT = r12(0, KT * NT).rearrange("p (k n) -> p k n", k=KT)
        cat = r12(R2, KT * NT).rearrange("p (k n) -> p k n", k=KT)
        UPW, USW = CTX + NP, CTX + NS
        uP = R3[:, 0:CT * UPW].rearrange("p (c n) -> p c n", c=CT)
        uS = R3[:, CT * UPW:CT * (UPW + NB * USW)].rearrange("p (c b n) -> p c b n", c=CT, b=NB)
        UEND = CT * (UPW + NB * USW)
        kT = R3[:, UEND:UEND + CT * NT].rearrange("p (c n) -> p c n", c=CT)
        sig = VS.rearrange("p (b n) -> p b n", b=2)
        vst = VS[:, 0:1024].rearrange("p (b n) -> p b n", b=4)
        ost = r12(0, 4096).rearrange("p (b n) -> p b n", b=4)
        sP = r12(0, 4096).rearrange("p (b i n) -> p b i n", b=2, i=TP)
        uC = r12(4096, CC).rearrange("p (c n) -> p c n", c=CT)
        pT = r12(4096, 1536)
        sS = r12(5632, 512).rearrange("p (b n) -> p b n", b=2)
        biasP = r12(6144, 1024).rearrange("p (b n) -> p b n", b=2)
        vP = r12(7168, 2 * T * P).rearrange("p (b t n) -> p b t n", b=2, t=T)
        kC = R3[:, 0:2048].rearrange("p (b s n) -> p b s n", b=2, s=NB)
        vC = R3[:, 2048:4096].rearrange("p (b s n) -> p b s n", b=2, s=NB)
        kCT = R3[:, 4096:6144].rearrange("p (b s n) -> p b s n", b=2, s=NB)
        qX = R3[:, 6144:7168].rearrange("p (s n) -> p s n", s=NB)
        qXd = bass.AP(tensor=qX.tensor, offset=qX.offset, ap=[list(qX.ap)[0], [P + NS, NB], [1, NS]])
        x1 = r12(0, T * D).rearrange("p (t n) -> p t n", t=T)
        g1b = R3[:, 8192:12288].rearrange("p (b n) -> p b n", b=2)
        otmp = VS[:, 0:512].rearrange("p (b n) -> p b n", b=2)
        A2 = R3[:, 0:2 * D].rearrange("p (b n) -> p b n", b=2)
        B2 = R3[:, 2 * D:4 * D].rearrange("p (b n) -> p b n", b=2)
        n2g = B2[:, 0]
        h2A = r12(R2, KT * GT * P).rearrange("p (k n) -> p k n", k=KT)
        h2B = r12(R2 + KT * GT * P, KT * ND).rearrange("p (k n) -> p k n", k=KT)
        q2s = VS.rearrange("p (b n) -> p b n", b=2)
        S = R3[:, 0:T * D].rearrange("p (t r n) -> p t r n", t=T, r=16)
        Sf = R3[:, 0:T * D]
        idx_all = R3[:, 10240:10880].bitcast(U32)
        gates = R3[:, 10880:11520]
        wq = [R0[:, 8192:10240], R0[:, 10240:12288], x1[:, 1]]
        wq = [w.rearrange("p (k n) -> p k n", k=KT) for w in wq]
        dstage = R3[:, 11520:11520 + 2 * ND].rearrange("p (b n) -> p b n", b=2)
        ux = R0[:, 0:4 * D].rearrange("p (s n) -> p s n", s=4)
        vx = [x1[:, 2], x1[:, 3], x1[:, 4], R0[:, 7 * D:8 * D]]
        uchunk = [r12(R2 + b * D, D).rearrange("p (q n) -> p q n", q=4) for b in range(2)]
        x1r, g2b, acc = (R0[:, i * D:(i + 1) * D] for i in (4, 5, 6))
        fgb = x1[:, 0]
        uT = MS[:, 3776 - D:3776].rearrange("p (k n) -> p k n", k=KT)
        tk_at = [P]

        def tk(n):
            tk_at[0] += n
            return MS[:, tk_at[0] - n:tk_at[0]]

        tv2, ti2, tf2 = tk(32), tk(32).bitcast(U32), tk(32)
        tks, cand = tk(256), tk(256)
        eqa, eqb = cand, tks
        tv, tpos, tau, tbu = tk(16), tk(16).bitcast(U32), tk(16).bitcast(U32), tk(16).bitcast(U32)
        taf, tbf, ti0, ti1, tef, tsub, tex = (tk(16) for _ in range(7))
        tsum, trc = tk(8), tk(8)
        iota_u, iota_f = tk(16).bitcast(U32), tk(16)
        token_u, token_f = tk(8).bitcast(U32), tk(8)
        iu, iv = tk(16).bitcast(U32), tk(16).bitcast(U32)
        ief, ie = tk(16), tk(16).bitcast(U32)
        dots, dots_in, dhold, gel, wgt = (tk(16) for _ in range(5))
        fin = tk(16)
        assert ms_at[0] <= 3776 and tk_at[0] <= 3776 - D
        assert KT * GT * P == 2 * D and (2 + 3) * D <= T * D

        mod_d = nc.dram_tensor("mod_scratch", (NCND, 6 * D), F32)
        ext_d = nc.dram_tensor("ext_scratch", (NH, P, EXT), F32)
        biasC_d = nc.dram_tensor("biasC_scratch", (NH, P, P), F32)
        x1_d = nc.dram_tensor("x1_scratch", (T, P, D), F32)
        h2_d = nc.dram_tensor("h2_scratch", (P, D), F32)
        dots_d = nc.dram_tensor("dots_scratch", (NEXP, ND), F32)

        def rows(t, p, n, off=0):
            return bass.AP(tensor=t, offset=off, ap=[*p, [1, n]])

        xp = ins["x_prompt"].rearrange("o (t p) n -> (o t) p n", p=P)
        xs = ins["x_sample"].rearrange("b s n -> (b s) n")
        kvo = {}
        for kind in "kv":
            kvo[kind, 0] = outs[f"new_{kind}_prompt"].rearrange("l o (t p) h d -> (l o t) p (h d)", p=P)
            kvo[kind, 1] = outs[f"new_{kind}_sample"].rearrange("l b s h d -> (l b s) (h d)")
        kcache = ins["cache_attn_k"].rearrange("l b k h d -> k (l b) (h d)")
        vcache = ins["cache_attn_v"].rearrange("l b k h d -> k (l b) (h d)")
        yp = outs["y_prompt"].rearrange("o (t p) n -> (o t) p n", p=P)
        ys = outs["y_sample"].rearrange("b s n -> (b s) n")
        u_tab = ins["u_experts"].rearrange("l e n -> (l e) n")
        v_tab = ins["v_experts"].rearrange("l e n -> (l e) n")
        wv = {n: ins[n].rearrange("l (k p) n -> p (l k) n", p=P) for n in ("w_ada", "w_in", "w_out", "w_pq")}

        w_in_s = [sem(f"weights_{j}") for j in range(NRING)]
        s_small, s_x, s_cc, s_ext = sem("small_in"), sem("x_in"), sem("conv_cache_in"), sem("ext_saved")
        s_bada = sem("b_ada_in")
        s_const, s_pool = sem("consts"), sem("pool_chain")
        s_silu, s_setT, s_setE = sem("cond_silu"), sem("setup_transposed"), sem("setup_copied")
        mod_done, mod_free, mod_saved = sem("mod_done"), sem("mod_free"), sem("mod_saved")
        s_modT, s_A1 = sem("mod_transposed"), sem("A1_ready")
        s_sq, s_v1, s_r1, s_xn = sem("sumsq"), sem("var_ready"), sem("sqrt_ready"), sem("xn_ready")
        xT_done, xT_act, xT_dve = sem("xT_done"), sem("xT_copied_act"), sem("xT_copied_dve")
        cc_T, cc_E = sem("cc_transposed"), sem("cc_copied")
        z_done, z_free, s_sig, s_u = sem("z_done"), sem("z_free"), sem("sigmoid_ready"), sem("u_ready")
        s_vst = [sem(f"v_stored_{i}") for i in range(4)]
        s_uc, s_oT, s_oE = sem("u_packed"), sem("out_transposed"), sem("out_copied")
        s_ost = [sem(f"rows_stored_{i}") for i in range(4)]
        s_cso = sem("conv_cache_moved")
        s_hp = [sem(f"pair_in_{i}") for i in range(2)]
        s_kc = [sem(f"k_cache_in_{i}") for i in range(2)]
        s_bc = sem("biasC_saved")
        s_b = [sem(f"bias_in_{i}") for i in range(2)]
        s_bn, s_q0, s_qx = sem("biasN_in"), sem("qX_zeroed"), sem("qX_ready")
        kct_T, kct_E = sem("kct_transposed"), sem("kct_copied")
        sc_ready, sc_read, mx_ready, ex_ready = sem("scores"), sem("scores_read"), sem("max"), sem("exp")
        p_ready, pt_ready, pt_read, pv_done, pv_read = (sem(n) for n in ("p", "pT", "pT_read", "pv", "pv_read"))
        s_conv, s_mean, s_xc, s_ysq, s_ysq_used = (sem(n) for n in ("conv", "mean", "centred", "ysq", "ysq_used"))
        s_var, s_lnv, s_lnr, s_lnx, s_cat = (sem(n) for n in ("var", "ln_var", "ln_sqrt", "ln_x", "cat_ready"))
        s_x5, s_g1, s_m2 = sem("x_again"), sem("g1_in"), sem("mod2_in")
        o_done, o_free = sem("wout_done"), sem("wout_free")
        s_h2, s_h2T, s_h2E = sem("h2_ready"), sem("h2_T"), sem("h2_copied")
        q_done, q_read, s_s, s_se = sem("q2_done"), sem("q2_read"), sem("key_scores"), sem("key_scores_read")
        u_in = [sem(f"u_rows_{i}") for i in range(4)]
        v_in = [sem(f"v_rows_{i}") for i in range(4)]
        s_iota = sem("iota")
        idx_rdy, sub_rdy, exp_rdy = sem("idx_ready"), sem("gate_logits"), sem("gate_exp")
        dots_done, dh_rdy, gel_rdy = sem("dots"), sem("dots_held"), sem("gelu")
        v_used, dots_el = sem("v_used"), sem("dots_fetched")
        ch_in = [[sem(f"u_chunk_{b}_{q}") for q in range(4)] for b in range(2)]
        tr_done, uT_rdy, mm_done, sc_out = sem("u_transposed"), sem("uT_ready"), sem("dots_dense"), sem("dots_staged")
        sc_st = [sem(f"dots_stored_{i}") for i in range(2)]
        w_q = [sem(f"w_pq_{i}") for i in range(3)]
        s_x1t = [sem(f"x1_saved_{t}") for t in range(T)]
        s_n2, s_A2 = sem("n2g_in"), sem("A2_ready")
        s_h2s, s_h2b = sem("h2_saved"), sem("h2_back")
        s_fg, s_x1b, s_y, s_yst = sem("final_g_in"), sem("x1_back"), sem("y_ready"), sem("y_stored")
        f_v, f_r = sem("f_var"), sem("f_sqrt")
        s_dve = sem("dve_chain")
        dve_passed, pool_passed = sem("dve_passed"), sem("pool_passed")

        class Chain:

            def __init__(self, eng, s):
                self.eng, self.s, self.n, self.base = eng, s, 0, 0

            def mark(self, ins):
                ins.then_inc(self.s, 1)
                self.n += 1

            def sync(self):
                self.eng.wait_ge(self.s, self.base + self.n)

            def link(self, ins):
                self.mark(ins)
                self.sync()

        def loop(eng, ch, n0, n1, per, body):
            at = ch.n
            with eng.Fori(n0, n1) as i:
                ch.base = (i - n0) * per if n0 else i * per
                body(i)
                assert ch.n - at == per, (ch.n - at, per)
            ch.base, ch.n = 0, at + per * (n1 - n0)

        GG = GT * NPH
        cuts = [0, 1, 2, 3, 4, 8, 9, 10, 11, 15, 16, 17, 18, 19, 24, 25, 26, 27, 32, 33, 34, 35, 38, 39, 40, 41, 42]
        SEG = list(zip(cuts, cuts[1:]))
        EARLY = 4
        CPP = 10
        CP0 = NCH - CPP * (GG - EARLY)
        assert CP0 % 2 == 0 and CPP % 2 == 0 and SEG[-1][1] == NG + 2

        def v_slot(g, p0, s):
            if p0 < GG:
                return vx[s % 4], v_in[s % 4], g * 64 + 16 * (s // 4 + 1)
            n, last = g * 32 + 16 * (s // 8 + 1), GG - 2
            if s % 8 < 4:
                return vx[s % 4], v_in[s % 4], n + (64 - 32) * last
            return ux[:, s % 4], u_in[s % 4], n + 64 * GG - 32 * last

        def periods(eng, ch, per, body):
            for a, z in SEG:
                if z - a == 1:
                    body(a, a)
                elif ch is None:
                    with eng.Fori(a, z) as p:
                        body(p, a)
                else:
                    loop(eng, ch, a, z, per, lambda p: body(p, a))

        NM1, NM = 2 * D // BW, 6 * D // BW
        ring_adj = [16 * (n - 14) for n in (8, 8, 20, 20)]

        block = ctx.enter_context(nc.Block())

        @block.sync
        def _(sp):
            def load(name, j, col):
                sp.dma_start(ring[:, j], wv[name][:, :, bass.ds(col, BW)]).then_inc(w_in_s[j], 16)

            for j in range(NRING):
                load("w_ada", j, j * BW)
            with sp.Fori(1, NM1 // 4) as it:
                for j in range(NRING):
                    sp.wait_ge(mod_done, it * 4 + (j - 3))
                    load("w_ada", j, it * (4 * BW) + j * BW)
            for j in range(2):
                sp.wait_ge(mod_done, NM1 - 4 + j + 1)
                load("w_in", j, j * BW)
            for j in range(2):
                sp.wait_ge(mod_done, NM1 - 2 + j + 1)
                load("w_ada", 2 + j, (NM1 + j) * BW)

            def beside(w, b, more):
                for a in range(2, 6 if more else 4):
                    sp.wait_ge(mod_done, w * 4 + (NM1 + a - 1))
                    load("w_ada", 2 + a % 2, w * (4 * BW) + (NM1 + a) * BW)
                if more:
                    sp.wait_ge(z_done, w * 2 + 2)
                    load("w_in", b, w * BW + 2 * BW)

            with sp.Fori(0, 3) as i:
                for b in range(2):
                    beside(i * 2 + b, b, True)
            beside(6, 0, True)
            beside(7, 1, False)
            sp.wait_ge(z_done, 16)
            load("w_in", 1, 9 * BW)
            for j in range(2, 4):
                sp.wait_ge(mod_done, NM - 3 + j)
                load("w_in", j, (8 + j) * BW)
            for j in range(NRING):
                sp.wait_ge(z_done, 16 + 2 * (j + 1))
                load("w_in", j, 3072 + j * BW)
            for j in range(NRING):
                sp.wait_ge(z_done, 24 + 2 * (j + 1))
                load("w_in", j, 4096 + j * BW)
            for j in range(NRING):
                sp.wait_ge(z_done, 32 + 5 * (j + 1))
                load("w_out", j, j * BW)
            for j in range(NRING):
                sp.wait_ge(o_done, 5 * (j + 1))
                load("w_out", j, 1024 + j * BW)
            def load_pq(n):
                sp.dma_start(wq[n % 3], wv["w_pq"][:, :, n * P:(n + 1) * P]).then_inc(w_q[n % 3], 16)

            sp.wait_ge(o_done, 35)
            load_pq(0)
            load_pq(1)
            sp.wait_ge(s_h2, 2)
            sp.dma_start(h2_d[:, :], x1[:, 1]).then_inc(s_h2s, 16)
            sp.wait_ge(s_h2s, 16)
            sp.wait_ge(s_h2E, 8)
            load_pq(2)
            for n in range(3, 2 * NPH):
                sp.wait_ge(q_done, n - 2)
                load_pq(n)

            def chunk_in(n, b, q):
                sp.dma_start(uchunk[b][:, q], u_tab[bass.ds(n * P, P), q * 512:(q + 1) * 512]).then_inc(ch_in[b][q], 16)

            def dots_out(n, b):
                sp.wait_ge(sc_out, n + 3)
                sp.dma_start(dots_d[bass.ds(n * P, P), :], dstage[:, b]).then_inc(sc_st[b], 16)

            sp.wait_ge(q_done, 16)
            for n in range(2):
                for q in range(4):
                    chunk_in(n, n, q)
            sp.dma_start(x1[:, 1], h2_d[:, :]).then_inc(s_h2b, 16)
            sp.wait_ge(s_x1t[0], 16)
            sp.wait_ge(mod_saved, 16)
            sp.dma_start(g2b, rows(mod_d, [[0, P]], D, 5 * D)).then_inc(s_x1b, 16)
            sp.dma_start(x1r, x1_d[0]).then_inc(s_x1b, 16)
            for q in range(4):
                sp.wait_ge(tr_done, q + 1)
                chunk_in(2, 0, q)
            with sp.Fori(0, NCH // 2 - 2) as i:
                for b in range(2):
                    for q in range(4):
                        sp.wait_ge(tr_done, i * 8 + (4 * b + q + 5))
                        chunk_in(i * 2 + (b + 3), 1 - b, q)
                    dots_out(i * 2 + b, b)
            for q in range(4):
                sp.wait_ge(tr_done, 4 * (NCH - 3) + q + 1)
                chunk_in(NCH - 1, 1, q)
            for b in range(4):
                dots_out(NCH - 4 + b, b % 2)
            for t in range(T):
                if t >= 1:
                    sp.wait_ge(s_yst, 16 * t)
                if t == TP:
                    for b in range(NB):
                        sp.dma_start(g2b[NS * b:NS * b + NS],
                                     rows(mod_d, [[0, NS]], D, (1 + b) * 6 * D + 5 * D)).then_inc(s_x1b, 16)
                if t >= 1:
                    sp.wait_ge(s_x1t[t], 16)
                    sp.dma_start(x1r, x1_d[t]).then_inc(s_x1b, 16)
                sp.wait_ge(s_y, t + 1)
                sp.dma_start(yp[t] if t < TP else ys, x1r).then_inc(s_yst, 16)
            sp.wait_ge(s_yst, 16 * T)

        @block.gpsimd
        def _(pool):
            ch = Chain(pool, s_pool)
            dma = pool.dma_start
            dma(cnd[0:1, :], ins["c_prompt"]).then_inc(s_small, 16)
            dma(cnd[1:NCND, :], ins["c_sample"]).then_inc(s_small, 16)
            dma(prm[0:16, :], ins["norm1_g"].rearrange("l (k p) -> (l k) p", p=P)).then_inc(s_small, 16)
            for i, n in enumerate(("b_dw", "conv_ln_g", "conv_ln_b")):
                dma(prm[16 + 8 * i:24 + 8 * i, :], ins[n].rearrange("l (k p) -> (l k) p", p=P)).then_inc(s_small, 16)
            dma(wdw, ins["w_dw"].rearrange("l k c -> (l k) c")).then_inc(s_small, 16)
            dma(skn, ins["sub_keys"].rearrange("l h n d -> n (l h) d")).then_inc(s_small, 16)
            dma(ext[:, 255:EXT - 1], ins["rel_bias_table"].rearrange("l h n -> (l h) n")[:, 0:384]).then_inc(s_small, 16)
            dma(mrow, rows(ins["b_ada"].tensor, [[0, NCND]], 2 * D)).then_inc(s_bada, 16)
            dma(mrow2, rows(ins["b_ada"].tensor, [[0, NCND]], 4 * D, 2 * D)).then_inc(s_bada, 16)
            ch.link(pool.memset(ident, 0.0))
            pool.affine_select(out=ident, in_=ident, compare_op=ALU.not_equal, fill=1.0, base=0,
                               pattern=[[-1, P]], channel_multiplier=1).then_inc(s_const, 1)
            pool.memset(mean_w, 1.0 / CC).then_inc(s_const, 1)
            bm = blockmask.rearrange("p (b s) -> p b s", s=NS)
            ch.link(pool.memset(blockmask, 0.0))
            ch.link(pool.affine_select(out=bm, in_=bm, compare_op=ALU.is_ge, fill=NEG, base=0,
                                       pattern=[[-NS, NB], [0, NS]], channel_multiplier=1))
            pool.affine_select(out=bm, in_=bm, compare_op=ALU.is_ge, fill=NEG, base=NS - 1,
                               pattern=[[NS, NB], [0, NS]], channel_multiplier=-1).then_inc(s_const, 1)
            for t in range(TP):
                dma(xt[:, t], xp[t]).then_inc(s_x, 16)
            dma(xt[:, TP], xs).then_inc(s_x, 16)
            dma(outs["new_conv_sample"].rearrange("l b k c -> (l b) k c")[:, 0:CTX - NS, :],
                ins["cache_conv"].rearrange("l b k c -> (l b) k c")[:, NS:CTX, :]).then_inc(s_cso, 16)
            pool.wait_ge(s_sq, 5)
            ccv = ins["cache_conv"].rearrange("l (h b) k c -> (l h) (b k) c", h=2)
            for h in range(2):
                dma(ccx[:, h], ccv[h]).then_inc(s_cc, 16)
            pool.wait_ge(s_setE, 2)
            pool.wait_ge(mod_done, NM1)
            dma(ext_d[:, :, :], ext.unsqueeze(1).to_broadcast([NH, P, EXT])).then_inc(s_ext, 16)
            pool.wait_ge(s_ext, 16)
            for b in range(NB):
                dma(biasN[NS * b:NS * b + NS], bass.AP(tensor=ext_d, offset=511,
                    ap=[[EXT - 1, NS], [P * EXT, NH], [1, NS]])).then_inc(s_bn, 16)
            for h in range(NH):
                dma(biasC_d[h].rearrange("(b s) n -> b s n", s=NS),
                    rows(ext_d, [[0, NB], [EXT - 1, NS]], P, h * P * EXT + 383)).then_inc(s_bc, 16)
            pool.wait_ge(mod_free, 4 + NM)
            dma(mod_d[:, 2 * D:], mrow2).then_inc(mod_saved, 16)
            for v in range(4 * T):
                j, t = divmod(v, T)
                pool.wait_ge(z_free, 2 + 32 + v + 1)
                dst = kvo["v", 0][t] if t < TP else kvo["v", 1]
                dma(dst[:, j * BW:(j + 1) * BW], vst[:, v % 4]).then_inc(s_vst[v % 4], 16)
            for i in range(7):
                pool.wait_ge(s_oE, i + 1)
                if i == 0:
                    dma(outs["new_conv_prompt"].rearrange("l o k c -> (l o k) c"), ost[0:CTX, 0]).then_inc(s_ost[0], 16)
                elif i == 1:
                    for b in range(NB):
                        dma(outs["new_conv_sample"].rearrange("l b k c -> (l b) k c")[b, CTX - NS:, :],
                            ost[NS * b:NS * b + NS, 1]).then_inc(s_ost[1], 16)
                else:
                    dma(kvo["k", 0][i - 2] if i < 6 else kvo["k", 1], ost[:, i % 4]).then_inc(s_ost[i % 4], 16)
            for i in range(4):
                pool.wait_ge(s_vst[i], 16 * T)
            pool.wait_ge(s_conv, 1)
            ch.link(pool.memset(qX, 0.0))
            pool.sem_inc(s_q0, 1)
            pool.wait_ge(s_bc, 16 * NH)

            def k_cache(hp):
                if hp >= 2:
                    pool.wait_ge(kct_T, hp - 1)
                dma(kC[:, hp % 2], kcache[:, :, hp * P:(hp + 1) * P]).then_inc(s_kc[hp % 2], 16)

            def values(hp):
                pb, cs = hp % 2, slice(hp * P, (hp + 1) * P)
                if hp >= 2:
                    pool.wait_ge(pv_done, 2 * (hp - 1))
                dma(vP[:, pb, 0:TP], kvo["v", 0].rearrange("t p n -> p t n")[:, :, cs]).then_inc(s_hp[pb], 16)
                dma(vP[:, pb, TP], kvo["v", 1][:, cs]).then_inc(s_hp[pb], 16)
                dma(vC[:, pb], vcache[:, :, cs]).then_inc(s_hp[pb], 16)

            k_cache(0)
            for h in range(NH):
                hp, b = divmod(h, 2)
                if h >= 2:
                    pool.wait_ge(sc_read, h - 1)
                dma(biasP[:, b], rows(ext_d, [[EXT - 1, P]], 512, h * P * EXT + 127)).then_inc(s_b[b], 16)
                dma(biasC[:, b], biasC_d[h]).then_inc(s_b[b], 16)
                if b == 0 and h + 2 < NH:
                    k_cache(hp + 1)
                if b == 1:
                    values(hp)
            pool.wait_ge(pv_done, NH)
            pool.wait_ge(p_ready, NH)
            for t in range(TP):
                dma(x1[:, t], xp[t]).then_inc(s_x5, 16)
            dma(x1[:, TP], xs).then_inc(s_x5, 16)

            def spread(dst, chunk, s):
                dma(dst(0), rows(mod_d, [[0, P]], D, chunk * D)).then_inc(s, 16)
                for b in range(NB):
                    dma(dst(1)[NS * b:NS * b + NS], rows(mod_d, [[0, NS]], D, (1 + b) * 6 * D + chunk * D)).then_inc(s, 16)

            pool.wait_ge(mod_saved, 16)
            spread(lambda b: g1b[:, b], 2, s_g1)
            pool.wait_ge(s_lnx, 1)
            spread(lambda b: A2[:, b], 4, s_m2)
            dma(n2g, rows(ins["norm2_g"].tensor, [[0, P]], D)).then_inc(s_n2, 16)
            pool.wait_ge(s_A2, 2)
            spread(lambda b: B2[:, b], 3, s_m2)
            for t in range(T):
                pool.wait_ge(o_free, 4 + 35 + t + 1)
                dma(x1_d[t], x1[:, t]).then_inc(s_x1t[t], 16)
            pool.wait_ge(s_h2E, 4 * T)
            pool.iota(iota_u, pattern=[[1, TOPK]], base=0, channel_multiplier=0).then_inc(s_iota, 1)
            pool.iota(token_u, pattern=[[P, 8]], base=0, channel_multiplier=1).then_inc(s_iota, 1)

            HALF = TOPK // 2

            def gather(dst, table, ix, g, s, signal):
                if s % HALF == 0:
                    ch.link(pool.tensor_copy(ix[:, s:s + HALF], idx_all[:, bass.ds(g * TOPK + s, HALF)]))
                pool.sem_inc(pool_passed, 1)
                pool.indirect_dma_start(dst, None, table,
                                        bass.IndirectOffsetOnAxis(ap=ix[:, s:s + 1], axis=0)).then_inc(signal, 16)

            dots_rows = bass.AP(tensor=dots_d, offset=0, ap=[[1, NEXP * ND], [1, 1]])

            def fetch_prepare(p, p0):
                if p0 == GG:
                    for b in range(2):
                        pool.wait_ge(sc_st[b], 16 * NCH // 2)
                else:
                    pool.wait_ge(dots_el, (p - GG) * (16 * TOPK))
                ch.link(pool.tensor_copy(ief, idx_all[:, bass.ds(p * TOPK, TOPK)]))
                pool.sem_inc(pool_passed, 1)
                tile = p0 // NPH - GT
                ch.link(pool.tensor_scalar(ie, ief, float(ND), token_f[:, tile:tile + 1], ALU.mult, ALU.add))
                pool.wait_ge(dh_rdy, p)
                pool.sem_inc(pool_passed, 1)

            def fetch(e):
                pool.indirect_dma_start(dots_in[:, e:e + 1], None, dots_rows,
                                        bass.IndirectOffsetOnAxis(ap=ie[:, e:e + 1], axis=0)).then_inc(dots_el, 16)

            def gathers(p, p0):
                if p0 < GG:
                    pool.wait_ge(idx_rdy, p + 1)
                for s in range(TOPK):
                    if p0 < GG:
                        if p0 >= 1 or s >= 4:
                            pool.wait_ge(dots_done, p * TOPK + (s - 3))
                        elif s == 0:
                            pool.wait_ge(o_done, 40)
                        gather(ux[:, s % 4], u_tab, iu, p, s, u_in[s % 4])
                    if 2 <= p0 < GG or p0 == GG and s < 4:
                        pool.wait_ge(v_used, (p - 2) * TOPK + (s + 1))
                    elif p0 >= GG:
                        if p0 == GG and s == 4:
                            pool.wait_ge(dots_done, GG * TOPK)
                        pool.wait_ge(v_used, (p - 2) * TOPK + (s - 3))
                    if p0 >= 2:
                        dst, signal, _ = v_slot(p - 2, p0, s)
                        gather(dst, v_tab, iv, p - 2, s, signal)
                    if p0 == GG and s == TOPK - 1:
                        fetch_prepare(p, p0)
                        for e in range(TOPK):
                            fetch(e)
                    if GG < p0 < NG and s >= FETCH:
                        if s == FETCH:
                            fetch_prepare(p, p0)
                        for e in fetches[s - FETCH]:
                            fetch(e)

            FETCH = 4
            fetches = [(0,), (1,), (2,), (3,), (4, 5), (6, 7), (8, 9), (10, 11), (12,), (13,), (14,), (15,)]
            assert FETCH + len(fetches) == TOPK and sum(len(f) for f in fetches) == TOPK
            periods(pool, ch, 4, gathers)
            pool.wait_ge(s_cso, 16)
            pool.wait_ge(s_ost[0], 16 * 2)
            pool.wait_ge(s_ost[1], 16 * (NB + 1))
            pool.wait_ge(s_ost[2], 16 * 2)
            pool.wait_ge(s_ost[3], 16)

        @block.tensor
        def _(pe):
            def tr(out, in_, k):
                return pe.transpose(out, in_, ident[0:k, 0:k])

            pe.wait_ge(s_const, 1)
            pe.wait_ge(s_small, 16 * 9)
            tr(PB[4][:, 0:40], prm, 40).then_inc(s_setT, 1)
            for c in range(CT):
                t = tr(PB[5][:, 32 * c:32 * c + WID], wdw[:, c * P:(c + 1) * P], WID)
            t.then_inc(s_setT, 1)
            for h in range(2):
                t = tr(PB[6][:, h * P:(h + 1) * P], skn[:, h], P)
            t.then_inc(s_setT, 1)
            pe.wait_ge(s_silu, 1)
            for k in range(KT):
                t = tr(PB[7][:, 9 * k:9 * k + 9], cnd[:, k * P:(k + 1) * P], NCND)
            t.then_inc(s_setT, 1)
            pe.wait_ge(s_setE, 6)
            def modulate(n, b, slot):
                pe.wait_ge(mod_free, n + 1)
                for k in range(KT):
                    g = k % 4
                    m = pe.matmul(PB[4 + b][32 * g:32 * g + NCND, 0:BW], cT[:, k, :],
                                  ring[:, slot, k, :], start=(k < 4), stop=(k >= KT - 4))
                m.then_inc(mod_done, 1)

            with pe.Fori(0, NM1 // 4) as it:
                for j in range(NRING):
                    pe.wait_ge(w_in_s[j], it * 16 + 16)
                    modulate(it * 4 + j, j, j)
            pe.wait_ge(mod_free, 4 + NM1)
            for k in range(2 * KT):
                t = tr(PB[4][:, 16 * k:16 * k + 9], mrow[:, k * P:(k + 1) * P], NCND)
            t.then_inc(s_modT, 1)
            pe.wait_ge(s_xn, T)
            for g in range(KT + 4):
                if g >= 4:
                    pe.wait_ge(xT_act, g - 3)
                for i in range(4):
                    src = xt[:, i, g * P:(g + 1) * P] if g < KT else xt[:, TP, (4 * (g - KT) + i) * P:][:, 0:P]
                    t = tr(PB[g % 4][:, i * P:(i + 1) * P], src, P)
                t.then_inc(xT_done, 1)
            pe.wait_ge(s_cc, 32)
            pe.wait_ge(s_A1, 1)
            for c2 in range(4):
                for i in range(4):
                    c, h = 2 * c2 + i // 2, i % 2
                    t = tr(PB[4 + c2][:, i * 120:(i + 1) * 120], ccx[:, h, c * P:(c + 1) * P], 120)
                t.then_inc(cc_T, 1)

            pe.wait_ge(xT_act, KT)
            pe.wait_ge(xT_dve, 4)

            def project(srcs, weights, par, signal):
                for k in range(KT):
                    w = weights[:, k]
                    for i, src in enumerate(srcs):
                        m = pe.matmul(PB[2 * par + i][:, 0:src.shape[-1]], w, src[:, k],
                                      start=(k == 0), stop=(k == KT - 1))
                m.then_inc(signal, 1)

            pe.wait_ge(cc_E, 4)
            with pe.Fori(0, 4) as i:
                for b in range(2):
                    pe.wait_ge(w_in_s[b], i * 16 + 16 * 5)
                    for c in range(2):
                        pe.wait_ge(z_free, i * 4 + (2 * b + c + 1))
                        project((hT[:, :, 0:NP], hT[:, :, NP:NT]), ring[:, b, :, c * P:(c + 1) * P], c, z_done)
                        for a in range(2 * c, 2 * c + 2):
                            pe.wait_ge(w_in_s[2 + a % 2], i * 64 + 16 * (5 + 2 * b + a // 2))
                            modulate(i * 8 + (NM1 + 4 * b + a), a, 2 + a % 2)
            with pe.Fori(2, 4) as kd:
                for j in range(NRING):
                    pe.wait_ge(w_in_s[j], kd * 16 + (16 * 13 + ring_adj[j]))
                    for c in range(2):
                        pe.wait_ge(z_free, kd * 8 + (2 * j + c + 1))
                        project((hT[:, :, 0:NP], hT[:, :, NP:NT]), ring[:, j, :, c * P:(c + 1) * P], c, z_done)
            for v in range(4 * T):
                j, t = divmod(v, T)
                if t == 0:
                    pe.wait_ge(w_in_s[j], 16 * 17 + ring_adj[j])
                pe.wait_ge(z_free, 32 + v + 1)
                for k in range(KT):
                    m = pe.matmul(PB[2 * (v % 2)][:, 0:BW], hT[:, k, t * P:(t + 1) * P], ring[:, j, k, :],
                                  start=(k == 0), stop=(k == KT - 1))
                m.then_inc(z_done, 1)
            pe.wait_ge(s_u, 8)
            pe.wait_ge(cc_E, 4)
            for i in range(7):
                if i >= 2:
                    pe.wait_ge(s_oE, i - 1)
                if i == 1:
                    pe.wait_ge(s_uc, 1)
                for c in range(CT):
                    src = (uP[:, c, NP:NP + CTX] if i == 0 else uC[:, c] if i == 1
                           else kT[:, c, (i - 2) * P:(i - 1) * P])
                    n = CTX if i == 0 else P
                    t = pe.transpose(PB[4 + 2 * (i % 2) + c // 4][0:n, (c % 4) * P:(c % 4 + 1) * P], src, ident)
                t.then_inc(s_oT, 1)

            def pair_keys(hp):
                b = hp % 2
                pe.wait_ge(s_kc[b], 16 * (hp // 2 + 1))
                if hp == 0:
                    pe.wait_ge(s_oE, 7)
                else:
                    pe.wait_ge(kct_E, hp)
                    if hp >= 2:
                        pe.wait_ge(pt_read, 2 * hp - 2)
                for s in range(NB):
                    t = tr(PB[3 + s // 4][:, (s % 4) * P:(s % 4 + 1) * P], kC[:, b, s], P)
                t.then_inc(kct_T, 1)

            def scores(h):
                hp, b = divmod(h, 2)
                r = slice(DH * b, DH * b + DH)
                q, k = cat[r, CT + hp], kT[r, hp]
                if h >= 1:
                    pe.wait_ge(sc_read, h)
                else:
                    pe.wait_ge(z_free, 2 + 52)
                pe.matmul(PB[0][:, 0:512], q[:, 384:512], k[:, 0:512], start=True, stop=True)
                pe.matmul(PB[1][:, 0:384], q[:, 256:384], k[:, 0:384], start=True, stop=True)
                pe.matmul(PB[1][:, 384:512], q[:, 0:128], k[:, 0:128], start=True, stop=True)
                pe.matmul(PB[2][:, 0:256], q[:, 128:256], k[:, 0:256], start=True, stop=True)
                pe.matmul(PB[2][:, 384:512], q[:, NP:NT], k[:, NP:NT], start=True, stop=True)
                pe.wait_ge(s_qx, hp + 1)
                pe.wait_ge(kct_E, hp + 1)
                for s in range(NB):
                    m = pe.matmul(PB[2][:, 256:384], qX[r, s], kCT[r, hp % 2, s], start=(s == 0), stop=(s == NB - 1))
                m.then_inc(sc_ready, 1)

            def turn_weights(h):
                b = h % 2
                pe.wait_ge(p_ready, h + 1)
                if h >= 1:
                    pe.wait_ge(pt_read, h)
                pe.wait_ge(kct_E, min(h // 2 + 2, NH // 2))
                for i in range(4):
                    tr(PB[3][:, i * P:(i + 1) * P], sP[:, b, i, 384 - P * i:512 - P * i], P)
                for i in range(1, 4):
                    tr(PB[4][:, (i - 1) * P:i * P], sP[:, b, i, 512 - P * i:640 - P * i], P)
                tr(PB[4][:, 384:512], sP[:, b, 3, 384:512], P)
                for i in range(2, 4):
                    tr(PB[5][:, (i - 2) * P:(i - 1) * P], sP[:, b, i, 640 - P * i:768 - P * i], P)
                tr(PB[5][:, 256:384], sS[:, b, 0:P], P)
                tr(PB[5][:, 384:512], sS[:, b, P:2 * P], P).then_inc(pt_ready, 1)

            def weigh(h):
                hp, b = divmod(h, 2)
                pb = hp % 2
                r, vc = slice(DH * b, DH * b + DH), slice(DH * b, DH * b + DH)
                pe.wait_ge(s_hp[pb], 48 * (hp // 2 + 1))
                pe.wait_ge(pt_read, h + 1)
                if h >= 1:
                    pe.wait_ge(pv_read, h)
                o, os = PB[6][r], PB[7][r]
                pe.matmul(o[:, 0:512], vP[:, pb, 0, vc], pT[:, 0:512], start=True, stop=False)
                pe.matmul(o[:, 128:512], vP[:, pb, 1, vc], pT[:, 512:896], start=False, stop=False)
                pe.matmul(o[:, 256:512], vP[:, pb, 2, vc], pT[:, 1024:1280], start=False, stop=False)
                pe.matmul(o[:, 384:512], vP[:, pb, 3, vc], pT[:, 896:1024], start=False, stop=True)
                pe.matmul(os[:, 0:P], vP[:, pb, 4, vc], pT[:, 1408:1536], start=True, stop=False)
                for s in range(NB):
                    m = pe.matmul(os[:, NS * s:NS * s + NS], vC[:, pb, s, vc],
                                  pT[:, 1280 + NS * s:1280 + NS * s + NS], start=False, stop=(s == NB - 1))
                m.then_inc(pv_done, 1)

            pair_keys(0)
            for h in range(NH + 2):
                if h < NH:
                    scores(h)
                    if h % 2 == 1 and h + 1 < NH:
                        pair_keys((h + 1) // 2)
                if h >= 2:
                    weigh(h - 2)
                if 1 <= h <= NH:
                    turn_weights(h - 1)

            def channel_sum(banks, src, wait, used):
                for c in range(CT):
                    if wait is not None:
                        pe.wait_ge(wait, c + 1)
                    pe.matmul(PB[banks][:, 0:NP], mean_w, src(c)[:, 0:NP], start=(c == 0), stop=(c == CT - 1))
                    m = pe.matmul(PB[banks + 1][:, 0:P], mean_w, src(c)[:, NP:NT], start=(c == 0), stop=(c == CT - 1))
                    if used is not None:
                        m.then_inc(used, 1)
                return m

            pe.wait_ge(s_const, 2)
            pe.wait_ge(s_conv, 1)
            pe.wait_ge(sc_read, NH)
            channel_sum(0, lambda c: cat[:, c], None, None).then_inc(s_mean, 1)
            pe.wait_ge(pt_read, NH)
            channel_sum(2, lambda c: q2s[:, c % 2], s_ysq, s_ysq_used)

            pe.wait_ge(s_cat, CT)
            pe.wait_ge(pv_read, NH)
            pe.wait_ge(s_lnv, 1)
            with pe.Fori(0, 2) as it:
                for v in range(4 * T):
                    j, t = divmod(v, T)
                    if t == 0:
                        pe.wait_ge(w_in_s[j], it * 16 + (16 * 18 + ring_adj[j]))
                    pe.wait_ge(o_free, it * 20 + (v + 1))
                    for k in range(KT):
                        m = pe.matmul(PB[v % 4][:, 0:BW], cat[:, k, t * P:(t + 1) * P], ring[:, j, k, :],
                                      start=(k == 0), stop=(k == KT - 1))
                    m.then_inc(o_done, 1)
            pe.wait_ge(o_free, 4 + 40)
            for t in range(T):
                pe.wait_ge(s_h2, t + 1)
                if t == 1:
                    pe.wait_ge(s_sq, 2 * T)
                if t >= 2:
                    pe.wait_ge(s_h2E, 4 * (t - 1))
                for q in range(4):
                    for i in range(4):
                        k = 4 * q + i
                        m = tr(PB[4 * (t % 2) + q][:, i * P:(i + 1) * P], x1[:, t, k * P:(k + 1) * P], P)
                    m.then_inc(s_h2T, 1)

            def key_scores(n):
                b = n % 2
                pe.wait_ge(q_read, n + 1)
                if n >= 2:
                    pe.wait_ge(s_se, n - 1)
                for t in range(TP):
                    pe.matmul(PB[4 + 2 * b][:, t * P:(t + 1) * P], q2s[:, b, t * P:(t + 1) * P], skT[:, n % 2],
                              start=True, stop=True)
                pe.matmul(PB[5 + 2 * b][:, 0:P], q2s[:, b, NP:NT], skT[:, n % 2], start=True, stop=True).then_inc(s_s, 1)

            pe.wait_ge(s_h2E, 4 * T)
            for n in range(16):
                pe.wait_ge(w_q[n % 3], 16 * (n // 3 + 1))
                if n >= 2:
                    pe.wait_ge(q_read, n - 1)
                project((h2A, h2B), wq[n % 3], n % 2, q_done)
                if n >= 1:
                    if n != 2:
                        key_scores(n - 1)
                    if n == 1:
                        key_scores(1)
            key_scores(15)

            def turn(b, q):
                for i in range(4):
                    m = tr(PB[q % 2][:, i * P:(i + 1) * P], uchunk[b][:, q, i * P:(i + 1) * P], P)
                m.then_inc(tr_done, 1)

            pe.wait_ge(q_read, 16)
            pe.sem_inc(sc_out, 2)
            for q in range(4):
                pe.wait_ge(ch_in[0][q], 16)
                if q >= 2:
                    pe.wait_ge(uT_rdy, q - 1)
                turn(0, q)

            def products(n, b, more):
                pe.wait_ge(sc_out, n + 1)
                for q in range(4):
                    pe.wait_ge(uT_rdy, n * 4 + (q + 1))
                    for k in range(4 * q, 4 * q + 4):
                        m = pe.matmul(PB[2 + b][:, 0:ND], uT[:, k], h2B[:, k], start=(k == 0), stop=(k == KT - 1))
                    if q == 3:
                        m.then_inc(mm_done, 1)
                    if more:
                        pe.wait_ge(ch_in[1 - b][q], (n - b) * 8 + 16 + 16 * b)
                        pe.wait_ge(uT_rdy, n * 4 + (q + 3))
                        turn(1 - b, q)

            with pe.Fori(0, NCH // 2 - 1) as i:
                for b in range(2):
                    products(i * 2 + b, b, True)
            products(NCH - 2, 0, True)
            products(NCH - 1, 1, False)

        @block.scalar
        def _(act):
            A = nc.scalar.activation
            act.wait_ge(s_small, 16 * 9)
            A(cnd, cnd, ACT.Silu).then_inc(s_silu, 1)
            act.wait_ge(s_x, 16 * T)
            for t in range(T):
                if t >= 1:
                    act.wait_ge(s_sq, t)
                A(junk1, xt[:, t], ACT.Square, accum_out=ssq[:, t:t + 1]).then_inc(s_sq, 1)
            act.wait_ge(s_v1, 1)
            A(rs, tmpa, ACT.Sqrt).then_inc(s_r1, 1)
            act.wait_ge(s_A1, 1)
            act.wait_ge(s_setE, 6)
            for k in range(KT):
                act.wait_ge(xT_done, k + 1)
                A(hT[:, k, 0:NP], PB[k % 4][:, :], ACT.Identity, scale=A1T[:, k, 0:1],
                  bias=modT[:, k, 0:1]).then_inc(xT_act, 1)
            act.sem_inc(z_free, 2)
            for n in range(32):
                kind, c = divmod(n, 8)
                pa, pb = PB[2 * (n % 2)][:, 0:NP], PB[2 * (n % 2) + 1][:, 0:P]
                act.wait_ge(z_done, n + 1)
                if kind == 0:
                    A(uP[:, c, CTX:], pa, ACT.Copy)
                    A(uS[:, c, :, CTX:], pb.rearrange("p (b s) -> p b s", s=NS), ACT.Copy).then_inc(z_free, 1)
                elif kind == 1:
                    if c >= 2:
                        act.wait_ge(s_u, c - 1)
                    A(sig[:, c % 2, 0:NP], pa, ACT.Sigmoid)
                    A(sig[:, c % 2, NP:NT], pb, ACT.Sigmoid).then_inc(z_free, 1)
                else:
                    dst = cat[:, CT + c] if kind == 2 else kT[:, c]
                    if n == 16:
                        act.wait_ge(mod_saved, 16)
                        act.wait_ge(s_ext, 16)
                        act.wait_ge(cc_E, 4)
                    A(dst[:, 0:NP], pa, ACT.Copy)
                    A(dst[:, NP:NT], pb, ACT.Copy).then_inc(z_free, 1)
            act.wait_ge(s_u, 8)
            for v in range(4 * T):
                act.wait_ge(z_done, 32 + v + 1)
                if v >= 4:
                    act.wait_ge(s_vst[v % 4], 16 * (v // 4))
                A(vst[:, v % 4], PB[2 * (v % 2)][:, 0:BW], ACT.Copy).then_inc(z_free, 1)
            for c in range(CT):
                m = A(uC[:, c].rearrange("p (b s) -> p b s", s=NS), uS[:, c, :, CTX:], ACT.Copy)
            m.then_inc(s_uc, 1)
            for i in range(7):
                n = CTX if i == 0 else P
                act.wait_ge(s_oT, i + 1)
                if i >= 4:
                    act.wait_ge(s_ost[i % 4], 16 * NB if i % 4 == 1 else 16)
                A(ost[0:n, i % 4, 0:512], PB[4 + 2 * (i % 2)][0:n, :], ACT.Copy)
                A(ost[0:n, i % 4, 512:1024], PB[5 + 2 * (i % 2)][0:n, :], ACT.Copy).then_inc(s_oE, 1)

            def copy_pT(h):
                act.wait_ge(pt_ready, h + 1)
                if h >= 1:
                    act.wait_ge(pv_done, h)
                for i in range(3):
                    m = A(pT[:, i * 512:(i + 1) * 512], PB[3 + i][:, :], ACT.Copy)
                m.then_inc(pt_read, 1)

            for h in range(-1, NH + 1):
                if h % 2 == 1 and h + 1 < NH:
                    hp = (h + 1) // 2
                    act.wait_ge(kct_T, hp + 1)
                    if hp >= 2:
                        act.wait_ge(sc_ready, 2 * (hp - 1))
                    if hp == 0:
                        act.wait_ge(s_conv, 1)
                    A(kCT[:, hp % 2, 0:4, :], PB[3][:, :].rearrange("p (s n) -> p s n", s=4), ACT.Copy)
                    A(kCT[:, hp % 2, 4:8, :], PB[4][:, :].rearrange("p (s n) -> p s n", s=4), ACT.Copy).then_inc(kct_E, 1)
                if 0 <= h < NH:
                    b = h % 2
                    act.wait_ge(mx_ready, h + 1)
                    for i in range(4):
                        s = sP[:, b, i, 384 - P * i:512]
                        A(s, s, ACT.Exp, bias=nmax[:, b, i:i + 1], accum_out=esum[:, b, i:i + 1])
                    A(sS[:, b], sS[:, b], ACT.Exp, bias=nmax[:, b, 4:5], accum_out=esum[:, b, 4:5]).then_inc(ex_ready, 1)
                if h >= 1:
                    copy_pT(h - 1)

            for c in range(CT):
                act.wait_ge(s_xc, c + 1)
                if c >= 2:
                    act.wait_ge(s_ysq_used, c - 1)
                A(q2s[:, c % 2], cat[:, c], ACT.Square).then_inc(s_ysq, 1)
            act.wait_ge(s_lnv, 1)
            A(q2s[:, 1], q2s[:, 0], ACT.Sqrt).then_inc(s_lnr, 1)
            for c in range(CT):
                act.wait_ge(s_lnx, c + 1)
                A(cat[:, c], cat[:, c], ACT.Silu, scale=prmT[:, 24 + c:25 + c], bias=prmT[:, 32 + c:33 + c]).then_inc(s_cat, 1)
            for t in range(T):
                act.wait_ge(o_free, 4 + 35 + t + 1)
                for c in range(4):
                    if t >= 1:
                        act.wait_ge(s_sq, T + t)
                    m = A(PB[4 + c][:, :], x1[:, t, c * 512:(c + 1) * 512], ACT.Square, accum_out=part[:, t, c:c + 1])
                m.then_inc(s_sq, 1)
                act.wait_ge(s_v1, t + 2)
                A(rs[:, t:t + 1], tmpa[:, t:t + 1], ACT.Sqrt).then_inc(s_r1, 1)
            for t in range(T):
                for q in range(4):
                    act.wait_ge(s_h2T, 4 * t + q + 1)
                    dst = h2A[:, :, t * P:(t + 1) * P] if t < GT else h2B[:, :, (t - GT) * P:(t - GT + 1) * P]
                    A(dst[:, 4 * q:4 * q + 4],
                      PB[4 * (t % 2) + q][:, :].rearrange("p (k n) -> p k n", k=4), ACT.Copy).then_inc(s_h2E, 1)
            def gate_exp(g):
                act.wait_ge(sub_rdy, g + 1)
                A(tex, tsub, ACT.Exp, accum_out=tsum[:, 0:1]).then_inc(exp_rdy, 1)

            def gelu(g):
                act.wait_ge(dh_rdy, g + 1)
                A(gel, dhold, ACT.Gelu_apprx_tanh).then_inc(gel_rdy, 1)

            early = {1: [("exp", 0)], 4: [("exp", 1)], 6: [("gelu", 0)], 7: [("exp", 2)], 8: [("gelu", 1)],
                     10: [("exp", 3)], 13: [("exp", 4)], 14: [("gelu", 2)]}
            for n in range(16):
                act.wait_ge(q_done, n + 1)
                if n >= 2:
                    act.wait_ge(s_s, n - 1)
                A(q2s[:, n % 2, 0:GT * P], PB[2 * (n % 2)][:, 0:GT * P], ACT.Copy)
                A(q2s[:, n % 2, GT * P:NT], PB[2 * (n % 2) + 1][:, 0:ND], ACT.Copy).then_inc(q_read, 1)
                for what, i in early.get(n, ()):
                    gate_exp(i) if what == "exp" else gelu(i)
            def uT_copy(n):
                for q in range(4):
                    act.wait_ge(tr_done, n * 4 + (q + 1))
                    A(uT[:, 4 * q:4 * q + 4], PB[q % 2][:, :].rearrange("p (k n) -> p k n", k=4),
                      ACT.Copy).then_inc(uT_rdy, 1)

            def dense_step(n, b, last):
                if not last:
                    uT_copy(n + 1)
                act.wait_ge(mm_done, n + 1)
                act.wait_ge(sc_st[b], (n - b) * 8)
                A(dstage[:, b], PB[2 + b][:, 0:ND], ACT.Copy).then_inc(sc_out, 1)

            def scalar_part(p, p0):
                def steps(c0, c1):
                    if EARLY <= p0 < GG:
                        for c in range(c0, c1):
                            dense_step((p - EARLY) * CPP + (CP0 + c), c % 2, p0 == GG - 1 and c == CPP - 1)

                if p0 < EARLY:
                    return
                steps(0, CPP // 2)
                if p0 < NG - 1:
                    gate_exp(p + 1)
                if p0 <= NG:
                    gelu(p - 1)
                if p0 == NPH + 1:
                    act.wait_ge(dots_done, NPH * TOPK)
                    act.dma_start(fgb, rows(ins["final_g"].tensor, [[0, P]], D)).then_inc(s_fg, 16)
                if p0 >= NPH + 2 and (p0 - 2) % NPH == 0:
                    tile_sqrt((p0 - 2) // NPH - 1)
                steps(CPP // 2, CPP)

            def tile_sqrt(t):
                act.wait_ge(f_v, t + 1)
                A(fin[:, 2:3], fin[:, 1:2], ACT.Sqrt).then_inc(f_r, 1)

            act.wait_ge(s_s, 16)
            uT_copy(0)
            with act.Fori(0, CP0 // 2) as i:
                for b in range(2):
                    dense_step(i * 2 + b, b, False)
            periods(act, None, 0, scalar_part)
            tile_sqrt(T - 1)

        @block.vector
        def _(dve):
            ch = Chain(dve, s_dve)
            V = nc.vector
            STT, TT, TS, CP = V.scalar_tensor_tensor, V.tensor_tensor, V.tensor_scalar, V.tensor_copy

            def refine(r, v, t):
                ch.link(TT(t, r, r, ALU.mult))
                ch.link(TT(t, t, v, ALU.mult))
                ch.link(TS(t, t, -0.5, 1.5, ALU.mult, ALU.add))
                return TT(r, r, t, ALU.mult)

            dve.sem_inc(mod_free, 4)
            dve.sem_inc(o_free, 4)
            dve.wait_ge(s_small, 16 * 9)
            CP(ext[:, 0:255], ext[:, 255:256].to_broadcast([NH, 255])).then_inc(s_setE, 1)
            V.memset(ext[:, EXT - 1:EXT], 0.0).then_inc(s_setE, 1)
            dve.wait_ge(s_setT, 3)
            CP(prmT[:, 0:40], PB[4][:, 0:40]).then_inc(s_setE, 1)
            CP(wdT[:, :, 0:WID], PB[5][:, 0:256].rearrange("p (c k) -> p c k", k=32)[:, :, 0:WID]).then_inc(s_setE, 1)
            CP(skT, PB[6][:, 0:256].rearrange("p (h n) -> p h n", h=2)).then_inc(s_setE, 1)
            dve.wait_ge(s_setT, 4)
            CP(cT, PB[7][:, 0:9 * KT].rearrange("p (k c) -> p k c", c=9)).then_inc(s_setE, 1)
            dve.wait_ge(s_setE, 6)
            dve.wait_ge(s_bada, 32)

            def modulated(n, m, b):
                dve.wait_ge(mod_done, n + 1)
                for g in range(4):
                    t = TT(m, PB[4 + b][32 * g:32 * g + NCND, 0:BW], m, ALU.add)
                    if g < 3:
                        ch.link(t)
                t.then_inc(mod_free, 1)

            def first_blocks(it):
                for j in range(4):
                    modulated(it * 4 + j, mrow[:, bass.ds(it * (4 * BW) + j * BW, BW)], j)

            loop(dve, ch, 0, 2, 12, first_blocks)
            dve.wait_ge(s_sq, T)
            ch.link(TS(tmpa, ssq, 1.0 / D, EPS, ALU.mult, ALU.add))
            dve.sem_inc(s_v1, 1)
            dve.wait_ge(s_r1, 1)
            ch.link(V.reciprocal(rs, rs))
            ch.link(refine(rs, tmpa, ssq))
            for t in range(T):
                TS(xt[:, t], xt[:, t], rs[:, t:t + 1], None, ALU.mult).then_inc(s_xn, 1)
            loop(dve, ch, 2, NM1 // 4, 12, first_blocks)
            dve.wait_ge(s_modT, 1)
            ch.link(CP(modT[:, :, 0:9], PB[4][:, :].rearrange("p (k c) -> p k c", c=16)[:, :, 0:9]))
            STT(out=A1T[:, :, 0:9], in0=modT[:, KT:, 0:9], scalar=1.0,
                in1=prmT[:, 0:KT].unsqueeze(2).to_broadcast([P, KT, 9]), op0=ALU.add, op1=ALU.mult).then_inc(s_A1, 1)
            dve.wait_ge(s_A1, 1)
            for g in range(4):
                dve.wait_ge(xT_done, KT + g + 1)
                for i in range(4):
                    k = 4 * g + i
                    o = hT[:, k, NP:NT].rearrange("p (b s) -> p b s", s=NS)
                    src = PB[(KT + g) % 4][:, i * P:(i + 1) * P].rearrange("p (b s) -> p b s", s=NS)
                    ch.mark(TT(o, src, A1T[:, k, 1:9].unsqueeze(2).to_broadcast([P, NB, NS]), ALU.mult))
                ch.sync()
                for i in range(4):
                    k = 4 * g + i
                    o = hT[:, k, NP:NT].rearrange("p (b s) -> p b s", s=NS)
                    m = TT(o, o, modT[:, k, 1:9].unsqueeze(2).to_broadcast([P, NB, NS]), ALU.add)
                m.then_inc(xT_dve, 1)
            V.memset(uP[:, :, 0:CTX], 0.0)
            for c2 in range(4):
                dve.wait_ge(cc_T, c2 + 1)
                CP(uS[:, 2 * c2:2 * c2 + 2, :, 0:CTX].rearrange("p c b k -> p (c b) k"),
                   PB[4 + c2][:, 0:480].rearrange("p (a k) -> p a k", k=CTX)).then_inc(cc_E, 1)
            loop(dve, ch, 0, 4, 12, lambda w: [
                modulated(w * 4 + (NM1 + a), mrow2[:, bass.ds(w * (4 * BW) + a * BW, BW)], a) for a in range(4)])
            for c in range(CT):
                dve.wait_ge(z_free, 2 + 8 + c + 1)
                TT(uP[:, c, CTX:], uP[:, c, CTX:], sig[:, c % 2, 0:NP], ALU.mult)
                TT(uS[:, c, :, CTX:], uS[:, c, :, CTX:], sig[:, c % 2, NP:NT].rearrange("p (b s) -> p b s", s=NS),
                   ALU.mult).then_inc(s_u, 1)
                for a in range(16 + 2 * c, 18 + 2 * c):
                    modulated(NM1 + a, mrow2[:, a * BW:(a + 1) * BW], a % 4)
            dve.wait_ge(mod_saved, 16)
            dve.wait_ge(s_u, CT)
            dve.wait_ge(cc_E, 4)
            uSf = uS.rearrange("p c b n -> p (c b) n")
            catf = r12(R2, CT * NT)
            wdf = wdT.rearrange("p c k -> p (c k)")

            def conv(c):
                oP = catf[:, bass.ds(c * NT, NP)]
                oS = catf[:, bass.ds(c * NT + NP, P)].rearrange("p (b s) -> p b s", s=NS)
                uPf = R3[:, 0:CT * UPW]
                uSr = R3[:, CT * UPW:UEND]
                for k in range(WID):
                    w = wdf[:, bass.ds(c * 32 + k, 1)]
                    iP = uPf[:, bass.ds(c * UPW + k, NP)]
                    iS = uSr[:, bass.ds(c * (NB * USW), NB * USW)].rearrange("p (b n) -> p b n", b=NB)[:, :, k:k + NS]
                    if k == 0:
                        ch.mark(TS(oP, iP, w, prmT[:, bass.ds(c + 16, 1)], ALU.mult, ALU.add))
                        ch.mark(TS(oS, iS, w, prmT[:, bass.ds(c + 16, 1)], ALU.mult, ALU.add))
                    else:
                        ch.n -= 1
                        ch.sync()
                        ch.n += 1
                        ch.mark(STT(out=oP, in0=iP, scalar=w, in1=oP, op0=ALU.mult, op1=ALU.add))
                        ch.n -= 1
                        ch.sync()
                        ch.n += 1
                        ch.mark(STT(out=oS, in0=iS, scalar=w, in1=oS, op0=ALU.mult, op1=ALU.add))

            loop(dve, ch, 0, CT, 2 * WID, conv)
            ch.sync()
            dve.sem_inc(s_conv, 1)

            def head_max(h):
                b = h % 2
                dve.wait_ge(s_b[b], 16 * 2 * (h // 2 + 1))
                dve.wait_ge(sc_ready, h + 1)
                if h >= 2:
                    dve.wait_ge(pt_ready, h - 1)
                src = [PB[1][:, 384:512], PB[2][:, 0:256], PB[1][:, 0:384], PB[0][:, :]]
                for i in range(4):
                    ch.mark(STT(out=sP[:, b, i, 384 - P * i:512], in0=src[i], scalar=DH ** -0.5,
                                in1=biasP[:, b, 384 - P * i:512], op0=ALU.mult, op1=ALU.add))
                STT(out=sS[:, b, 0:P], in0=PB[2][:, 256:384], scalar=DH ** -0.5, in1=biasC[:, b],
                    op0=ALU.mult, op1=ALU.add)
                STT(out=sS[:, b, P:2 * P], in0=PB[2][:, 384:512], scalar=DH ** -0.5, in1=blockmask,
                    op0=ALU.mult, op1=ALU.add).then_inc(sc_read, 1)
                ch.sync()
                dve.wait_ge(sc_read, h + 1)
                ch.mark(V.memset(sP[0:DH, b, :, 448:512], NEG))
                n = sS[:, b, P:2 * P].rearrange("p (c s) -> p c s", s=NS)
                ch.mark(TT(n, n, biasN[:, h].unsqueeze(1).to_broadcast([P, NB, NS]), ALU.add))
                ch.sync()
                for i in range(4):
                    V.tensor_reduce(nmax[:, b, i:i + 1], sP[:, b, i, 384 - P * i:512], AX.X, ALU.max, negate=True)
                V.tensor_reduce(nmax[:, b, 4:5], sS[:, b], AX.X, ALU.max, negate=True).then_inc(mx_ready, 1)

            def head_out(h):
                hp, b = divmod(h, 2)
                r = slice(DH * b, DH * b + DH)
                dve.wait_ge(pv_done, h + 1)
                CP(cat[r, CT + hp, 0:NP], PB[6][r, :])
                CP(cat[r, CT + hp, NP:NT], PB[7][r, 0:P]).then_inc(pv_read, 1)

            def head_norm(h):
                b = h % 2
                dve.wait_ge(ex_ready, h + 1)
                ch.link(V.reciprocal(esum[:, b], esum[:, b]))
                for i in range(4):
                    s = sP[:, b, i, 384 - P * i:512]
                    TS(s, s, esum[:, b, i:i + 1], None, ALU.mult)
                TS(sS[:, b], sS[:, b], esum[:, b, 4:5], None, ALU.mult).then_inc(p_ready, 1)

            def pair_queries(hp):
                CP(qXd, cat[:, CT + hp, NP:NT].rearrange("p (b s) -> p b s", s=NS)).then_inc(s_qx, 1)

            dve.wait_ge(s_bn, 16 * NB)
            dve.wait_ge(s_const, 3)
            dve.wait_ge(s_q0, 1)
            for i in range(4):
                dve.wait_ge(s_ost[i], 16 * (9 if i == 1 else 1 if i == 3 else 2))
            pair_queries(0)
            for h in range(NH + 2):
                if h < NH:
                    head_max(h)
                    if h % 2 == 1 and h + 1 < NH:
                        pair_queries((h + 1) // 2)
                    head_norm(h)
                if h >= 2:
                    head_out(h - 2)

            dve.wait_ge(s_mean, 1)
            for c in range(CT):
                TT(cat[:, c, 0:NP], cat[:, c, 0:NP], PB[0][:, :], ALU.subtract)
                TT(cat[:, c, NP:NT], cat[:, c, NP:NT], PB[1][:, 0:P], ALU.subtract).then_inc(s_xc, 1)
            dve.wait_ge(s_ysq_used, CT)
            v, r, t = q2s[:, 0], q2s[:, 1], R3[:, 0:NT]
            dve.wait_ge(pv_done, NH)
            ch.mark(TS(v[:, 0:NP], PB[2][:, :], EPS, None, ALU.add))
            ch.link(TS(v[:, NP:NT], PB[3][:, 0:P], EPS, None, ALU.add))
            dve.sem_inc(s_lnv, 1)
            dve.wait_ge(s_lnr, 1)
            ch.link(V.reciprocal(r, r))
            ch.link(refine(r, v, t))
            for c in range(CT):
                TT(cat[:, c], cat[:, c], r, ALU.mult).then_inc(s_lnx, 1)

            dve.wait_ge(s_x5, 16 * T)
            dve.wait_ge(s_g1, 16 * (1 + NB))
            dve.wait_ge(s_lnx, CT)
            x1f = r12(0, T * D)
            g1f = R3[:, 8192:12288]

            def residual(it, v0, v1):
                for v in range(v0, v1):
                    j, t = divmod(v, T)
                    dve.wait_ge(o_done, it * 20 + (v + 1))
                    g = g1f[:, bass.ds(it * 1024 + ((0 if t < TP else D) + j * BW), BW)]
                    xx = x1f[:, bass.ds(it * 1024 + (t * D + j * BW), BW)]
                    ch.link(TT(otmp[:, v % 2], PB[v % 4][:, 0:BW], g, ALU.mult))
                    TT(xx, xx, otmp[:, v % 2], ALU.add).then_inc(o_free, 1)

            def norm_tile(t):
                b = 0 if t < TP else 1
                r, v, q = rs[:, t:t + 1], tmpa[:, t:t + 1], ssq[:, t:t + 1]
                dve.wait_ge(s_sq, T + t + 1)
                ch.link(V.tensor_reduce(q, part[:, t], AX.X, ALU.add))
                ch.link(TS(v, q, 1.0 / D, EPS, ALU.mult, ALU.add))
                dve.sem_inc(s_v1, 1)
                dve.wait_ge(s_r1, t + 2)
                ch.link(V.reciprocal(r, r))
                ch.link(refine(r, v, q))
                dve.wait_ge(s_x1t[t], 16)
                ch.link(STT(out=x1[:, t], in0=x1[:, t], scalar=r, in1=A2[:, b], op0=ALU.mult, op1=ALU.mult))
                TT(x1[:, t], x1[:, t], B2[:, b], ALU.add).then_inc(s_h2, 1)

            residual(0, 0, 4 * T)
            dve.wait_ge(s_m2, 16 * (1 + NB))
            dve.wait_ge(s_n2, 16)
            for b in range(2):
                STT(out=A2[:, b], in0=A2[:, b], scalar=1.0, in1=n2g, op0=ALU.add, op1=ALU.mult).then_inc(s_A2, 1)
            residual(1, 0, 3 * T + 1)
            dve.wait_ge(s_A2, 2)
            for t in range(T):
                if t < TP:
                    residual(1, 3 * T + 1 + t, 3 * T + 2 + t)
                if t == 0:
                    dve.wait_ge(s_m2, 16 * 2 * (1 + NB))
                norm_tile(t)
            dve.wait_ge(s_h2, T)
            A16 = [P, TOPK, TOPK]

            def settle():
                ch.sync()
                dve.sem_inc(dve_passed, 1)

            def top16(vals, idxs, srcs):
                settle()
                for v, s in zip(vals, srcs):
                    ch.mark(V.max(v[:, 0:8], s))
                settle()
                for v, i, s in zip(vals, idxs, srcs):
                    ch.mark(V.max_index(i[:, 0:8], v[:, 0:8], s))
                settle()
                for v, s in zip(vals, srcs):
                    ch.mark(V.match_replace(s, v[:, 0:8], s, -3e38))
                settle()
                for v, s in zip(vals, srcs):
                    ch.mark(V.max(v[:, 8:16], s))
                settle()
                for v, i, s in zip(vals, idxs, srcs):
                    ch.mark(V.max_index(i[:, 8:16], v[:, 8:16], s))
                ch.sync()

            def choose(g):
                ch.mark(CP(tks, Sf[:, bass.ds(g * 256, 256)]))
                rows2 = [tks[:, p * P:(p + 1) * P] for p in range(2)]
                top16([tv2[:, 0:16], tv2[:, 16:32]], [ti2[:, 0:16], ti2[:, 16:32]], rows2)
                c3 = cand.rearrange("p (a b) -> p a b", b=TOPK)
                ch.mark(CP(tf2, ti2))
                ch.link(TT(c3, tv2[:, 0:16].unsqueeze(2).to_broadcast(A16),
                           tv2[:, 16:32].unsqueeze(1).to_broadcast(A16), ALU.add))
                top16([tv], [tpos], [cand])
                TS(tsub, tv, tv[:, 0:1], None, ALU.subtract).then_inc(sub_rdy, 1)
                ch.mark(TS(tau, tpos, 4, None, ALU.logical_shift_right))
                ch.link(TS(tbu, tpos, 15, None, ALU.bitwise_and))
                ch.mark(CP(taf, tau))
                ch.link(CP(tbf, tbu))
                ea, eb = (e.rearrange("p (j a) -> p j a", a=TOPK) for e in (eqa, eqb))
                io = iota_f.unsqueeze(1).to_broadcast(A16)
                ch.mark(TT(ea, io, taf.unsqueeze(2).to_broadcast(A16), ALU.is_equal))
                ch.link(TT(eb, io, tbf.unsqueeze(2).to_broadcast(A16), ALU.is_equal))
                ch.mark(TT(ea, ea, tf2[:, 0:16].unsqueeze(1).to_broadcast(A16), ALU.mult))
                ch.link(TT(eb, eb, tf2[:, 16:32].unsqueeze(1).to_broadcast(A16), ALU.mult))
                ch.mark(V.tensor_reduce(ti0, ea, AX.X, ALU.add))
                ch.link(V.tensor_reduce(ti1, eb, AX.X, ALU.add))
                ch.link(STT(out=tef, in0=ti0, scalar=float(NKEY), in1=ti1, op0=ALU.mult, op1=ALU.add))
                CP(idx_all[:, bass.ds(g * TOPK, TOPK)], tef).then_inc(idx_rdy, 1)

            def gate(g):
                dve.wait_ge(exp_rdy, g + 1)
                ch.link(V.reciprocal(trc[:, 0:1], tsum[:, 0:1]))
                ch.mark(TS(gates[:, bass.ds(g * TOPK, TOPK)], tex, trc[:, 0:1], None, ALU.mult))

            def weighted(g, p0, s):
                row, signal, value = v_slot(g, p0, s)
                dve.wait_ge(signal, value)
                dve.wait_ge(v_used, g * TOPK + (s + 4))
                STT(out=acc, in0=row, scalar=wgt[:, s:s + 1], in1=acc,
                    op0=ALU.mult, op1=ALU.add).then_inc(v_used, 1)

            def residual_out(t):
                dve.wait_ge(s_x1b, 32 + 16 * t + (16 * NB if t == TP else 0))
                dve.wait_ge(v_used, 4 + TOPK * NPH * (t + 1))
                ch.link(TT(acc, acc, g2b, ALU.mult))
                ch.link(TT(x1r, x1r, acc, ALU.add))
                ch.link(V.tensor_tensor_reduce(acc, x1r, x1r, 1.0, 0.0, ALU.mult, ALU.add, fin[:, 0:1]))
                ch.link(TS(fin[:, 1:2], fin[:, 0:1], 1.0 / D, EPS, ALU.mult, ALU.add))
                dve.sem_inc(f_v, 1)
                if t < T - 1:
                    ch.link(V.memset(acc, 0.0))

            def final_norm(t):
                dve.wait_ge(f_r, t + 1)
                ch.link(V.reciprocal(fin[:, 3:4], fin[:, 2:3]))
                ch.link(refine(fin[:, 3:4], fin[:, 1:2], fin[:, 4:5]))
                if t == 0:
                    dve.wait_ge(s_fg, 16)
                ch.link(STT(out=x1r, in0=x1r, scalar=fin[:, 3:4], in1=fgb, op0=ALU.mult, op1=ALU.mult))
                dve.sem_inc(s_y, 1)

            def score_copy(n):
                b = n % 2
                dve.wait_ge(s_s, n + 1)
                CP(S[:, 0:TP, n], PB[4 + 2 * b][:, :].rearrange("p (t n) -> p t n", t=TP))
                CP(S[:, TP, n], PB[5 + 2 * b][:, 0:P]).then_inc(s_se, 1)

            copies = {0: {8: 2, 14: 3}, 1: {2: 4, 8: 5, 14: 6}, 2: {2: 7, 5: 8, 8: 9, 11: 10, 14: 11},
                      3: {0: 12, 3: 13, 6: 14, 9: 15}}
            choices = {0: (15, 1), 1: (9, 2), 2: (4, 3)}

            def vector_part(p, p0):
                if p0 == NPH:
                    dve.wait_ge(s_h2b, 16)
                for s in range(TOPK):
                    if s in copies.get(p0, ()):
                        score_copy(copies[p0][s])
                    if p0 in choices and choices[p0][0] == s:
                        g = choices[p0][1]
                        gate(g - 1)
                        dve.wait_ge(s_se, 2 * g + 2)
                        choose(g)
                    if 1 <= p0 < GG and s == 0:
                        dve.wait_ge(dh_rdy, p)
                    if p0 < GG:
                        dve.wait_ge(u_in[s % 4], p * 64 + 16 * (s // 4 + 1))
                        u = ux[:, s % 4]
                        V.tensor_tensor_reduce(u, u, x1[:, p0 // NPH], 1.0, 0.0, ALU.mult, ALU.add,
                                               dots[:, s:s + 1]).then_inc(dots_done, 1)
                    if p0 >= 2:
                        if p0 < EARLY and s == 0:
                            ch.sync()
                        weighted(p - 2, p0, s)
                if 2 <= p0 < NG - 1:
                    gate(p + 1)
                if 1 <= p0 <= NG:
                    dve.wait_ge(gel_rdy, p)
                    dve.wait_ge(v_used, (p - 1) * TOPK + 4) if p0 >= 2 else None
                    ch.sync()
                    ch.mark(TT(wgt, gel, gates[:, bass.ds((p - 1) * TOPK, TOPK)], ALU.mult))
                if p0 < NG:
                    if p0 < GG:
                        dve.wait_ge(dots_done, (p + 1) * TOPK)
                    else:
                        dve.wait_ge(dots_el, (p - (GG - 1)) * (16 * TOPK))
                    CP(dhold, dots if p0 < GG else dots_in).then_inc(dh_rdy, 1)
                if 2 <= p0 < NG - 2:
                    if p0 < 2 * NPH:
                        dve.wait_ge(s_se, min(2 * (p0 + 2) + 2, 16))
                    choose(p + 2)
                ch.sync()
                if p0 >= NPH + 1 and (p0 - 1) % NPH == 0:
                    residual_out((p0 - 1) // NPH - 1)
                if p0 >= NPH + 2 and (p0 - 2) % NPH == 0:
                    final_norm((p0 - 2) // NPH - 1)

            dve.wait_ge(s_h2E, 4 * T)
            dve.wait_ge(s_iota, 2)
            ch.mark(CP(iota_f, iota_u))
            ch.link(CP(token_f, token_u))
            dve.wait_ge(o_done, 40)
            ch.link(V.memset(acc, 0.0))
            dve.sem_inc(v_used, 4)
            score_copy(0)
            score_copy(1)
            dve.wait_ge(s_se, 2)
            choose(0)
            periods(dve, ch, 1 + 10 + 2 + 5 + 2 + 2 + 2 + 2 + 2 + 1 + 2 + 1, vector_part)
            final_norm(T - 1)


_INS = ["x_prompt", "x_sample", "c_prompt", "c_sample", "cache_conv", "cache_attn_k", "cache_attn_v", "norm1_g",
        "norm2_g", "w_ada", "b_ada", "w_in", "w_dw", "b_dw", "conv_ln_g", "conv_ln_b", "rel_bias_table", "w_out",
        "w_pq", "sub_keys", "u_experts", "v_experts", "final_g"]
_OUTS = [("y_prompt", (1, 512, 2048)), ("y_sample", (8, 16, 2048)), ("new_conv_prompt", (1, 1, 30, 1024)),
         ("new_k_prompt", (1, 1, 512, 16, 64)), ("new_v_prompt", (1, 1, 512, 16, 64)),
         ("new_conv_sample", (1, 8, 30, 1024)), ("new_k_sample", (1, 8, 16, 16, 64)),
         ("new_v_sample", (1, 8, 16, 16, 64))]


def kernel(**inputs):
    import numpy as _np
    import concourse.bacc as _bacc
    from concourse import mybir as _mybir
    from concourse.bass_utils import run_bass_kernel_spmd as _run

    nc = _bacc.Bacc("TRN2", target_bir_lowering=False, num_devices=1)
    arrays, ins, outs = {}, {}, {}
    for name in _INS:
        a = _np.ascontiguousarray(inputs[name])
        arrays[f"in_{name}"] = a
        ins[name] = nc.dram_tensor(f"in_{name}", a.shape, _mybir.dt.from_np(a.dtype), kind="ExternalInput").ap()
    for name, shape in _OUTS:
        outs[name] = nc.dram_tensor(f"out_{name}", shape, _mybir.dt.float32, kind="ExternalOutput").ap()
    hybrid_encoder_step(nc, ins, outs)
    r = _run(nc, [arrays], core_ids=[0])
    return tuple(r.results[0][f"out_{name}"] for name, _ in _OUTS)
```
